# Optimizing a Trainium2 kernel written in Bass

```python
import math
import jax
import jax.numpy as jnp
from jax import lax
import numpy as np
import jax, jax.numpy as jnp

D_MODEL = 1024
BATCH = 1
SEQ = 256
DEPTH = 1

RET_HEADS = 4
RET_DK = 128
RET_DV = D_MODEL // RET_HEADS
GDN_HEADS = 4
GDN_DK = 128
GDN_DV = D_MODEL // GDN_HEADS
CHUNK = 64
CONV_K = 4
N_GROUPS = 4
EXPERTS_PER_GROUP = 4
TOP_K = 2
D_FF_EXPERT = 512
ROPE_BASE = 10000.0
NORM_EPS = 1e-6
L2_EPS = 1e-6
N_MOD = 6

RET_QK = RET_HEADS * RET_DK
RET_V = RET_HEADS * RET_DV
GDN_QK = GDN_HEADS * GDN_DK
GDN_V = GDN_HEADS * GDN_DV
IN_WIDTHS = (RET_QK, RET_QK, RET_V, RET_V, GDN_QK, GDN_QK, GDN_V, GDN_V, GDN_HEADS, GDN_HEADS, D_MODEL, D_MODEL)
D_IN = sum(IN_WIDTHS)
F32 = jnp.float32


def _rms_norm(x, w=None):
    xf = x.astype(F32)
    y = xf * lax.rsqrt(jnp.mean(xf * xf, axis=-1, keepdims=True) + NORM_EPS)
    if w is not None:
        y = y * w.astype(F32)
    return y.astype(x.dtype)

def _l2_normalize(x):
    xf = x.astype(F32)
    return xf * lax.rsqrt(jnp.sum(xf * xf, axis=-1, keepdims=True) + L2_EPS)

def _split_columns(t, widths):
    out, start = [], 0
    for w in widths:
        out.append(t[..., start:start + w])
        start += w
    return out

def _rope(x):
    d = x.shape[-1]
    half = d // 2
    inv_freq = 1.0 / (ROPE_BASE ** (jnp.arange(half, dtype=F32) / half))
    ang = jnp.arange(x.shape[1], dtype=F32)[:, None] * inv_freq[None, :]
    cos = jnp.cos(ang)[None, :, None, :]
    sin = jnp.sin(ang)[None, :, None, :]
    xf = x.astype(F32)
    x1, x2 = xf[..., :half], xf[..., half:]
    return jnp.concatenate([x1 * cos - x2 * sin, x1 * sin + x2 * cos], axis=-1)

def _to_chunks(t):
    b, s, h, d = t.shape
    return t.reshape(b, s // CHUNK, CHUNK, h, d).transpose(0, 3, 1, 2, 4)

def _from_chunks(t):
    b, h, n, c, d = t.shape
    return t.transpose(0, 2, 3, 1, 4).reshape(b, n * c, h, d)

def _causal_conv(x, w):
    s = x.shape[1]
    xp = jnp.pad(x, ((0, 0), (CONV_K - 1, 0), (0, 0)))
    out = xp[:, 0:s] * w[0]
    for i in range(1, CONV_K):
        out = out + xp[:, i:i + s] * w[i]
    return out

def _retention_chunkwise(q, k, v):
    n_heads, dk = q.shape[2], q.shape[3]
    q = _to_chunks(q.astype(F32))
    k = _to_chunks(k.astype(F32)) * (dk ** -0.5)
    v = _to_chunks(v.astype(F32))
    b, h, _, _, dv = v.shape
    log_gamma = jnp.log(1.0 - 2.0 ** (-5.0 - jnp.arange(n_heads, dtype=F32)))
    pos = jnp.arange(CHUNK, dtype=F32)
    rel = pos[:, None] - pos[None, :]
    causal = rel >= 0
    intra_decay = jnp.where(causal, jnp.exp(jnp.where(causal, rel, 0.0) * log_gamma[:, None, None]), 0.0)
    q_decay = jnp.exp((pos + 1.0) * log_gamma[:, None])
    k_decay = jnp.exp((CHUNK - 1.0 - pos) * log_gamma[:, None])
    chunk_decay = jnp.exp(CHUNK * log_gamma)[None, :, None, None]
    scores = jnp.einsum('bhnid,bhnjd->bhnij', q, k) * intra_decay[None, :, None]
    o_intra = jnp.einsum('bhnij,bhnjv->bhniv', scores, v)
    q_in = q * q_decay[None, :, None, :, None]
    k_in = k * k_decay[None, :, None, :, None]

    def step(state, xs):
        q_n, k_n, v_n = xs
        o_n = jnp.einsum('bhcd,bhdv->bhcv', q_n, state)
        state = state * chunk_decay + jnp.einsum('bhcd,bhcv->bhdv', k_n, v_n)
        return state, o_n

    state0 = jnp.zeros((b, h, dk, dv), F32)
    _, o_inter = lax.scan(step, state0, (jnp.moveaxis(q_in, 2, 0), jnp.moveaxis(k_in, 2, 0), jnp.moveaxis(v, 2, 0)))
    return _from_chunks(o_intra + jnp.moveaxis(o_inter, 0, 2))

def _gated_delta_rule_chunked(q, k, v, log_decay, beta):
    dk = q.shape[-1]
    q = _to_chunks(q.astype(F32)) * (dk ** -0.5)
    k = _to_chunks(k.astype(F32))
    v = _to_chunks(v.astype(F32))
    b, h, n, c, dv = v.shape
    g = log_decay.astype(F32).reshape(b, n, c, h).transpose(0, 3, 1, 2)
    bt = beta.astype(F32).reshape(b, n, c, h).transpose(0, 3, 1, 2)
    g_cum = jnp.cumsum(g, axis=-1)
    idx = jnp.arange(CHUNK)
    causal = idx[:, None] >= idx[None, :]
    strict = idx[:, None] > idx[None, :]
    decay = jnp.exp(jnp.where(causal, g_cum[..., :, None] - g_cum[..., None, :], -jnp.inf))
    k_beta = k * bt[..., None]
    v_beta = v * bt[..., None]
    a_mat = jnp.where(strict, jnp.einsum('bhnid,bhnjd->bhnij', k_beta, k) * decay, 0.0) + jnp.eye(CHUNK, dtype=F32)
    rhs = jnp.concatenate([v_beta, k_beta * jnp.exp(g_cum)[..., None]], axis=-1)
    sol = lax.linalg.triangular_solve(a_mat, rhs, left_side=True, lower=True, unit_diagonal=True)
    u, w = sol[..., :dv], sol[..., dv:]
    qk = jnp.einsum('bhnid,bhnjd->bhnij', q, k) * decay
    q_g = q * jnp.exp(g_cum)[..., None]
    g_last = g_cum[..., -1]
    k_g = k * jnp.exp(g_last[..., None] - g_cum)[..., None]

    def step(state, xs):
        u_n, w_n, qk_n, q_n, k_n, gl_n = xs
        v_new = u_n - jnp.einsum('bhcd,bhdv->bhcv', w_n, state)
        o_n = jnp.einsum('bhcd,bhdv->bhcv', q_n, state) + jnp.einsum('bhij,bhjv->bhiv', qk_n, v_new)
        state = state * jnp.exp(gl_n)[..., None, None] + jnp.einsum('bhcd,bhcv->bhdv', k_n, v_new)
        return state, o_n

    xs = tuple(jnp.moveaxis(t, 2, 0) for t in (u, w, qk, q_g, k_g, g_last))
    state0 = jnp.zeros((b, h, dk, dv), F32)
    _, o = lax.scan(step, state0, xs)
    return _from_chunks(jnp.moveaxis(o, 0, 2))

def _hybrid_mixer(xm, w_in, conv_w, a_log, dt_bias, gdn_norm_w, w_out):
    b, s, _ = xm.shape
    proj = jnp.einsum('bsd,de->bse', xm, w_in)
    rq, rk, rv, rg, gq, gk, gv, gz, ga, gb, gate_a, gate_b = _split_columns(proj, IN_WIDTHS)
    q_r = _rope(rq.reshape(b, s, RET_HEADS, RET_DK))
    k_r = _rope(rk.reshape(b, s, RET_HEADS, RET_DK))
    o_r = _retention_chunkwise(q_r, k_r, rv.reshape(b, s, RET_HEADS, RET_DV))
    o_r = _rms_norm(o_r).reshape(b, s, RET_V).astype(xm.dtype)
    y_ret = jax.nn.silu(rg) * o_r
    qkv = jax.nn.silu(_causal_conv(jnp.concatenate([gq, gk, gv], axis=-1), conv_w))
    q_g, k_g, v_g = _split_columns(qkv, (GDN_QK, GDN_QK, GDN_V))
    q_g = _l2_normalize(q_g.reshape(b, s, GDN_HEADS, GDN_DK))
    k_g = _l2_normalize(k_g.reshape(b, s, GDN_HEADS, GDN_DK))
    beta = jax.nn.sigmoid(gb.astype(F32))
    log_decay = -jnp.exp(a_log.astype(F32)) * jax.nn.softplus(ga.astype(F32) + dt_bias.astype(F32))
    o_g = _gated_delta_rule_chunked(q_g, k_g, v_g.reshape(b, s, GDN_HEADS, GDN_DV), log_decay, beta)
    o_g = _rms_norm(o_g, gdn_norm_w) * jax.nn.silu(gz.reshape(b, s, GDN_HEADS, GDN_DV).astype(F32))
    y_gdn = o_g.reshape(b, s, GDN_V).astype(xm.dtype)
    merged = jax.nn.sigmoid(gate_a) * y_ret + jax.nn.sigmoid(gate_b) * y_gdn
    return jnp.einsum('bsd,de->bse', merged, w_out)

def _hierarchical_moe(xm, w_group, b_group, w_router, b_router, w_gate, w_up, w_down):
    b, s, d = xm.shape
    xf = xm.reshape(-1, d)
    t = xf.shape[0]
    group_prob = jax.nn.softmax((xf @ w_group).astype(F32) + b_group.astype(F32), axis=-1)
    g_top, g_idx = lax.top_k(group_prob, 1)
    exp_logits = (xf @ w_router).astype(F32).reshape(t, N_GROUPS, EXPERTS_PER_GROUP) + b_router.astype(F32)
    exp_logits = jnp.take_along_axis(exp_logits, g_idx[:, :, None], axis=1)[:, 0]
    exp_prob = jax.nn.softmax(exp_logits, axis=-1)
    e_top, e_idx = lax.top_k(exp_prob, TOP_K)
    e_w = e_top / jnp.sum(e_top, axis=-1, keepdims=True)
    within = jnp.sum(jax.nn.one_hot(e_idx, EXPERTS_PER_GROUP, dtype=F32) * e_w[..., None], axis=1)
    comb = jax.nn.one_hot(g_idx[:, 0], N_GROUPS, dtype=F32)[:, :, None] * (g_top[:, :, None] * within[:, None, :])
    comb = comb.astype(xm.dtype)
    out = jnp.zeros_like(xf)
    for gi in range(N_GROUPS):
        hg = jnp.einsum('td,edf->tef', xf, w_gate[gi])
        hu = jnp.einsum('td,edf->tef', xf, w_up[gi])
        act = jax.nn.silu(hg) * hu * comb[:, gi, :, None]
        out = out + jnp.einsum('tef,efd->td', act, w_down[gi])
    return out.reshape(b, s, d)

def first_inputs(seed: int = 0) -> dict:
    key = jax.random.key(seed)
    ks = jax.random.split(key, 20)
    L, G, E, F = DEPTH, N_GROUPS, EXPERTS_PER_GROUP, D_FF_EXPERT

    def nrm(k, shape, scale):
        return jax.random.normal(k, shape, F32) * scale

    dt = jnp.exp(jax.random.uniform(ks[8], (L, GDN_HEADS), F32, math.log(1e-3), math.log(1e-1)))
    return {
        'x': nrm(ks[0], (BATCH, SEQ, D_MODEL), 1.0),
        'c': nrm(ks[1], (BATCH, D_MODEL), 1.0),
        'mod_w': nrm(ks[2], (L, D_MODEL, N_MOD * D_MODEL), 0.5 * D_MODEL ** -0.5),
        'mod_b': nrm(ks[3], (L, N_MOD * D_MODEL), 0.02),
        'norm_mix_w': 1.0 + nrm(ks[4], (L, D_MODEL), 0.02),
        'w_in': nrm(ks[5], (L, D_MODEL, D_IN), D_MODEL ** -0.5),
        'gdn_conv_w': nrm(ks[6], (L, CONV_K, 2 * GDN_QK + GDN_V), CONV_K ** -0.5),
        'gdn_a_log': jnp.log(jax.random.uniform(ks[7], (L, GDN_HEADS), F32, 1.0, 16.0)),
        'gdn_dt_bias': dt + jnp.log(-jnp.expm1(-dt)),
        'gdn_norm_w': 1.0 + nrm(ks[9], (L, GDN_DV), 0.02),
        'w_out': nrm(ks[10], (L, D_MODEL, D_MODEL), D_MODEL ** -0.5),
        'norm_ffn_w': 1.0 + nrm(ks[11], (L, D_MODEL), 0.02),
        'w_group': nrm(ks[12], (L, D_MODEL, G), D_MODEL ** -0.5),
        'b_group': nrm(ks[13], (L, G), 0.01),
        'w_router': nrm(ks[14], (L, D_MODEL, G * E), D_MODEL ** -0.5),
        'b_router': nrm(ks[15], (L, G, E), 0.01),
        'w_gate': nrm(ks[16], (L, G, E, D_MODEL, F), D_MODEL ** -0.5),
        'w_up': nrm(ks[17], (L, G, E, D_MODEL, F), D_MODEL ** -0.5),
        'w_down': nrm(ks[18], (L, G, E, F, D_MODEL), F ** -0.5),
        'norm_out_w': 1.0 + nrm(ks[19], (D_MODEL,), 0.02),
    }

def first_block(x, c, mod_w, mod_b, norm_mix_w, w_in, gdn_conv_w, gdn_a_log, gdn_dt_bias, gdn_norm_w, w_out,
              norm_ffn_w, w_group, b_group, w_router, b_router, w_gate, w_up, w_down, norm_out_w):
    h = x
    for l in range(DEPTH):
        mod = jax.nn.silu(c) @ mod_w[l] + mod_b[l]
        shift_m, scale_m, gate_m, shift_f, scale_f, gate_f = jnp.split(mod[:, None, :], N_MOD, axis=-1)
        xm = _rms_norm(h, norm_mix_w[l]) * (1.0 + scale_m) + shift_m
        h = h + gate_m * _hybrid_mixer(xm, w_in[l], gdn_conv_w[l], gdn_a_log[l], gdn_dt_bias[l], gdn_norm_w[l], w_out[l])
        xf = _rms_norm(h, norm_ffn_w[l]) * (1.0 + scale_f) + shift_f
        h = h + gate_f * _hierarchical_moe(xf, w_group[l], b_group[l], w_router[l], b_router[l], w_gate[l], w_up[l], w_down[l])
    return _rms_norm(h, norm_out_w)


DEPTH_2 = 2

EPS = 1e-6
SSM_EXPAND = 2
SSM_D_INNER = SSM_EXPAND * D_MODEL
SSM_HEAD_DIM = 64
SSM_HEADS = SSM_D_INNER // SSM_HEAD_DIM
SSM_GROUPS = 4
SSM_STATE = 128
SSM_CONV = 4
SSM_CHUNK = 128
SSM_CONV_DIM = SSM_D_INNER + 2 * SSM_GROUPS * SSM_STATE
ATT_HEAD_DIM = 64
ATT_KV_HEADS = D_MODEL // ATT_HEAD_DIM
ATT_PATTERNS = ((128, 1), (512, 4), (2048, 16))
ATT_GROUPS = len(ATT_PATTERNS)
ATT_Q_HEADS = ATT_GROUPS * ATT_KV_HEADS
ATT_WIDTH = ATT_KV_HEADS * ATT_HEAD_DIM
REL_BUCKETS = 32
REL_MAX_DIST = 2048
HY_SIZES = (SSM_D_INNER, SSM_CONV_DIM, SSM_HEADS, ATT_Q_HEADS * ATT_HEAD_DIM, ATT_WIDTH, ATT_WIDTH)
HY_SPLITS = tuple(int(v) for v in np.cumsum(HY_SIZES)[:-1])
HY_IN_DIM = sum(HY_SIZES)
HY_OUT_DIM = SSM_D_INNER + ATT_WIDTH
CONV_WIDTH = 31
FFN_HIDDEN = -(-8 * D_MODEL // (3 * 256)) * 256
N_EVEN = (DEPTH_2 + 1) // 2
N_ODD = DEPTH_2 // 2


def rms_norm(x, g):
    xf = x.astype(jnp.float32)
    y = xf * lax.rsqrt(jnp.mean(xf * xf, -1, keepdims=True) + EPS)
    return (y * g.astype(jnp.float32)).astype(x.dtype)

def layer_norm(x, g, b):
    xf = x.astype(jnp.float32)
    mu = jnp.mean(xf, -1, keepdims=True)
    var = jnp.mean(jnp.square(xf - mu), -1, keepdims=True)
    y = (xf - mu) * lax.rsqrt(var + EPS)
    return (y * g.astype(jnp.float32) + b.astype(jnp.float32)).astype(x.dtype)

def causal_depthwise_conv(x, w, b):
    k = w.shape[0]
    out = lax.conv_general_dilated(
        x, w[:, None, :].astype(x.dtype), window_strides=(1,), padding=[(k - 1, 0)],
        dimension_numbers=('NWC', 'WIO', 'NWC'), feature_group_count=x.shape[-1])
    return out + b

def t5_bucket(dist):
    max_exact = REL_BUCKETS // 2
    n = jnp.maximum(dist, 1).astype(jnp.float32)
    large = max_exact + jnp.log(n / max_exact) / math.log(REL_MAX_DIST / max_exact) * (REL_BUCKETS - max_exact)
    large = jnp.minimum(large.astype(jnp.int32), REL_BUCKETS - 1)
    return jnp.where(dist < max_exact, dist, large)

def ssd_chunked(x, dt, A, Bm, Cm):
    f32 = jnp.float32
    b_, s, h, p = x.shape
    g, n = Bm.shape[2], Bm.shape[3]
    r, q = h // g, SSM_CHUNK
    nc = s // q
    x = x.astype(f32).reshape(b_, nc, q, g, r, p)
    dt = dt.astype(f32).reshape(b_, nc, q, g, r)
    Bm = Bm.astype(f32).reshape(b_, nc, q, g, n)
    Cm = Cm.astype(f32).reshape(b_, nc, q, g, n)
    a_cs = jnp.cumsum(dt * A.astype(f32).reshape(g, r), axis=2)
    xdt = x * dt[..., None]
    seg = a_cs[:, :, :, None] - a_cs[:, :, None, :]
    causal = jnp.tril(jnp.ones((q, q), bool))[:, :, None, None]
    decay = jnp.exp(jnp.where(causal, seg, -jnp.inf))
    cb = jnp.einsum('bclgn,bcsgn->bclsg', Cm, Bm)
    y_diag = jnp.einsum('bclsgr,bcsgrp->bclgrp', cb[..., None] * decay, xdt)
    decay_end = jnp.exp(a_cs[:, :, -1:] - a_cs)
    states = jnp.einsum('bcsgn,bcsgrp->bcgrpn', Bm, xdt * decay_end[..., None])
    chunk_decay = jnp.exp(a_cs[:, :, -1])

    def step(hs, inp):
        st, dec = inp
        return dec[..., None, None] * hs + st, hs

    h0 = jnp.zeros((b_, g, r, p, n), f32)
    _, prev = lax.scan(step, h0, (jnp.moveaxis(states, 1, 0), jnp.moveaxis(chunk_decay, 1, 0)))
    prev = jnp.moveaxis(prev, 0, 1)
    y_off = jnp.einsum('bclgn,bcgrpn->bclgrp', Cm, prev) * jnp.exp(a_cs)[..., None]
    return (y_diag + y_off).reshape(b_, s, h, p)

def dilated_branch(q, k, v, bias_tab, window, dil):
    b_, s, h, dh = q.shape
    blk = window // dil
    L = s // dil
    nb = -(-L // blk)
    lp = nb * blk

    def blocks(t):
        t = t.reshape(b_, L, dil, h, dh)
        t = jnp.pad(t, ((0, 0), (0, lp - L), (0, 0), (0, 0), (0, 0)))
        return t.reshape(b_, nb, blk, dil, h, dh)

    def band_keys(t):
        prev = jnp.pad(t, ((0, 0), (1, 0), (0, 0), (0, 0), (0, 0), (0, 0)))[:, :-1]
        return jnp.concatenate([prev, t], axis=2)

    qb = blocks(q)
    kw, vw = band_keys(blocks(k)), band_keys(blocks(v))
    i = jnp.arange(blk)[:, None]
    j = jnp.arange(2 * blk)[None, :]
    delta = blk + i - j
    band = (delta >= 0) & (delta <= blk)
    kpos = jnp.arange(nb)[:, None] * blk + jnp.arange(2 * blk)[None, :] - blk
    mask = band[None] & (kpos >= 0)[:, None, :]
    bias = jnp.transpose(bias_tab[t5_bucket(jnp.maximum(delta, 0) * dil)], (2, 0, 1)).astype(jnp.float32)
    sc = jnp.einsum('bnirhd,bnjrhd->bnrhij', qb, kw).astype(jnp.float32) * (dh ** -0.5) + bias
    sc = jnp.where(mask[None, :, None, None], sc, -jnp.inf)
    m = jnp.max(sc, -1, keepdims=True)
    pr = jnp.exp(sc - m)
    l = jnp.sum(pr, -1, keepdims=True)
    o = jnp.einsum('bnrhij,bnjrhd->bnirhd', (pr / l).astype(v.dtype), vw)
    lse = jnp.transpose((m + jnp.log(l))[..., 0], (0, 1, 4, 2, 3))
    lse = lse.reshape(b_, lp, dil, h)[:, :L].reshape(b_, s, h)
    o = o.reshape(b_, lp, dil, h, dh)[:, :L].reshape(b_, s, h, dh)
    return o, lse

def dilated_attention(q, k, v, rel_table):
    b_, s, _, h, dh = q.shape
    outs, lses = [], []
    for gi, (w, d) in enumerate(ATT_PATTERNS):
        o, lse = dilated_branch(q[:, :, gi], k, v, rel_table[:, gi * h:(gi + 1) * h], w, d)
        outs.append(o)
        lses.append(lse)
    wgt = jax.nn.softmax(jnp.stack(lses, 0), axis=0)
    o = jnp.einsum('gbsh,gbshd->bshd', wgt.astype(outs[0].dtype), jnp.stack(outs, 0))
    return o.reshape(b_, s, h * dh)

def hybrid_mixer(h, w_in, conv_w, conv_b, dt_bias, a_log, d_skip, ssm_norm_g, w_out, rel_table):
    b_, s, _ = h.shape
    z, xbc, dt_raw, q, k, v = jnp.split(h @ w_in, HY_SPLITS, axis=-1)
    xbc = jax.nn.silu(causal_depthwise_conv(xbc, conv_w, conv_b))
    xs, bm, cm = jnp.split(xbc, (SSM_D_INNER, SSM_D_INNER + SSM_GROUPS * SSM_STATE), axis=-1)
    xs = xs.reshape(b_, s, SSM_HEADS, SSM_HEAD_DIM)
    dt = jax.nn.softplus((dt_raw + dt_bias).astype(jnp.float32))
    A = -jnp.exp(a_log.astype(jnp.float32))
    y = ssd_chunked(xs, dt, A, bm.reshape(b_, s, SSM_GROUPS, SSM_STATE), cm.reshape(b_, s, SSM_GROUPS, SSM_STATE))
    y = y + d_skip.astype(jnp.float32)[:, None] * xs.astype(jnp.float32)
    y = y.reshape(b_, s, SSM_D_INNER).astype(h.dtype)
    y = rms_norm(y * jax.nn.silu(z), ssm_norm_g)
    att = dilated_attention(q.reshape(b_, s, ATT_GROUPS, ATT_KV_HEADS, ATT_HEAD_DIM),
                            k.reshape(b_, s, ATT_KV_HEADS, ATT_HEAD_DIM),
                            v.reshape(b_, s, ATT_KV_HEADS, ATT_HEAD_DIM), rel_table)
    return jnp.concatenate([y, att.astype(y.dtype)], axis=-1) @ w_out

def conformer_conv(h, w1, b1, w_dw, b_dw, ln_g, ln_b, w2, b2):
    a, gt = jnp.split(h @ w1 + b1, 2, axis=-1)
    u = a * jax.nn.sigmoid(gt)
    u = causal_depthwise_conv(u, w_dw, b_dw)
    u = jax.nn.silu(layer_norm(u, ln_g, ln_b))
    return u @ w2 + b2

def swiglu(h, wg, wu, wd):
    return (jax.nn.silu(h @ wg) * (h @ wu)) @ wd

def second_inputs(seed: int = 0) -> dict:
    key = jax.random.key(seed)
    ks = iter(jax.random.split(key, 40))
    f32 = jnp.float32

    def nrm(shape, scale=1.0):
        return jax.random.normal(next(ks), shape, f32) * scale

    D = D_MODEL
    dt0 = jnp.exp(jax.random.uniform(next(ks), (N_EVEN, SSM_HEADS), f32, math.log(1e-3), math.log(1e-1)))
    return {
        "x": nrm((BATCH, SEQ, D)),
        "c": nrm((BATCH, D)),
        "ada_w": nrm((DEPTH_2, D, N_MOD * D), 0.5 * D ** -0.5),
        "ada_b": nrm((DEPTH_2, N_MOD * D), 0.02),
        "norm_mix_g": 1.0 + nrm((DEPTH_2, D), 0.05),
        "norm_ffn_g": 1.0 + nrm((DEPTH_2, D), 0.05),
        "hy_w_in": nrm((N_EVEN, D, HY_IN_DIM), D ** -0.5),
        "hy_conv_w": nrm((N_EVEN, SSM_CONV, SSM_CONV_DIM), SSM_CONV ** -0.5),
        "hy_conv_b": nrm((N_EVEN, SSM_CONV_DIM), 0.02),
        "hy_dt_bias": dt0 + jnp.log(-jnp.expm1(-dt0)),
        "hy_a_log": jnp.log(jax.random.uniform(next(ks), (N_EVEN, SSM_HEADS), f32, 1.0, 16.0)),
        "hy_d_skip": 1.0 + nrm((N_EVEN, SSM_HEADS), 0.1),
        "hy_ssm_norm_g": 1.0 + nrm((N_EVEN, SSM_D_INNER), 0.05),
        "hy_w_out": nrm((N_EVEN, HY_OUT_DIM, D), HY_OUT_DIM ** -0.5),
        "rel_table": nrm((REL_BUCKETS, ATT_Q_HEADS), 0.2),
        "cv_w_pw1": nrm((N_ODD, D, 2 * D), D ** -0.5),
        "cv_b_pw1": nrm((N_ODD, 2 * D), 0.02),
        "cv_w_dw": nrm((N_ODD, CONV_WIDTH, D), CONV_WIDTH ** -0.5),
        "cv_b_dw": nrm((N_ODD, D), 0.02),
        "cv_ln_g": 1.0 + nrm((N_ODD, D), 0.05),
        "cv_ln_b": nrm((N_ODD, D), 0.02),
        "cv_w_pw2": nrm((N_ODD, D, D), D ** -0.5),
        "cv_b_pw2": nrm((N_ODD, D), 0.02),
        "ffn_w_gate": nrm((DEPTH_2, D, FFN_HIDDEN), D ** -0.5),
        "ffn_w_up": nrm((DEPTH_2, D, FFN_HIDDEN), D ** -0.5),
        "ffn_w_down": nrm((DEPTH_2, FFN_HIDDEN, D), FFN_HIDDEN ** -0.5),
        "final_norm_g": 1.0 + nrm((D,), 0.05),
    }

def second_block(x, c, ada_w, ada_b, norm_mix_g, norm_ffn_g, hy_w_in, hy_conv_w, hy_conv_b, hy_dt_bias,
              hy_a_log, hy_d_skip, hy_ssm_norm_g, hy_w_out, rel_table, cv_w_pw1, cv_b_pw1, cv_w_dw,
              cv_b_dw, cv_ln_g, cv_ln_b, cv_w_pw2, cv_b_pw2, ffn_w_gate, ffn_w_up, ffn_w_down,
              final_norm_g):
    cs = jax.nn.silu(c)
    for i in range(DEPTH_2):
        mod = cs @ ada_w[i] + ada_b[i]
        sh1, sc1, g1, sh2, sc2, g2 = [m[:, None, :] for m in jnp.split(mod, N_MOD, axis=-1)]
        h = rms_norm(x, norm_mix_g[i]) * (1 + sc1) + sh1
        j = i // 2
        if i % 2 == 0:
            mix = hybrid_mixer(h, hy_w_in[j], hy_conv_w[j], hy_conv_b[j], hy_dt_bias[j], hy_a_log[j],
                               hy_d_skip[j], hy_ssm_norm_g[j], hy_w_out[j], rel_table)
        else:
            mix = conformer_conv(h, cv_w_pw1[j], cv_b_pw1[j], cv_w_dw[j], cv_b_dw[j], cv_ln_g[j],
                                 cv_ln_b[j], cv_w_pw2[j], cv_b_pw2[j])
        x = x + g1 * mix
        h = rms_norm(x, norm_ffn_g[i]) * (1 + sc2) + sh2
        x = x + g2 * swiglu(h, ffn_w_gate[i], ffn_w_up[i], ffn_w_down[i])
    return rms_norm(x, final_norm_g)


def setup_inputs(seed=0):
    out = dict(first_inputs(seed))
    for name, value in second_inputs(seed + 1).items():
        if name != "x":
            out[name + "_2"] = value
    return out


def reference(
    x, c, mod_w, mod_b, norm_mix_w, w_in, gdn_conv_w, gdn_a_log, gdn_dt_bias, gdn_norm_w, w_out,
    norm_ffn_w, w_group, b_group, w_router, b_router, w_gate, w_up, w_down, norm_out_w, c_2,
    ada_w_2, ada_b_2, norm_mix_g_2, norm_ffn_g_2, hy_w_in_2, hy_conv_w_2, hy_conv_b_2,
    hy_dt_bias_2, hy_a_log_2, hy_d_skip_2, hy_ssm_norm_g_2, hy_w_out_2, rel_table_2, cv_w_pw1_2,
    cv_b_pw1_2, cv_w_dw_2, cv_b_dw_2, cv_ln_g_2, cv_ln_b_2, cv_w_pw2_2, cv_b_pw2_2,
    ffn_w_gate_2, ffn_w_up_2, ffn_w_down_2, final_norm_g_2,
):
    x = first_block(
        x, c, mod_w, mod_b, norm_mix_w, w_in, gdn_conv_w, gdn_a_log, gdn_dt_bias, gdn_norm_w,
        w_out, norm_ffn_w, w_group, b_group, w_router, b_router, w_gate, w_up, w_down,
        norm_out_w,
    )
    return second_block(
        x, c_2, ada_w_2, ada_b_2, norm_mix_g_2, norm_ffn_g_2, hy_w_in_2, hy_conv_w_2,
        hy_conv_b_2, hy_dt_bias_2, hy_a_log_2, hy_d_skip_2, hy_ssm_norm_g_2, hy_w_out_2,
        rel_table_2, cv_w_pw1_2, cv_b_pw1_2, cv_w_dw_2, cv_b_dw_2, cv_ln_g_2, cv_ln_b_2,
        cv_w_pw2_2, cv_b_pw2_2, ffn_w_gate_2, ffn_w_up_2, ffn_w_down_2, final_norm_g_2,
    )


_drawn_inputs = setup_inputs


def setup_inputs(seed=0):
    import zlib

    import numpy as np

    out = dict(_drawn_inputs(seed))
    spreads = {}
    factors = {'mod_b': 2.781,
     'norm_mix_w': 6.305,
     'gdn_norm_w': 8.0,
     'norm_ffn_w': 4.856,
     'b_group': 32.305,
     'b_router': 8.0,
     'norm_mix_g_2': 2.936,
     'norm_ffn_g_2': 3.043,
     'hy_conv_b_2': 8.0,
     'hy_d_skip_2': 32.552,
     'hy_ssm_norm_g_2': 4.684,
     'rel_table_2': 8.0,
     'cv_b_pw1_2': 8.0,
     'cv_b_dw_2': 8.0,
     'cv_ln_g_2': 5.308,
     'cv_ln_b_2': 31.547,
     'cv_b_pw2_2': 23.442}
    for name, (base, spread) in spreads.items():
        noise = np.random.default_rng([zlib.crc32(name.encode()), seed]).standard_normal(out[name].shape)
        drawn = base * np.exp(spread * noise) if base else spread * noise
        out[name] = jnp.asarray(drawn.astype(out[name].dtype))
    for name, factor in factors.items():
        out[name] = (out[name] * factor).astype(out[name].dtype)
    return out
```

```python
from contextlib import ExitStack

import numpy as np
import concourse.bass as bass
from concourse import mybir

F32 = mybir.dt.float32
ACT = mybir.ActivationFunctionType
ALU = mybir.AluOpType
AX_X = mybir.AxisListType.X

P = 128
D = 1024
T = 256
KC = D // P
NA, NB = 8, 4
UNIT = 2048
HEADS = 4
EPS = 1e-6
N_EXP = 16
FF_EXP = 512
FF = 2816
SSM_H = 32
ATT_H = 16
BIG = -1e30
TWIDE = 384

A_UNITS = [("mod", 8), ("win", 32), ("wout", 4), ("moe", 4 * N_EXP), ("hyin", 20), ("hyqkv", 20),
           ("ffn0", 2 * FF // 256), ("cv1", 8), ("cv2", 4), ("ffn1", 2 * FF // 256)]
B_UNITS = [("moe", 2 * N_EXP), ("hyout", 12), ("ffn0", FF // 256), ("ffn1", FF // 256)]


C_UNITS = {"win": (0, 32), "hyin": (32, 16), "hyqkv": (48, 16)}
C_ALL = 64
NC = 2


def starts(units):
    at, n = {}, 0
    for name, k in units:
        at[name] = (n, k)
        n += k
    return at, n


A_AT, A_ALL = starts(A_UNITS)
B_AT, B_ALL = starts(B_UNITS)

PAR_WIDTHS = [("c", 8), ("c2", 8), ("mod_b", 48), ("ada_b", 96), ("norm_mix", 8), ("norm_ffn", 8), ("norm_out", 8),
              ("norm_mix2", 16), ("norm_ffn2", 16), ("final", 8), ("gconv", 64), ("a_log", 4),
              ("dt_bias", 4), ("gdn_w", 2), ("b_route", 20), ("w_route", 160), ("w_ab", 64),
              ("hconv", 96), ("hconv_b", 24), ("w_dt", 256), ("dt_bias2", 1), ("a_log2", 1), ("d_skip", 16),
              ("ssm_g", 16), ("rel", 48), ("b1", 16), ("dw", 248), ("dw_b", 8), ("ln_g", 8), ("ln_b", 8), ("b2", 8)]
PAR = {}
N_PAR = 0
for _name, _w in PAR_WIDTHS:
    PAR[_name] = (N_PAR, _w)
    N_PAR += _w

CON_WIDTHS = [("ident", 128), ("ones", 128), ("upto", 512), ("eps", 1),
              ("cos", 256), ("sin", 256), ("turn", 128), ("ret", 4 * 384),
              ("strict", 128), ("levels", 7 * 128),
              ("bucket", TWIDE), ("band", TWIDE)]
CON = {}
N_CON = 0
for _name, _w in CON_WIDTHS:
    CON[_name] = (N_CON, _w)
    N_CON += _w
N_KEPT = CON["cos"][0]


def constants():
    c = np.zeros((P, N_CON), np.float32)

    def put(name, a):
        at, w = CON[name]
        a = np.asarray(a, np.float32)
        c[:a.shape[0], at:at + w] = a.reshape(a.shape[0], w)

    p = np.arange(P)
    i = np.arange(T)
    put("ident", np.eye(P))
    put("ones", np.ones((P, P)))
    put("upto", np.stack([p[:, None] + P * t <= i[None, :] for t in range(2)], 1))
    put("eps", np.full((P, 1), EPS))
    half = 64
    inv = (1.0 / (np.float32(10000.0) ** (np.arange(half, dtype=np.float32) / np.float32(half)))).astype(np.float32)
    ang = (np.arange(T, dtype=np.float32)[:, None] * inv[None, :]).astype(np.float32)
    put("cos", np.tile(np.cos(ang).T, (2, 1)))
    put("sin", np.tile(np.sin(ang).T, (2, 1)))
    turn = np.zeros((P, P))
    for m in range(half):
        turn[m + half, m] = -1.0
        turn[m, m + half] = 1.0
    put("turn", turn)
    ret = np.zeros((P, HEADS, 384))
    for h in range(HEADS):
        lg = np.log(1.0 - 2.0 ** (-5.0 - h))
        rel = i[None, :] - p[:, None]
        dec = np.where(rel >= 0, np.exp(np.maximum(rel, 0) * lg), 0.0) * 128 ** -0.5
        ret[:, h, :T] = dec
        ret[:, h, T:] = dec[:, :P]
    put("ret", ret)
    put("strict", p[:, None] < p[None, :])
    lv = np.zeros((P, 7, P))
    for n in range(7):
        s = 1 << n
        lv[:, n] = (p[:, None] // (2 * s) == p[None, :] // (2 * s)) & ((p[:, None] // s) % 2 == 0) & ((p[None, :] // s) % 2 == 1)
    put("levels", lv)
    dist = np.arange(TWIDE) - 127
    n = np.maximum(dist, 1).astype(np.float32)
    large = 16 + np.log(n / np.float32(16)) / np.float32(np.log(2048 / 16)) * 16
    large = np.minimum(large.astype(np.int32), 31)
    bk = np.where(dist < 16, np.maximum(dist, 0), large)
    put("bucket", (bk[None, :] == np.arange(32)[:, None]) & (dist >= 0)[None, :])
    band = np.zeros((48, TWIDE))
    for g, dil in enumerate((1, 4, 16)):
        ok = (dist >= 0) & (dist % dil == 0) & (dist // dil <= 128)
        band[g * 16:(g + 1) * 16] = np.where(ok, 0.0, BIG)[None, :]
    put("band", band)
    return c


def rep(ap, n):
    return bass.AP(tensor=ap.tensor, offset=ap.offset, ap=[list(ap.ap[0]), [0, n]] + [list(x) for x in ap.ap[1:]])


def wide(ap, m):
    return bass.AP(tensor=ap.tensor, offset=ap.offset, ap=[list(x) for x in ap.ap] + [[0, m]])


class Chain:

    def __init__(self, engine, semaphore):
        self.engine, self.semaphore, self.count = engine, semaphore, 0

    def __call__(self, instruction):
        self.count += 1
        instruction.then_inc(self.semaphore, 1)
        self.engine.wait_ge(self.semaphore, self.count)


class Stages:

    SIZE = 66

    def __init__(self, nc):
        self.nc, self.k = nc, 0
        self.pools = [[nc.alloc_semaphore(f"stage{q}_{i}") for i in range(self.SIZE)] for q in range(2)]

    def begin(self):
        taken = {}
        pool = self.pools[self.k % 2]

        def sem(name):
            if name not in taken:
                taken[name] = pool[len(taken)]
            return taken[name]

        return sem

    def end(self):
        pool = self.pools[self.k % 2]
        self.nc.gpsimd.sem_clear(range(pool[0].num, pool[-1].num + 1))
        self.k += 1


def program(nc, ins, out):
    wa, wb, wc, par_dram, con_dram, x_dram = ins
    bias_rows = nc.dram_tensor("bias_rows", (48, TWIDE), F32, kind="Internal").ap()
    ctx = ExitStack()

    def sb(name, shape, on=ctx):
        return on.enter_context(nc.sbuf_tensor(name + "_sb", shape, F32))

    ringA = sb("ringA", [P, NA, KC, 256])
    ringB = sb("ringB", [P, NB, 2, D])
    h = sb("h", [P, KC, T])
    xm = sb("xm", [P, KC, T])
    par = sb("par", [P, N_PAR])
    con = sb("con", [P, N_KEPT])
    mods3 = sb("mods", [P, 3, 48])
    normw3 = sb("normw", [P, 3, 2, KC])
    cs = sb("cs", [P, 2, KC])
    rstd = sb("rstd", [P, T])
    PS = ctx.enter_context(nc.psum_tensor("PS", [P, 8, 512], F32))

    a_full = [nc.alloc_semaphore(f"a_full{i}") for i in range(NA)]
    b_full = [nc.alloc_semaphore(f"b_full{i}") for i in range(NB)]
    c_full = [nc.alloc_semaphore(f"c_full{i}") for i in range(NC)]
    a_used = nc.alloc_semaphore("a_used")
    b_used = nc.alloc_semaphore("b_used")
    stages = Stages(nc)

    def pr(name, a=0, b=None):
        at, w = PAR[name]
        return par[:, at + a:at + (w if b is None else b)]

    def cn(name):
        at, w = CON[name]
        return con[:, at:at + w]

    ident, ones, eps = cn("ident"), cn("ones"), cn("eps")
    upto = cn("upto").rearrange("p (t i) -> p t i", t=2)

    def load_a(sp, slot, n):
        sp.dma_start(ringA[:, slot].rearrange("p k c -> p (k c)"), wa[n]).then_inc(a_full[slot], 16)

    def load_b(sp, slot, n):
        sp.dma_start(ringB[:, slot].rearrange("p k c -> p (k c)"), wb[n]).then_inc(b_full[slot], 16)

    def refill_a(sp, first, n):
        n = min(n, A_ALL - NA - first)
        turns = n // NA
        if turns > 1:
            with sp.Fori(0, turns) as i:
                for j in range(NA):
                    sp.wait_ge(a_used, i * NA + (first + j + 1))
                    sp.dma_start(ringA[:, (first + j) % NA].rearrange("p k c -> p (k c)"),
                                 wa[bass.ds(i * NA + (first + j + NA), 1)].rearrange("a p c -> p (a c)")
                                 ).then_inc(a_full[(first + j) % NA], 16)
        else:
            turns = 0
        for m in range(first + turns * NA, first + n):
            sp.wait_ge(a_used, m + 1)
            load_a(sp, m % NA, m + NA)

    def refill_b(sp, first, n):
        for m in range(first, first + min(n, B_ALL - NB - first)):
            sp.wait_ge(b_used, m + 1)
            load_b(sp, m % NB, m + NB)

    def refill_ab(sp, a0, b0, steps):
        def step(s):
            for j in (0, 1):
                m = a0 + 2 * s + j
                if m + NA < A_ALL:
                    sp.wait_ge(a_used, m + 1)
                    load_a(sp, m % NA, m + NA)
            m = b0 + s - 1
            if s > 0 and m + NB < B_ALL:
                sp.wait_ge(b_used, m + 1)
                load_b(sp, m % NB, m + NB)

        last = min(steps, (A_ALL - NA - a0) // 2, B_ALL - NB - b0)
        turns = (last - 4) // 4
        for s in range(4):
            step(s)
        if turns > 1:
            with sp.Fori(1, turns + 1) as i:
                for s in range(4):
                    loop_step(sp, a0, b0, s, i)
            done = 4 + 4 * turns
        else:
            done = 4
        for s in range(done, steps):
            step(s)
        m = b0 + steps - 1
        if m + NB < B_ALL:
            sp.wait_ge(b_used, m + 1)
            load_b(sp, m % NB, m + NB)

    def loop_step(sp, a0, b0, s, i):
        for j in (0, 1):
            m = a0 + 2 * s + j
            sp.wait_ge(a_used, i * 8 + (m + 1))
            sp.dma_start(ringA[:, m % NA].rearrange("p k c -> p (k c)"),
                         wa[bass.ds(i * 8 + (m + NA), 1)].rearrange("a p c -> p (a c)")).then_inc(a_full[m % NA], 16)
        m = b0 + s - 1
        sp.wait_ge(b_used, i * 4 + (m + 1))
        sp.dma_start(ringB[:, m % NB].rearrange("p k c -> p (k c)"),
                     wb[bass.ds(i * 4 + (m + NB), 1)].rearrange("a p c -> p (a c)")).then_inc(b_full[m % NB], 16)

    def a_wait(pe, n, i=None):
        pe.wait_ge(a_full[n % NA], 16 * (n // NA + 1) if i is None else i * 16 + 16 * (n // NA + 1))

    def b_wait(pe, n, i=None):
        pe.wait_ge(b_full[n % NB], 16 * (n // NB + 1) if i is None else i * 16 + 16 * (n // NB + 1))

    def rms_pe(pe, sem, squares, blocks, psum):
        pe.wait_ge(sem("squares"), 1)
        for k in range(blocks):
            mm = pe.matmul(psum, ones, squares[:, k, :], start=(k == 0), stop=(k == blocks - 1))
        mm.then_inc(sem("square_sums"), 1)

    def proj_pe(pe, sem, first, units, dst_token=(), src=None, c_units=None, acc=None):
        src = xm if src is None else src

        def unit(u, j, token, i=None):
            if i is not None or u >= 4:
                done = (sem("evac_act"), sem("evac_dve"))[j % 2]
                n = (j - 4) // 2 + 1
                pe.wait_ge(done, n if i is None else i * (NA // 2) + n)
            a_wait(pe, first + j, i)
            w = ringA[:, (first + j) % NA]
            bank = PS[:, j % 4, :]
            for b in range(2):
                for k in range(KC):
                    if token:
                        mm = pe.matmul(bank[:, b * 256:(b + 1) * 256], src[:, k, b * P:(b + 1) * P], w[:, k, :],
                                       start=(k == 0), stop=(k == KC - 1))
                    else:
                        mm = pe.matmul(bank[:, b * 256:(b + 1) * 256], w[:, k, b * P:(b + 1) * P], src[:, k, :],
                                       start=(k == 0), stop=(k == KC - 1))
            mm.then_inc(a_used, 1)
            if c_units and j % 2 and (i is not None or 2 <= u <= c_units[1] + 1):
                for cj in range(NC):
                    c_sum(pe, sem, acc, 16 + 2 * (c_units[0] + j - 3 + cj), cj, j - 3 + cj if i is not None else u - 3 + cj, i, NA) \
                        if i is not None else c_sum(pe, sem, acc, 16 + 2 * (c_units[0] + u - 3 + cj), cj, u - 3 + cj)

        turns = (units - NA) // NA
        for u in range(min(NA, units)):
            unit(u, u, u in dst_token)
        if turns > 0:
            with pe.Fori(1, turns + 1) as i:
                for j in range(NA):
                    unit(None, j, False, i)
        for u in range(NA + max(turns, 0) * NA, units):
            unit(u, u, u in dst_token)
        if c_units and units == c_units[1]:
            for cj in range(NC):
                m = c_units[1] - NC + cj
                c_sum(pe, sem, acc, 16 + 2 * (c_units[0] + m), cj, m)

    def proj_evac(eng, which, copy, sem, first, units, dst, c=None):
        name = ("evac_act", "evac_dve")[which]
        turns = units // NA

        def one(j, i=None):
            eng.wait_ge(a_used, first + j + 1 if i is None else i * NA + (first + j + 1))
            to = dst[:, 2 * j:2 * j + 2, :] if i is None else dst[:, bass.ds(i * (2 * NA) + 2 * j, 2), :]
            copy(to, PS[:, j % 4, :].rearrange("p (b t) -> p b t", b=2)).then_inc(sem(name), 1)
            if c and (i is not None or j < c[3][1]):
                for cj in range(NC):
                    c_scale(eng, sem, c[0], c[1], c[2](j - 1 + cj, i), c[3][0], cj, j - 1 + cj, i, NA)

        ahead = c[4] if c else 0
        if turns > 1:
            for j in range(which, ahead, 2):
                one(j)
            with eng.Fori(ahead // NA, turns) as i:
                for j in range(which, NA, 2):
                    one(j, i)
            done = turns * NA
        else:
            done = 0
        for j in range(done + which, units, 2):
            one(j)

    def mod_unit(pe, n, layer, bank, col):
        a_wait(pe, n)
        w = ringA[:, n % NA]
        for b in range(2):
            for k in range(KC):
                mm = pe.matmul(PS[:, bank, col + b:col + b + 1], w[:, k, b * P:(b + 1) * P],
                               cs[:, min(layer, 1), k:k + 1], start=(k == 0), stop=(k == KC - 1))
        mm.then_inc(a_used, 1)

    mods_flat = mods3[:, :, :].rearrange("p l c -> p (l c)")

    def mods_out(dve, sem, counter, count, bank, lo, hi, scales):
        dve.wait_ge(counter, count)
        dve.tensor_tensor(mods_flat[:, lo:hi], PS[:, bank, lo:hi], par[:, PAR["mod_b"][0] + lo:PAR["mod_b"][0] + hi], ALU.add).then_inc(sem("mods"), 1)
        dve.wait_ge(sem("mods"), 1)
        for layer, q, w in scales:
            at = 8 + 24 * q
            dve.scalar_tensor_tensor(normw3[:, layer, q, :], mods3[:, layer, at:at + 8], 1.0, w, ALU.add, ALU.mult
                                     ).then_inc(sem("normw"), 1)

    def c_loads(pool, sem, ringC, name):
        first, n = C_UNITS[name]
        for j in range(NC):
            pool.dma_start(ringC[:, j].rearrange("p k c -> p (k c)"), wc[first + j]).then_inc(c_full[j], 16)
        with pool.Fori(1, n // NC) as i:
            for j in range(NC):
                pool.wait_ge(sem("c_used"), i * NC + (j + 1 - NC))
                pool.dma_start(ringC[:, j].rearrange("p k c -> p (k c)"),
                               wc[bass.ds(i * NC + (first + j), 1)].rearrange("a p c -> p (a c)")
                               ).then_inc(c_full[j], 16)

    def c_scale(dve, sem, ringC, acc, c_of, first, j, m, i=None, per=0):
        plus = lambda v, r=1: v if i is None else i * (per * r) + v
        dve.wait_ge(c_full[j], plus(16 * ((first + m) // NC + 1), 16 // NC))
        if i is not None or m >= NC:
            dve.wait_ge(sem("c_summed"), plus(m - NC + 1))
        cc = c_of
        for k in range(KC):
            if k == 0:
                ins_ = dve.tensor_scalar(acc[:, j, :], ringC[:, j, k, :], cc[:, k:k + 1], None, ALU.mult)
            else:
                dve.wait_ge(sem("c_block"), plus((KC - 1) * m + k, KC - 1))
                ins_ = dve.scalar_tensor_tensor(acc[:, j, :], ringC[:, j, k, :], cc[:, k:k + 1], acc[:, j, :], ALU.mult, ALU.add)
            if k < KC - 1:
                ins_.then_inc(sem("c_block"), 1)
        ins_.then_inc(sem("c_used"), 1)

    def c_sum(pe, sem, acc, col, j, m, i=None, per=0):
        pe.wait_ge(sem("c_used"), m + 1 if i is None else i * per + (m + 1))
        for b in range(2):
            to = PS[:, 5, col + b:col + b + 1] if i is None else PS[:, 5, bass.ds(i * (2 * per) + (col + b), 1)]
            mm = pe.matmul(to, acc[:, j, b * P:(b + 1) * P], ones[:, 0:1], start=True, stop=True)
        mm.then_inc(sem("c_summed"), 1)

    def first_stage():
        sem = stages.begin()
        a0, n = A_AT["mod"]
        with nc.Block(no_gpsimd_drain=True) as block:
            @block.sync
            def _(sp):
                sp.dma_start(par[:, :], par_dram).then_inc(sem("par"), 16)
                for m in range(NA):
                    load_a(sp, m, m)
                sp.dma_start(h[:, :, :], x_dram).then_inc(sem("x"), 16)
                sp.dma_start(con[:, :], con_dram[:, 0:N_KEPT]).then_inc(sem("con"), 16)
                refill_a(sp, a0, n)
                for m in range(NB):
                    load_b(sp, m, m)
                sp.wait_ge(sem("con"), 16)
                sp.wait_ge(sem("x"), 16)

            @block.scalar
            def _(act):
                act.wait_ge(sem("par"), 16)
                act.activation(cs[:, 0, :], pr("c"), ACT.Silu).then_inc(sem("cs"), 1)
                act.activation(cs[:, 1, :], pr("c2"), ACT.Silu).then_inc(sem("cs"), 1)

            @block.tensor
            def _(pe):
                pe.wait_ge(sem("cs"), 2)
                for j in range(n):
                    mod_unit(pe, a0 + j, 0, 0, 2 * j)

            @block.vector
            def _(dve):
                dve.wait_ge(sem("par"), 16)
                mods_out(dve, sem, a_used, a0 + n, 0, 0, 16, [(0, 0, pr("norm_mix"))])
        stages.end()

    def norm_stage(which, layer):
        sem = stages.begin()
        with ExitStack() as st:
            squares = sb(f"squares{stages.k}", [P, KC, T], st)
            with nc.Block(no_gpsimd_drain=True) as block:
                @block.scalar
                def _(act):
                    act.activation(squares[:, :, :], h[:, :, :], ACT.Square).then_inc(sem("squares"), 1)
                    act.wait_ge(sem("square_sums"), 1)
                    act.activation(rstd[:, :], PS[:, 0, 0:T], ACT.Sqrt, bias=eps, scale=1.0 / D).then_inc(sem("root"), 1)

                @block.tensor
                def _(pe):
                    rms_pe(pe, sem, squares, KC, PS[:, 0, 0:T])

                @block.vector
                def _(dve):
                    link = Chain(dve, sem("dve"))
                    dve.wait_ge(sem("root"), 1)
                    link(dve.reciprocal(rstd[:, :], rstd[:, :]))
                    link(dve.tensor_tensor(squares[:, :, :], h[:, :, :], rep(rstd[:, :], KC), ALU.mult))
                    for k in range(KC):
                        dve.tensor_scalar(xm[:, k, :], squares[:, k, :], normw3[:, layer, which, k:k + 1],
                                          mods3[:, layer, 24 * which + k:24 * which + k + 1], ALU.mult, ALU.add
                                          ).then_inc(sem("xm"), 1)
        stages.end()

    def norm_h(w, dst):
        sem = stages.begin()
        with ExitStack() as st:
            squares = sb(f"squares{stages.k}", [P, KC, T], st)
            with nc.Block(no_gpsimd_drain=True) as block:
                @block.scalar
                def _(act):
                    act.activation(squares[:, :, :], h[:, :, :], ACT.Square).then_inc(sem("squares"), 1)
                    act.wait_ge(sem("square_sums"), 1)
                    act.activation(rstd[:, :], PS[:, 0, 0:T], ACT.Sqrt, bias=eps, scale=1.0 / D).then_inc(sem("root"), 1)

                @block.tensor
                def _(pe):
                    rms_pe(pe, sem, squares, KC, PS[:, 0, 0:T])

                @block.vector
                def _(dve):
                    link = Chain(dve, sem("dve"))
                    dve.wait_ge(sem("root"), 1)
                    link(dve.reciprocal(rstd[:, :], rstd[:, :]))
                    link(dve.tensor_tensor(squares[:, :, :], h[:, :, :], rep(rstd[:, :], KC), ALU.mult))
                    for k in range(KC):
                        dve.tensor_scalar(dst[:, k, :], squares[:, k, :], w[:, k:k + 1], None, ALU.mult
                                          ).then_inc(sem("normed"), 1)

                if dst is not h:
                    @block.sync
                    def _(sp):
                        sp.wait_ge(sem("normed"), KC)
                        sp.dma_start(out, dst[:, :, :]).then_inc(sem("stored"), 16)
                        sp.wait_ge(sem("stored"), 16)
        stages.end()

    def mixer_one():
        with ExitStack() as st:
            proj = sb("proj", [P, 64, T], st)
            gab = sb("gab", [P, 2, 8], st)
            sem = stages.begin()
            a0, n = A_AT["win"]
            w_ab = pr("w_ab").rearrange("p (k c) -> p k c", k=KC)
            cst = ExitStack()
            ringC, acc = sb("ringC1", [P, NC, KC, 256], cst), sb("acc1", [P, NC, 256], cst)
            with nc.Block(no_gpsimd_drain=True) as block:
                @block.gpsimd
                def _(pool):
                    c_loads(pool, sem, ringC, "win")

                @block.sync
                def _(sp):
                    refill_a(sp, a0, n)

                @block.tensor
                def _(pe):
                    for t in range(2):
                        for k in range(KC):
                            mm = pe.matmul(PS[:, 4, t * 8:t * 8 + 8], xm[:, k, t * P:(t + 1) * P], w_ab[:, k, :],
                                           start=(k == 0), stop=(k == KC - 1))
                    mm.then_inc(sem("gab_done"), 1)
                    proj_pe(pe, sem, a0, n, dst_token=(4, 5, 6, 7), c_units=C_UNITS["win"], acc=acc)

                @block.scalar
                def _(act):
                    proj_evac(act, 0, act.copy, sem, a0, n, proj)

                @block.vector
                def _(dve):
                    dve.wait_ge(sem("gab_done"), 1)
                    dve.tensor_copy(gab[:, :, :], PS[:, 4, 0:16].rearrange("p (t c) -> p t c", t=2)).then_inc(sem("gab"), 1)
                    proj_evac(dve, 1, dve.tensor_copy, sem, a0, n, proj,
                              (ringC, acc, lambda m, i: cs[:, 0 if i is None and m < 16 else 1, :], C_UNITS["win"], 16))
                    mods_out(dve, sem, sem("c_summed"), 32, 5, 16, 80, [(0, 1, pr("norm_ffn")), (1, 0, pr("norm_mix2", 0, 8))])
            cst.close()
            stages.end()
            mix = sb("mix", [P, KC, T], st)
            retention(proj, mix)
            delta_rule(proj, gab, mix)
            out_proj("wout", mix, None, 0)

    def out_proj(name, src, bias, layer):
        sem = stages.begin()
        a0, n = A_AT[name]
        with ExitStack() as st:
            biased = sb(f"biased{stages.k}", [P, KC, T], st) if bias is not None else None
            with nc.Block(no_gpsimd_drain=True) as block:
                @block.sync
                def _(sp):
                    refill_a(sp, a0, n)

                @block.tensor
                def _(pe):
                    proj_pe(pe, sem, a0, n, src=src)

                @block.vector
                def _(dve):
                    for b in range(KC):
                        dve.wait_ge(a_used, a0 + b // 2 + 1)
                        psum = PS[:, b // 2, (b % 2) * T:(b % 2 + 1) * T]
                        gate = mods3[:, layer, 16 + b:17 + b]
                        if bias is None:
                            dve.scalar_tensor_tensor(h[:, b, :], psum, gate, h[:, b, :], ALU.mult, ALU.add
                                                     ).then_inc(sem("h"), 1)
                        else:
                            dve.tensor_scalar(biased[:, b, :], psum, bias[:, b:b + 1], gate, ALU.add, ALU.mult
                                              ).then_inc(sem("biased"), 1)
                            dve.wait_ge(sem("biased"), b + 1)
                            dve.tensor_tensor(h[:, b, :], h[:, b, :], biased[:, b, :], ALU.add).then_inc(sem("h"), 1)
            stages.end()

    def retention(proj, mix):
        sem = stages.begin()
        with ExitStack() as st:
            at0 = CON["cos"][0]
            rcon = sb("rcon", [P, CON["strict"][0] - at0], st)

            def rc(name):
                at, w = CON[name]
                return rcon[:, at - at0:at - at0 + w]

            cos, sin, turn = rc("cos"), rc("sin"), rc("turn")
            ret = rc("ret").rearrange("p (h i) -> p h i", h=HEADS)
            turned = xm
            qk = proj[:, 0:8, :]
            S = proj[:, 0:6, :].rearrange("p a b -> p (a b)").rearrange("p (h i) -> p h i", h=HEADS)
            with nc.Block(no_gpsimd_drain=True) as block:
                @block.sync
                def _(sp):
                    sp.dma_start(rcon[:, :], con_dram[:, at0:CON["strict"][0]]).then_inc(sem("rcon"), 16)

                @block.tensor
                def _(pe):
                    pe.wait_ge(sem("rcon"), 16)
                    for b in range(8):
                        mm = pe.matmul(PS[:, b // 2, (b % 2) * T:(b % 2 + 1) * T], turn, qk[:, b, :], start=True, stop=True)
                    mm.then_inc(sem("halves_swapped"), 1)
                    pe.wait_ge(sem("roped"), 1)
                    for hd in range(HEADS):
                        q, k = qk[:, hd, :], qk[:, 4 + hd, :]
                        pe.matmul(PS[:, 4 + hd, 0:T], k[:, 0:P], q, start=True, stop=True)
                        pe.matmul(PS[:, 4 + hd, T:384], k[:, P:T], q[:, P:T], start=True, stop=True
                                  ).then_inc(sem("scores"), 1)
                    for hd in range(HEADS):
                        pe.wait_ge(sem("decayed"), hd + 1)
                        for b in range(2):
                            o = PS[:, hd, b * T:(b + 1) * T]
                            v = [proj[:, 8 + 2 * hd + t, b * P:(b + 1) * P] for t in range(2)]
                            pe.matmul(o, v[0], S[:, hd, 0:T], start=True, stop=False, skip_group_check=True)
                            mm = pe.matmul(o[:, P:T], v[1], S[:, hd, T:384], start=False, stop=True, skip_group_check=True)
                        mm.then_inc(sem("outputs"), 1)
                    for hd in range(HEADS):
                        pe.wait_ge(sem("squares"), hd + 1)
                        for b in range(2):
                            mm = pe.matmul(PS[:, 4 + hd // 2, (hd % 2) * T:(hd % 2 + 1) * T], ones, turned[:, 2 * hd + b, :],
                                           start=(b == 0), stop=(b == 1))
                        mm.then_inc(sem("square_sums"), 1)

                @block.scalar
                def _(act):
                    act.activation(proj[:, 16:24, :], proj[:, 16:24, :], ACT.Silu).then_inc(sem("silu"), 1)
                    for hd in range(HEADS):
                        act.wait_ge(sem("outputs"), hd + 1)
                        act.activation(turned[:, 2 * hd:2 * hd + 2, :], PS[:, hd, :].rearrange("p (b t) -> p b t", b=2),
                                       ACT.Square).then_inc(sem("squares"), 1)
                    act.wait_ge(sem("square_sums"), HEADS)
                    act.activation(S[:, :, 0:T].rearrange("p h i -> p h i"), PS[:, 4:6, :].rearrange("p a (b t) -> p (a b) t", b=2),
                                   ACT.Sqrt, bias=eps, scale=1.0 / 256).then_inc(sem("root"), 1)

                @block.vector
                def _(dve):
                    link = Chain(dve, sem("dve"))
                    dve.wait_ge(sem("halves_swapped"), 1)
                    dve.tensor_tensor(turned[:, :, :], PS[:, 0:4, :].rearrange("p a (b t) -> p (a b) t", b=2), rep(sin, 8),
                                      ALU.mult).then_inc(sem("turned"), 1)
                    link(dve.tensor_tensor(qk, qk, rep(cos, 8), ALU.mult))
                    dve.wait_ge(sem("turned"), 1)
                    dve.tensor_tensor(qk, qk, turned[:, :, :], ALU.add).then_inc(sem("roped"), 1)
                    dve.wait_ge(sem("scores"), HEADS)
                    for hd in range(HEADS):
                        dve.tensor_tensor(S[:, hd, :], PS[:, 4 + hd, 0:384], ret[:, hd, :], ALU.mult).then_inc(sem("decayed"), 1)
                    dve.wait_ge(sem("root"), 1)
                    link(dve.reciprocal(S[:, :, 0:T], S[:, :, 0:T]))
                    dve.wait_ge(sem("silu"), 1)
                    for hd in range(HEADS):
                        link(dve.tensor_tensor(mix[:, 2 * hd:2 * hd + 2, :], PS[:, hd, :].rearrange("p (b t) -> p b t", b=2),
                                               rep(S[:, hd, 0:T], 2), ALU.mult))
                    dve.tensor_tensor(mix[:, :, :], mix[:, :, :], proj[:, 16:24, :], ALU.mult).then_inc(sem("mix"), 1)
        stages.end()

    def delta_rule(proj, gab, mix):
        C8 = 2 * HEADS
        with ExitStack() as st:
            cv = proj[:, 0:16, :]
            sem = stages.begin()
            squares = proj[:, 16:24, :]
            vtok = xm[:, :, :]
            ktok = sb("ktok", [P, HEADS, P], st)
            small = sb("small", [P, 120], st)
            ld = small[:, 0:8]
            beta = small[:, 8:16]
            t0, t1, t2, t3, t4 = [small[:, 16 + 8 * i:24 + 8 * i] for i in range(5)]
            nea = small[:, 56:60]
            gcc = small[:, 64:72]
            nbe = small[:, 72:80]
            ekd = small[:, 80:88]
            with nc.Block(no_gpsimd_drain=True) as block:
                @block.vector
                def _(dve):
                    link = Chain(dve, sem("dve"))
                    cw = pr("gconv").rearrange("p (b i) -> p b i", b=16)
                    for tap in range(4):
                        for b in range(16):
                            x = proj[:, 24 + b, :]
                            if tap == 0:
                                i = dve.tensor_scalar(cv[:, b, :], x, cw[:, b, 3:4], None, ALU.mult)
                            else:
                                dve.wait_ge(sem("conv"), 16 * (tap - 1) + b + 1)
                                i = dve.scalar_tensor_tensor(cv[:, b, tap:T], x[:, 0:T - tap], cw[:, b, 3 - tap:4 - tap],
                                                             cv[:, b, tap:T], ALU.mult, ALU.add)
                            i.then_inc(sem("conv"), 1)
                    ga = gab[:, :, 0:4].rearrange("p t c -> p t c")
                    s2 = lambda a: a.rearrange("p (t c) -> p t c", t=2)
                    link(dve.tensor_tensor(s2(t0), ga, rep(pr("dt_bias"), 2), ALU.add))
                    link(dve.tensor_scalar(t1, t0, -1.0, None, ALU.mult))
                    link(dve.tensor_tensor(t1, t0, t1, ALU.min))
                    dve.tensor_scalar(t4, t0, 0.0, None, ALU.max).then_inc(sem("minus_abs"), 1)
                    dve.wait_ge(sem("exp_minus_abs"), 1)
                    link(dve.tensor_scalar(t2, t1, 1.0, None, ALU.add))
                    link(dve.tensor_scalar(t3, t2, -1.0, None, ALU.add))
                    link(dve.tensor_scalar(t0, t3, 0.0, None, ALU.is_equal))
                    dve.tensor_tensor(t3, t3, t0, ALU.add).then_inc(sem("u_minus_1"), 1)
                    dve.wait_ge(sem("ln_u"), 1)
                    link(dve.tensor_tensor(t2, t2, t0, ALU.add))
                    link(dve.reciprocal(t3, t3))
                    link(dve.tensor_tensor(t2, t2, t3, ALU.mult))
                    link(dve.tensor_tensor(t2, t2, t1, ALU.mult))
                    link(dve.tensor_tensor(t2, t2, t4, ALU.add))
                    link(dve.tensor_scalar(nea, nea, -1.0, None, ALU.mult))
                    dve.tensor_tensor(s2(ld), s2(t2), rep(nea, 2), ALU.mult).then_inc(sem("ld"), 1)
                    for q in range(2):
                        dve.wait_ge(sem("root"), q + 1)
                        link(dve.reciprocal(squares[:, 4 * q:4 * q + 4, :], squares[:, 4 * q:4 * q + 4, :]))
                        if q == 0:
                            i = dve.scalar_tensor_tensor(cv[:, 0:4, :], cv[:, 0:4, :], float(P) ** -0.5, squares[:, 0:4, :],
                                                         ALU.mult, ALU.mult)
                        else:
                            i = dve.tensor_tensor(cv[:, 4:8, :], cv[:, 4:8, :], squares[:, 4:8, :], ALU.mult)
                        i.then_inc(sem("qk_normed"), 1)
                    for c in range(2):
                        for hd in range(HEADS):
                            if hd % 2 == 0:
                                dve.wait_ge(sem("v_turned"), 2 * c + hd // 2 + 1)
                            dve.tensor_scalar(vtok[:, 4 * c + hd, :], PS[:, 4 + 2 * c + hd // 2, (hd % 2) * 256:(hd % 2 + 1) * 256],
                                              beta[:, 4 * c + hd:4 * c + hd + 1], None, ALU.mult).then_inc(sem("vtok"), 1)
                    dve.wait_ge(sem("gcc_done"), 1)
                    dve.tensor_copy(gcc, PS[:, 3, 0:8]).then_inc(sem("gcc"), 1)
                    dve.wait_ge(sem("k_turned"), 1)
                    dve.tensor_copy(ktok[:, :, :], PS[:, 0, :].rearrange("p (h d) -> p h d", h=HEADS)).then_inc(sem("ktok"), 1)

                @block.scalar
                def _(act):
                    act.activation(proj[:, 48:64, :], proj[:, 48:64, :], ACT.Sigmoid).then_inc(sem("act"), 1)
                    act.activation(beta.rearrange("p (t c) -> p t c", t=2), gab[:, :, 4:8], ACT.Sigmoid).then_inc(sem("beta"), 1)
                    act.activation(proj[:, 40:48, :], proj[:, 40:48, :], ACT.Silu).then_inc(sem("act"), 1)
                    act.wait_ge(sem("conv"), 64)
                    act.activation(cv, cv, ACT.Silu).then_inc(sem("silu"), 1)
                    act.wait_ge(sem("silu"), 1)
                    act.activation(squares, cv[:, 0:8, :], ACT.Square).then_inc(sem("squares"), 1)
                    act.activation(nea, pr("a_log"), ACT.Exp).then_inc(sem("act"), 1)
                    act.wait_ge(sem("minus_abs"), 1)
                    act.activation(t1, t1, ACT.Exp).then_inc(sem("exp_minus_abs"), 1)
                    act.wait_ge(sem("u_minus_1"), 1)
                    act.activation(t2, t2, ACT.Ln).then_inc(sem("ln_u"), 1)
                    for q in range(2):
                        act.wait_ge(sem("square_sums"), 4 * q + 4)
                        act.activation(squares[:, 4 * q:4 * q + 4, :], PS[:, 2 * q:2 * q + 2, :].rearrange("p a (b t) -> p (a b) t", b=2),
                                       ACT.Sqrt, bias=eps).then_inc(sem("root"), 1)

                @block.tensor
                def _(pe):
                    pe.wait_ge(sem("squares"), 1)
                    for b in range(8):
                        pe.matmul(PS[:, b // 2, (b % 2) * T:(b % 2 + 1) * T], ones, squares[:, b, :], start=True, stop=True
                                  ).then_inc(sem("square_sums"), 1)
                    for c in range(2):
                        for hd in range(HEADS):
                            for b in range(2):
                                mm = pe.transpose(PS[:, 4 + 2 * c + hd // 2, (hd % 2) * 256 + b * P:(hd % 2) * 256 + (b + 1) * P],
                                                  cv[:, 8 + 2 * hd + b, c * P:(c + 1) * P], ident)
                            if hd % 2:
                                mm.then_inc(sem("v_turned"), 1)
                    pe.wait_ge(sem("root"), 2)
                    pe.wait_ge(sem("ld"), 1)
                    pe.matmul(PS[:, 3, 0:8], upto[:, 0, 0:P], ld, start=True, stop=True).then_inc(sem("gcc_done"), 1)
                    pe.wait_ge(sem("qk_normed"), 2)
                    for hd in range(HEADS):
                        mm = pe.transpose(PS[:, 0, hd * P:(hd + 1) * P], cv[:, 4 + hd, 0:P], ident)
                    mm.then_inc(sem("k_turned"), 1)
            stages.end()

            sem = stages.begin()
            at0 = CON["strict"][0]
            gcon = sb("gcon", [P, CON["bucket"][0] - at0], st)
            strict = gcon[:, 0:P]
            levels = gcon[:, P:].rearrange("p (n i) -> p n i", n=7)
            V4 = lambda a: proj[:, a:a + 4, :].rearrange("p a (b i) -> p (a b) i", b=2)
            dec, LT, M, MT = V4(24), V4(28), V4(32), V4(36)
            QK = V4(16)
            Loff, Pm = V4(20), sb("Pm", [P, C8, P], st)
            egB = sb("egB", [P, HEADS, P], st)
            two = lambda b: PS[:, b:b + 2, :].rearrange("p a (c i) -> p (a c) i", c=4)
            with nc.Block(no_gpsimd_drain=True) as block:
                @block.sync
                def _(sp):
                    sp.dma_start(gcon[:, :], con_dram[:, at0:CON["bucket"][0]]).then_inc(sem("gcon"), 16)

                @block.tensor
                def _(pe):
                    for q in range(C8):
                        c, hd = q // 4, q % 4
                        kc = cv[:, 4 + hd, c * P:(c + 1) * P]
                        at = slice((q % 4) * P, (q % 4 + 1) * P)
                        pe.matmul(PS[:, c, at], ld[:, q:q + 1].to_broadcast([P, P]), upto[:, 0, 0:P], start=True, stop=True)
                        pe.matmul(PS[:, 2 + c, at], beta[:, q:q + 1].to_broadcast([P, P]), ident, start=True, stop=True)
                        pe.matmul(PS[:, 4 + c, at], kc, kc, start=True, stop=True)
                        mm = pe.matmul(PS[:, 6 + c, at], kc, cv[:, hd, c * P:(c + 1) * P], start=True, stop=True)
                    mm.then_inc(sem("products"), 1)
                    pe.wait_ge(sem("MT"), 1)
                    for q in range(C8):
                        mm = pe.transpose(PS[:, q // 4, (q % 4) * P:(q % 4 + 1) * P], MT[:, q, :], ident)
                    mm.then_inc(sem("M_turned"), 1)
                    for n in range(1, 7):
                        pe.wait_ge(sem("M"), n)
                        pe.wait_ge(sem("MT"), n)
                        pe.wait_ge(sem("Loff"), n)
                        for q in range(C8):
                            mm = pe.matmul(PS[:, 2 + q // 4, (q % 4) * P:(q % 4 + 1) * P], Loff[:, q, :], M[:, q, :],
                                           start=True, stop=True)
                        mm.then_inc(sem("P_done"), 1)
                        pe.wait_ge(sem("P"), n)
                        for q in range(C8):
                            mm = pe.matmul(PS[:, 4 + q // 4, (q % 4) * P:(q % 4 + 1) * P], Pm[:, q, :], MT[:, q, :],
                                           start=True, stop=True)
                        mm.then_inc(sem("N2_done"), 1)
                        if n < 6:
                            for q in range(C8):
                                mm = pe.matmul(PS[:, 6 + q // 4, (q % 4) * P:(q % 4 + 1) * P], MT[:, q, :], Pm[:, q, :],
                                               start=True, stop=True)
                            mm.then_inc(sem("N1_done"), 1)

                @block.scalar
                def _(act):
                    act.wait_ge(sem("products"), 1)
                    act.activation(egB[:, :, :], PS[:, 1, :].rearrange("p (h i) -> p h i", h=HEADS), ACT.Exp).then_inc(sem("egB"), 1)
                    act.activation(ekd[:, 4:8], gcc[:, 4:8], ACT.Exp).then_inc(sem("egc"), 1)
                    act.wait_ge(sem("last_less"), 1)
                    act.activation(ekd[:, 0:4], ekd[:, 0:4], ACT.Exp).then_inc(sem("act"), 1)
                    act.wait_ge(sem("less"), C8)
                    act.activation(dec, dec, ACT.Exp).then_inc(sem("decays"), 1)
                    for n in range(1, 7):
                        act.wait_ge(sem("P_done"), n)
                        if n > 1:
                            act.wait_ge(sem("N2_done"), n - 1)
                            act.wait_ge(sem("N1_done"), n - 1)
                        act.copy(Pm[:, :, :], two(2)).then_inc(sem("P"), 1)

                @block.vector
                def _(dve):
                    link = Chain(dve, sem("dve"))
                    dve.wait_ge(sem("products"), 1)
                    for q in range(C8):
                        if q == 4:
                            dve.wait_ge(sem("egB"), 1)
                        dve.tensor_scalar(dec[:, q, :], PS[:, q // 4, (q % 4) * P:(q % 4 + 1) * P], gcc[:, q:q + 1], 0.0,
                                          ALU.subtract, ALU.min).then_inc(sem("less"), 1)
                    dve.tensor_tensor(ekd[:, 0:4], PS[:, 0, P - 1:512:P], gcc[:, 0:4], ALU.subtract).then_inc(sem("last_less"), 1)
                    dve.wait_ge(sem("egc"), 1)
                    dve.scalar_tensor_tensor(nbe[:, 4:8], ekd[:, 4:8], -1.0, beta[:, 4:8], ALU.mult, ALU.mult).then_inc(sem("nbe"), 1)
                    dve.wait_ge(sem("decays"), 1)
                    link(dve.tensor_tensor(dec, dec, rep(upto[:, 0, 0:P], C8), ALU.mult))
                    dve.tensor_tensor(QK, two(6), dec, ALU.mult).then_inc(sem("QK"), 1)
                    link(dve.tensor_tensor(LT, two(4), dec, ALU.mult))
                    link(dve.tensor_tensor(LT, LT, two(2), ALU.mult))
                    dve.wait_ge(sem("gcon"), 16)
                    link(dve.tensor_tensor(LT, LT, rep(strict, C8), ALU.mult))
                    link(dve.tensor_tensor(MT, LT, rep(levels[:, 0, :], C8), ALU.mult))
                    dve.scalar_tensor_tensor(MT, MT, -1.0, rep(ident, C8), ALU.mult, ALU.add).then_inc(sem("MT"), 1)
                    dve.tensor_tensor(Loff, LT, rep(levels[:, 1, :], C8), ALU.mult).then_inc(sem("Loff"), 1)
                    dve.wait_ge(sem("M_turned"), 1)
                    dve.tensor_copy(M, two(0)).then_inc(sem("M"), 1)
                    for n in range(1, 7):
                        if n < 6:
                            dve.wait_ge(sem("P_done"), n)
                            dve.tensor_tensor(Loff, LT, rep(levels[:, n + 1, :], C8), ALU.mult).then_inc(sem("Loff"), 1)
                            dve.wait_ge(sem("N1_done"), n)
                            dve.wait_ge(sem("M"), n)
                            dve.tensor_tensor(M, M, two(6), ALU.subtract).then_inc(sem("M"), 1)
                        dve.wait_ge(sem("N2_done"), n)
                        dve.wait_ge(sem("MT"), n)
                        dve.tensor_tensor(MT, MT, two(4), ALU.subtract).then_inc(sem("MT"), 1)
            stages.end()

            sem = stages.begin()
            vn = Pm[:, :, :].rearrange("p a b -> p (a b)").rearrange("p (h v) -> p h v", h=HEADS)
            vs = dec.rearrange("p a b -> p (a b)").rearrange("p (h v) -> p h v", h=HEADS)
            state = M.rearrange("p a b -> p (a b)").rearrange("p (h v) -> p h v", h=HEADS)
            rhs = Loff.rearrange("p a b -> p (a b)").rearrange("p (h v) -> p h v", h=HEADS)
            qg = LT[:, 0:4, :]
            sq = cv[:, 8:16, :]
            r4 = proj[:, 24:28, :]
            y = cv[:, 0:8, :]
            heads2 = lambda b: PS[:, b:b + 2, :].rearrange("p a (c v) -> p (a c) v", c=2)
            o_of = lambda hd, b, c: PS[:, 4 + hd, b * T + c * P:b * T + (c + 1) * P]
            with nc.Block(no_gpsimd_drain=True) as block:
                @block.tensor
                def _(pe):
                    for hd in range(HEADS):
                        mm = pe.matmul(PS[:, hd // 2, (hd % 2) * 256:(hd % 2 + 1) * 256], MT[:, hd, :], vtok[:, hd, :], start=True, stop=True)
                    mm.then_inc(sem("u_done"), 1)
                    pe.wait_ge(sem("vs"), HEADS)
                    for hd in range(HEADS):
                        mm = pe.matmul(PS[:, 2 + hd // 2, (hd % 2) * 256:(hd % 2 + 1) * 256], ktok[:, hd, :], vs[:, hd, :], start=True, stop=True)
                    mm.then_inc(sem("state_done"), 1)
                    pe.wait_ge(sem("vn"), 1)
                    for hd in range(HEADS):
                        for b in range(2):
                            mm = pe.matmul(o_of(hd, b, 0), vn[:, hd, b * P:(b + 1) * P], QK[:, hd, :], start=True, stop=True)
                    mm.then_inc(sem("o0_done"), 1)
                    pe.wait_ge(sem("state"), 1)
                    for hd in range(HEADS):
                        mm = pe.matmul(PS[:, hd // 2, (hd % 2) * 256:(hd % 2 + 1) * 256], cv[:, 4 + hd, P:T], state[:, hd, :], start=True, stop=True)
                    mm.then_inc(sem("ks_done"), 1)
                    pe.wait_ge(sem("rhs"), HEADS)
                    for hd in range(HEADS):
                        mm = pe.matmul(PS[:, 2 + hd // 2, (hd % 2) * 256:(hd % 2 + 1) * 256], MT[:, 4 + hd, :], rhs[:, hd, :], start=True, stop=True)
                    mm.then_inc(sem("u1_done"), 1)
                    pe.wait_ge(sem("vn"), 2)
                    pe.wait_ge(sem("qg"), 1)
                    for hd in range(HEADS):
                        for b in range(2):
                            pe.matmul(o_of(hd, b, 1), vn[:, hd, b * P:(b + 1) * P], QK[:, 4 + hd, :], start=True, stop=False)
                            mm = pe.matmul(o_of(hd, b, 1), state[:, hd, b * P:(b + 1) * P], qg[:, hd, :], start=False, stop=True)
                        mm.then_inc(sem("o_done"), 1)
                    for hd in range(HEADS):
                        pe.wait_ge(sem("squares"), hd + 1)
                        for b in range(2):
                            mm = pe.matmul(PS[:, hd // 2, (hd % 2) * T:(hd % 2 + 1) * T], ones, sq[:, 2 * hd + b, :],
                                           start=(b == 0), stop=(b == 1))
                        mm.then_inc(sem("square_sums"), 1)

                @block.scalar
                def _(act):
                    act.wait_ge(sem("u_done"), 1)
                    act.copy(vn[:, :, :], heads2(0)).then_inc(sem("vn"), 1)
                    act.wait_ge(sem("state_done"), 1)
                    act.copy(state, heads2(2)).then_inc(sem("state"), 1)
                    act.wait_ge(sem("u1_done"), 1)
                    act.wait_ge(sem("o0_done"), 1)
                    act.wait_ge(sem("vs"), HEADS)
                    act.copy(vn[:, :, :], heads2(2)).then_inc(sem("vn"), 1)
                    for hd in range(HEADS):
                        act.wait_ge(sem("o_done"), hd + 1)
                        act.activation(sq[:, 2 * hd:2 * hd + 2, :], PS[:, 4 + hd, :].rearrange("p (b t) -> p b t", b=2),
                                       ACT.Square).then_inc(sem("squares"), 1)
                    act.wait_ge(sem("square_sums"), HEADS)
                    act.activation(r4, PS[:, 0:2, :].rearrange("p a (b t) -> p (a b) t", b=2), ACT.Sqrt, bias=eps, scale=1.0 / 256
                                   ).then_inc(sem("root"), 1)

                @block.vector
                def _(dve):
                    link = Chain(dve, sem("dve"))
                    dve.tensor_tensor(qg, cv[:, 0:4, P:T], egB[:, :, :], ALU.mult).then_inc(sem("qg"), 1)
                    dve.wait_ge(sem("vn"), 1)
                    for hd in range(HEADS):
                        dve.tensor_scalar(vs[:, hd, :], vn[:, hd, :], ekd[:, hd:hd + 1], None, ALU.mult).then_inc(sem("vs"), 1)
                    dve.wait_ge(sem("ks_done"), 1)
                    for hd in range(HEADS):
                        dve.scalar_tensor_tensor(rhs[:, hd, :], PS[:, hd // 2, (hd % 2) * 256:(hd % 2 + 1) * 256],
                                                 nbe[:, 4 + hd:5 + hd], vtok[:, 4 + hd, :], ALU.mult, ALU.add).then_inc(sem("rhs"), 1)
                    dve.wait_ge(sem("root"), 1)
                    link(dve.reciprocal(r4, r4))
                    for hd in range(HEADS):
                        for b in range(2):
                            i = dve.scalar_tensor_tensor(y[:, 2 * hd + b, :], PS[:, 4 + hd, b * T:(b + 1) * T],
                                                         pr("gdn_w", b, b + 1), r4[:, hd, :], ALU.mult, ALU.mult)
                    link(i)
                    link(dve.tensor_tensor(y, y, proj[:, 40:48, :], ALU.mult))
                    link(dve.tensor_tensor(y, y, proj[:, 56:64, :], ALU.mult))
                    link(dve.tensor_tensor(mix[:, :, :], mix[:, :, :], proj[:, 48:56, :], ALU.mult))
                    dve.tensor_tensor(mix[:, :, :], mix[:, :, :], y, ALU.add).then_inc(sem("mix"), 1)
            stages.end()

    def down_pe(pe, b_slot, rhs_blocks, first, last):
        for kf in range(2):
            for ob in range(KC):
                mm = pe.matmul(PS[:, 4 + ob // 2, (ob % 2) * T:(ob % 2 + 1) * T], ringB[:, b_slot, kf, ob * P:(ob + 1) * P],
                               rhs_blocks[kf], start=(first and kf == 0 and ob % 2 == 0), stop=last,
                               skip_group_check=True)
        mm.then_inc(b_used, 1)

    def swiglu(name, steps, combB, layer):
        sem = stages.begin()
        a0, b0 = A_AT[name][0], B_AT[name][0]
        with ExitStack() as st:
            silu = sb(f"silu{stages.k}", [P, 2, 512], st)
            act_ = sb(f"act{stages.k}", [P, 2, 2, T], st)
            tail = steps % 4
            turns = steps // 4
            with nc.Block(no_gpsimd_drain=True) as block:
                @block.sync
                def _(sp):
                    refill_ab(sp, a0, b0, steps)

                def pe_step(pe, s, i=None):
                    plus = lambda v, per: v if i is None else i * per + v
                    if i is not None or s >= 2:
                        pe.wait_ge(sem("hidden"), plus(s - 1, 4))
                    for j in range(2):
                        m = a0 + 2 * s + j
                        a_wait(pe, m, i)
                        w = ringA[:, m % NA]
                        for b in range(2):
                            for k in range(KC):
                                mm = pe.matmul(PS[:, 2 * (s % 2) + j, b * T:(b + 1) * T], w[:, k, b * P:(b + 1) * P], xm[:, k, :],
                                               start=(k == 0), stop=(k == KC - 1))
                        mm.then_inc(a_used, 1)
                    if i is not None or s >= 1:
                        down(pe, s - 1, i, first=(i is None and s == 1), last=False)

                def down(pe, s, i, first, last):
                    b_wait_at = b0 + s
                    b_wait(pe, b_wait_at, i)
                    pe.wait_ge(sem("hidden"), s + 1 if i is None else i * 4 + (s + 1))
                    down_pe(pe, b_wait_at % NB, [act_[:, s % 2, kf, :] for kf in range(2)], first, last)

                @block.tensor
                def _(pe):
                    for s in range(4):
                        pe_step(pe, s)
                    if turns > 2:
                        with pe.Fori(1, turns) as i:
                            for s in range(4):
                                pe_step(pe, s, i)
                        done = 4 * turns
                    else:
                        done = 4
                    for s in range(done, steps):
                        pe_step(pe, s)
                    down(pe, steps - 1, None, False, True)

                @block.scalar
                def _(act):
                    def step(s, i=None):
                        act.wait_ge(a_used, a0 + 2 * s + 1 if i is None else i * 8 + (a0 + 2 * s + 1))
                        if i is not None or s >= 2:
                            act.wait_ge(sem("hidden"), s - 1 if i is None else i * 4 + (s - 1))
                        act.activation(silu[:, s % 2, :], PS[:, 2 * (s % 2), :], ACT.Silu).then_inc(sem("silu"), 1)

                    for s in range(4):
                        step(s)
                    with act.Fori(1, turns) as i:
                        for s in range(4):
                            step(s, i)
                    for s in range(4 * turns, steps):
                        step(s)

                @block.vector
                def _(dve):
                    def step(s, i=None):
                        plus = lambda v, per: v if i is None else i * per + v
                        hid = act_[:, s % 2, :, :]
                        dve.wait_ge(a_used, plus(a0 + 2 * s + 2, 8))
                        dve.wait_ge(sem("silu"), plus(s + 1, 4))
                        if i is not None or s >= 2:
                            dve.wait_ge(b_used, plus(b0 + s - 1, 4))
                        if combB is None:
                            dve.tensor_tensor(hid, silu[:, s % 2, :].rearrange("p (b t) -> p b t", b=2),
                                              PS[:, 2 * (s % 2) + 1, :].rearrange("p (b t) -> p b t", b=2), ALU.mult
                                              ).then_inc(sem("hidden"), 1)
                        else:
                            dve.tensor_tensor(hid, silu[:, s % 2, :].rearrange("p (b t) -> p b t", b=2),
                                              PS[:, 2 * (s % 2) + 1, :].rearrange("p (b t) -> p b t", b=2), ALU.mult
                                              ).then_inc(sem("unweighted"), 1)
                            dve.wait_ge(sem("unweighted"), plus(s + 1, 4))
                            for b in range(2):
                                comb = combB[:, s // 2, :] if i is None else combB[:, bass.ds(i * 2 + s // 2, 1), :].rearrange("p a t -> p (a t)")
                                ins_ = dve.tensor_tensor(hid[:, b, :], hid[:, b, :], comb, ALU.mult)
                            ins_.then_inc(sem("hidden"), 1)

                    for s in range(4):
                        step(s)
                    with dve.Fori(1, turns) as i:
                        for s in range(4):
                            step(s, i)
                    for s in range(4 * turns, steps):
                        step(s)
                    dve.wait_ge(b_used, b0 + steps)
                    for b in range(KC):
                        dve.scalar_tensor_tensor(h[:, b, :], PS[:, 4 + b // 2, (b % 2) * T:(b % 2 + 1) * T], mods3[:, layer, 40 + b:41 + b],
                                                 h[:, b, :], ALU.mult, ALU.add).then_inc(sem("h"), 1)
            stages.end()

    def moe():
        with ExitStack() as st:
            combB = sb("combB", [P, N_EXP, T], st)
            w = sb("route", [P, 2, 80], st)
            sem = stages.begin()
            wr = pr("w_route").rearrange("p (k c) -> p k c", k=KC)
            lg = w[:, :, 0:20]
            eq, pre, oh = w[:, :, 20:24], w[:, :, 24:28], w[:, :, 28:32]
            el, pe_, oh1, oh2 = w[:, :, 32:36], w[:, :, 36:40], w[:, :, 40:44], w[:, :, 44:48]
            m1, m2, s1, gt = w[:, :, 48:49], w[:, :, 49:50], w[:, :, 50:51], w[:, :, 51:52]
            comb = sb("comb", [P, 2, N_EXP], st)
            prod = sb("prod", [P, 2, N_EXP], st)
            spread = lambda a, n: bass.AP(tensor=a.tensor, offset=a.offset, ap=[list(a.ap[0]), list(a.ap[1]), [0, n]])
            with nc.Block(no_gpsimd_drain=True) as block:
                @block.tensor
                def _(pe):
                    for t in range(2):
                        for k in range(KC):
                            mm = pe.matmul(PS[:, 0, t * 20:(t + 1) * 20], xm[:, k, t * P:(t + 1) * P], wr[:, k, :],
                                           start=(k == 0), stop=(k == KC - 1))
                    mm.then_inc(sem("logits"), 1)
                    pe.wait_ge(sem("comb"), 1)
                    for e in range(N_EXP):
                        if e >= 8 and e % 2 == 0:
                            pe.wait_ge(sem("combB"), (e - 8) // 2 + 1)
                        for t in range(2):
                            mm = pe.matmul(PS[:, 4 + e // 2 % 4, (e % 2) * T + t * P:(e % 2) * T + (t + 1) * P],
                                           comb[:, t, e:e + 1].to_broadcast([P, P]), ident, start=True, stop=True)
                        if e % 2:
                            mm.then_inc(sem("combB_done"), 1)

                @block.scalar
                def _(act):
                    act.wait_ge(sem("less_max"), 1)
                    act.activation(pre, eq, ACT.Exp).then_inc(sem("group_exp"), 1)
                    act.wait_ge(sem("less_max2"), 1)
                    act.activation(pe_, el, ACT.Exp).then_inc(sem("expert_exp"), 1)
                    for n in range(N_EXP // 2):
                        act.wait_ge(sem("combB_done"), n + 1)
                        act.copy(combB[:, 2 * n:2 * n + 2, :], PS[:, 4 + n % 4, :].rearrange("p (e t) -> p e t", e=2)
                                 ).then_inc(sem("combB"), 1)

                @block.vector
                def _(dve):
                    link = Chain(dve, sem("dve"))

                    def first_of(dst, hit, at):
                        link(dve.tensor_copy(at, hit))
                        link(dve.tensor_tensor(at[:, :, 1:4], at[:, :, 1:4], hit[:, :, 0:3], ALU.add))
                        link(dve.tensor_tensor(at[:, :, 2:4], at[:, :, 2:4], hit[:, :, 0:2], ALU.add))
                        link(dve.tensor_tensor(at[:, :, 3:4], at[:, :, 3:4], hit[:, :, 0:1], ALU.add))
                        link(dve.tensor_scalar(at, at, 1.0, None, ALU.is_equal))
                        link(dve.tensor_tensor(dst, at, hit, ALU.mult))

                    dve.wait_ge(sem("logits"), 1)
                    link(dve.tensor_tensor(lg, PS[:, 0, 0:40].rearrange("p (t c) -> p t c", t=2), rep(pr("b_route"), 2), ALU.add))
                    link(dve.tensor_reduce(m1, lg[:, :, 0:4], AX_X, ALU.max))
                    dve.tensor_tensor(eq, lg[:, :, 0:4], spread(m1, 4), ALU.subtract).then_inc(sem("less_max"), 1)
                    dve.wait_ge(sem("group_exp"), 1)
                    link(dve.tensor_reduce(gt, pre, AX_X, ALU.add))
                    link(dve.reciprocal(gt, gt))
                    link(dve.tensor_tensor(pre, pre, spread(gt, 4), ALU.mult))
                    link(dve.tensor_reduce(gt, pre, AX_X, ALU.max))
                    link(dve.tensor_tensor(eq, pre, spread(gt, 4), ALU.is_equal))
                    first_of(oh, eq, pre)
                    for g in range(4):
                        link(dve.tensor_tensor(prod[:, :, 4 * g:4 * g + 4], lg[:, :, 4 + 4 * g:8 + 4 * g], spread(oh[:, :, g:g + 1], 4), ALU.mult))
                    link(dve.tensor_tensor(prod[:, :, 0:8], prod[:, :, 0:8], prod[:, :, 8:16], ALU.add))
                    link(dve.tensor_tensor(el, prod[:, :, 0:4], prod[:, :, 4:8], ALU.add))
                    link(dve.tensor_reduce(m1, el, AX_X, ALU.max))
                    dve.tensor_tensor(el, el, spread(m1, 4), ALU.subtract).then_inc(sem("less_max2"), 1)
                    dve.wait_ge(sem("expert_exp"), 1)
                    link(dve.tensor_reduce(s1, pe_, AX_X, ALU.add))
                    link(dve.reciprocal(s1, s1))
                    link(dve.tensor_tensor(pe_, pe_, spread(s1, 4), ALU.mult))
                    link(dve.tensor_reduce(m1, pe_, AX_X, ALU.max))
                    link(dve.tensor_tensor(eq, pe_, spread(m1, 4), ALU.is_equal))
                    first_of(oh1, eq, pre)
                    link(dve.scalar_tensor_tensor(pe_, oh1, -2.0, pe_, ALU.mult, ALU.add))
                    link(dve.tensor_reduce(m2, pe_, AX_X, ALU.max))
                    link(dve.tensor_tensor(eq, pe_, spread(m2, 4), ALU.is_equal))
                    first_of(oh2, eq, pre)
                    link(dve.tensor_tensor(s1, m1, m2, ALU.add))
                    link(dve.reciprocal(s1, s1))
                    link(dve.tensor_tensor(oh1, oh1, spread(m1, 4), ALU.mult))
                    link(dve.tensor_tensor(oh2, oh2, spread(m2, 4), ALU.mult))
                    link(dve.tensor_tensor(oh1, oh1, oh2, ALU.add))
                    link(dve.tensor_tensor(oh1, oh1, spread(s1, 4), ALU.mult))
                    link(dve.tensor_tensor(oh1, oh1, spread(gt, 4), ALU.mult))
                    for g in range(4):
                        i = dve.tensor_tensor(comb[:, :, 4 * g:4 * g + 4], oh1, spread(oh[:, :, g:g + 1], 4), ALU.mult)
                    i.then_inc(sem("comb"), 1)
            stages.end()
            swiglu("moe", 2 * N_EXP, combB, 0)

    def mixer_two():
        with ExitStack() as st:
            yb = sb("yb", [P, 16, T], st)
            state_space(yb)
            att = sb("att", [P, KC, T], st)
            attention(att)
            sem = stages.begin()
            b0, n = B_AT["hyout"]
            with nc.Block(no_gpsimd_drain=True) as block:
                @block.sync
                def _(sp):
                    refill_b(sp, b0, n)

                @block.tensor
                def _(pe):
                    for u in range(n):
                        b_wait(pe, b0 + u)
                        src = [yb[:, 2 * u + kf, :] if u < 8 else att[:, 2 * (u - 8) + kf, :] for kf in range(2)]
                        down_pe(pe, (b0 + u) % NB, src, u == 0, u == n - 1)

                @block.vector
                def _(dve):
                    dve.wait_ge(b_used, b0 + n)
                    for b in range(KC):
                        dve.scalar_tensor_tensor(h[:, b, :], PS[:, 4 + b // 2, (b % 2) * T:(b % 2 + 1) * T], mods3[:, 1, 16 + b:17 + b],
                                                 h[:, b, :], ALU.mult, ALU.add).then_inc(sem("h"), 1)
            stages.end()

    def state_space(yb):
        with ExitStack() as st:
            zx = sb("zx", [P, 40, T], st)
            dts = sb("dts", [SSM_H, 7, T], st)
            sem = stages.begin()
            a0, n = A_AT["hyin"]
            w_dt = pr("w_dt").rearrange("p (k c) -> p k c", k=KC)
            cst = ExitStack()
            ringC, acc = sb("ringC2", [P, NC, KC, 256], cst), sb("acc2", [P, NC, 256], cst)
            with nc.Block(no_gpsimd_drain=True) as block:
                @block.gpsimd
                def _(pool):
                    c_loads(pool, sem, ringC, "hyin")

                @block.sync
                def _(sp):
                    refill_a(sp, a0, n)

                @block.tensor
                def _(pe):
                    for k in range(KC):
                        mm = pe.matmul(PS[0:SSM_H, 4, 0:T], w_dt[:, k, :], xm[:, k, :], start=(k == 0), stop=(k == KC - 1))
                    mm.then_inc(sem("dt_done"), 1)
                    proj_pe(pe, sem, a0, n, c_units=C_UNITS["hyin"], acc=acc)

                @block.scalar
                def _(act):
                    proj_evac(act, 0, act.copy, sem, a0, n, zx)

                @block.vector
                def _(dve):
                    dve.wait_ge(sem("dt_done"), 1)
                    dve.tensor_scalar(dts[:, 0, :], PS[0:SSM_H, 4, 0:T], pr("dt_bias2")[0:SSM_H, :], None, ALU.add).then_inc(sem("dt"), 1)
                    proj_evac(dve, 1, dve.tensor_copy, sem, a0, n, zx, (ringC, acc, lambda m, i: cs[:, 1, :], C_UNITS["hyin"], 8))
                    mods_out(dve, sem, sem("c_summed"), 16, 5, 80, 112, [(1, 1, pr("norm_ffn2", 0, 8)), (2, 0, pr("norm_mix2", 8, 16))])
            cst.close()
            stages.end()

            bc = sb("bc", [P, 8, T], st)
            sem = stages.begin()
            xdt = zx[:, 16:32, :].rearrange("p a b -> p (a b)").rearrange("p (t c) -> p t c", t=2)
            tok = sb("tok", [P, 3, 2, SSM_H], st)
            cbm = sb("cbm", [P, 4, 384], st)
            na = sb("na", [SSM_H, 1], st)
            conv_to = lambda b: yb[:, b, :] if b < 16 else bc[:, b - 16, :]
            with nc.Block(no_gpsimd_drain=True) as block:
                @block.vector
                def _(dve):
                    link = Chain(dve, sem("dve"))
                    y, e, u, um, m0, dt, dA = [dts[:, i, :] for i in range(7)]
                    link(dve.tensor_scalar(e, y, -1.0, None, ALU.mult))
                    link(dve.tensor_tensor(e, y, e, ALU.min))
                    dve.tensor_scalar(m0, y, 0.0, None, ALU.max).then_inc(sem("minus_abs"), 1)
                    dve.wait_ge(sem("exp_minus_abs"), 1)
                    link(dve.tensor_scalar(u, e, 1.0, None, ALU.add))
                    link(dve.tensor_scalar(um, u, -1.0, None, ALU.add))
                    link(dve.tensor_scalar(y, um, 0.0, None, ALU.is_equal))
                    dve.tensor_tensor(um, um, y, ALU.add).then_inc(sem("u_minus_1"), 1)
                    dve.wait_ge(sem("ln_u"), 1)
                    link(dve.tensor_tensor(u, u, y, ALU.add))
                    link(dve.reciprocal(um, um))
                    link(dve.tensor_tensor(u, u, um, ALU.mult))
                    link(dve.tensor_tensor(u, u, e, ALU.mult))
                    link(dve.tensor_tensor(dt, u, m0, ALU.add))
                    link(dve.tensor_scalar(na[:, :], na[:, :], -1.0, None, ALU.mult))
                    dve.tensor_scalar(dA, dt, na[:, 0:1], None, ALU.mult).then_inc(sem("dA"), 1)
                    cw = pr("hconv").rearrange("p (b i) -> p b i", b=24)
                    for tap_ in range(4):
                        for b in range(24):
                            x, o = zx[:, 16 + b, :], conv_to(b)
                            if tap_ == 0:
                                i = dve.tensor_scalar(o, x, cw[:, b, 3:4], pr("hconv_b", b, b + 1), ALU.mult, ALU.add)
                            else:
                                dve.wait_ge(sem("conv"), 24 * (tap_ - 1) + b + 1)
                                i = dve.scalar_tensor_tensor(o[:, tap_:T], x[:, 0:T - tap_], cw[:, b, 3 - tap_:4 - tap_],
                                                             o[:, tap_:T], ALU.mult, ALU.add)
                            i.then_inc(sem("conv"), 1)
                    dve.wait_ge(sem("turned"), 1)
                    dve.tensor_copy(tok[:, 0:2, :, :], PS[:, 0, 0:128].rearrange("p (a t c) -> p a t c", a=2, t=2)).then_inc(sem("tok"), 1)
                    dve.wait_ge(sem("sums_done"), 1)
                    dve.tensor_copy(tok[:, 2, :, :], PS[:, 1, 0:64].rearrange("p (t c) -> p t c", t=2)).then_inc(sem("acs"), 1)
                    dve.tensor_copy(dA, PS[0:SSM_H, 1, 128:384]).then_inc(sem("acs"), 1)
                    dve.wait_ge(sem("cb_done"), 1)
                    dve.tensor_tensor(cbm[:, :, 0:T], PS[:, 4:8, 0:T], rep(upto[:, 0, :], 4), ALU.mult).then_inc(sem("cbm"), 1)
                    dve.tensor_tensor(cbm[:, :, T:384], PS[:, 4:8, T:384], rep(upto[:, 0, 0:P], 4), ALU.mult).then_inc(sem("cbm"), 1)
                    for n8 in range(8):
                        t, c4 = n8 // 4, n8 % 4
                        dve.wait_ge(sem("x_turned"), n8 + 1)
                        dve.tensor_tensor(xdt[:, t, c4 * 512:(c4 + 1) * 512].rearrange("p (h d) -> p h d", h=8),
                                          PS[:, n8 % 4, :].rearrange("p (h d) -> p h d", h=8),
                                          wide(tok[:, 0, t, 8 * c4:8 * c4 + 8], 64), ALU.mult).then_inc(sem("xdt"), 1)

                @block.scalar
                def _(act):
                    act.activation(na[:, :], pr("a_log2")[0:SSM_H, :], ACT.Exp).then_inc(sem("act"), 1)
                    act.wait_ge(sem("minus_abs"), 1)
                    act.activation(dts[:, 1, :], dts[:, 1, :], ACT.Exp).then_inc(sem("exp_minus_abs"), 1)
                    act.wait_ge(sem("u_minus_1"), 1)
                    act.activation(dts[:, 2, :], dts[:, 2, :], ACT.Ln).then_inc(sem("ln_u"), 1)
                    act.activation(zx[:, 0:16, :], zx[:, 0:16, :], ACT.Silu).then_inc(sem("act"), 1)
                    act.wait_ge(sem("conv"), 96)
                    act.activation(yb[:, :, :], yb[:, :, :], ACT.Silu).then_inc(sem("silu"), 1)
                    act.activation(bc[:, :, :], bc[:, :, :], ACT.Silu).then_inc(sem("silu"), 1)

                @block.tensor
                def _(pe):
                    pe.wait_ge(sem("dA"), 1)
                    for a in range(2):
                        for t in range(2):
                            mm = pe.transpose(PS[:, 0, (2 * a + t) * 32:(2 * a + t + 1) * 32], dts[:, 5 + a, t * P:(t + 1) * P], ident[0:SSM_H, 0:SSM_H])
                    mm.then_inc(sem("turned"), 1)
                    pe.wait_ge(sem("tok"), 1)
                    pe.matmul(PS[:, 1, 0:32], upto[:, 0, 0:P], tok[:, 1, 0, :], start=True, stop=True)
                    pe.matmul(PS[:, 1, 32:64], upto[:, 0, P:T], tok[:, 1, 0, :], start=True, stop=False)
                    pe.matmul(PS[:, 1, 32:64], upto[:, 1, P:T], tok[:, 1, 1, :], start=False, stop=True)
                    pe.matmul(PS[0:SSM_H, 1, 128:384], tok[:, 1, 0, :], upto[:, 0, :], start=True, stop=False)
                    pe.matmul(PS[0:SSM_H, 1, 128:384], tok[:, 1, 1, :], upto[:, 1, :], start=False, stop=True).then_inc(sem("sums_done"), 1)
                    pe.wait_ge(sem("silu"), 2)
                    for g in range(4):
                        pe.matmul(PS[:, 4 + g, 0:T], bc[:, g, 0:P], bc[:, 4 + g, :], start=True, stop=True)
                        mm = pe.matmul(PS[:, 4 + g, T:384], bc[:, g, P:T], bc[:, 4 + g, P:T], start=True, stop=True)
                    mm.then_inc(sem("cb_done"), 1)
                    pe.wait_ge(sem("acs"), 2)
                    for n8 in range(8):
                        t, c4 = n8 // 4, n8 % 4
                        if n8 >= 4:
                            pe.wait_ge(sem("xdt"), n8 - 3)
                        for j in range(4):
                            mm = pe.transpose(PS[:, n8 % 4, j * P:(j + 1) * P], yb[:, 4 * c4 + j, t * P:(t + 1) * P], ident)
                        mm.then_inc(sem("x_turned"), 1)
            stages.end()

            sem = stages.begin()
            mt = sb("mt", [P, 2, 384], st)
            dl = sb("dl", [P, 2, 384], st)
            acsT, acs = dts[:, 6, :], tok[:, 2, :, :]
            with nc.Block(no_gpsimd_drain=True) as block:
                @block.tensor
                def _(pe):
                    def spread_head(hd):
                        if hd >= 2:
                            pe.wait_ge(sem("less"), 2 * (hd - 1))
                        pe.matmul(PS[:, hd % 2, 0:T], ident[0:SSM_H, hd:hd + 1].to_broadcast([SSM_H, P]), acsT,
                                  start=True, stop=True).then_inc(sem("spread"), 1)

                    spread_head(0)
                    for hd in range(SSM_H):
                        if hd + 1 < SSM_H:
                            spread_head(hd + 1)
                        pe.wait_ge(sem("mt"), hd + 1)
                        if hd >= 8:
                            pe.wait_ge(sem("y"), hd // 2 - 3)
                        at = (hd % 2) * 64
                        o = PS[at:at + 64, 4 + hd // 2 % 4, 0:T]
                        pe.matmul(o, xdt[:, 0, hd * 64:(hd + 1) * 64], mt[:, hd % 2, 0:T], start=True, stop=False, skip_group_check=True)
                        pe.matmul(o[:, P:T], xdt[:, 1, hd * 64:(hd + 1) * 64], mt[:, hd % 2, T:384], start=False, stop=True,
                                  skip_group_check=True).then_inc(sem("y_done"), 1)

                @block.scalar
                def _(act):
                    for hd in range(SSM_H):
                        act.wait_ge(sem("less"), 2 * hd + 2)
                        act.activation(dl[:, hd % 2, :], dl[:, hd % 2, :], ACT.Exp).then_inc(sem("decay"), 1)

                @block.vector
                def _(dve):
                    def out_pair(b):
                        dve.wait_ge(sem("y_done"), 2 * b + 2)
                        dve.scalar_tensor_tensor(yb[:, b, :], yb[:, b, :], pr("d_skip", b, b + 1), PS[:, 4 + b % 4, 0:T],
                                                 ALU.mult, ALU.add).then_inc(sem("y"), 1)

                    def less(hd):
                        dve.wait_ge(sem("spread"), hd + 1)
                        if hd >= 2:
                            dve.wait_ge(sem("mt"), hd - 1)
                        dve.tensor_scalar(dl[:, hd % 2, 0:T], PS[:, hd % 2, 0:T], acs[:, 0, hd:hd + 1], 0.0, ALU.subtract, ALU.min
                                          ).then_inc(sem("less"), 1)
                        dve.tensor_scalar(dl[:, hd % 2, T:384], PS[:, hd % 2, P:T], acs[:, 1, hd:hd + 1], 0.0, ALU.subtract, ALU.min
                                          ).then_inc(sem("less"), 1)

                    less(0)
                    for hd in range(SSM_H):
                        if hd + 1 < SSM_H:
                            less(hd + 1)
                        dve.wait_ge(sem("decay"), hd + 1)
                        if hd >= 2:
                            dve.wait_ge(sem("y_done"), hd - 1)
                        dve.tensor_tensor(mt[:, hd % 2, :], dl[:, hd % 2, :], cbm[:, hd // 8, :], ALU.mult).then_inc(sem("mt"), 1)
                        if hd % 2 and hd > 1:
                            out_pair(hd // 2 - 1)
                    out_pair(SSM_H // 2 - 1)
            stages.end()

            sem = stages.begin()
            z = zx[:, 0:16, :]
            with nc.Block(no_gpsimd_drain=True) as block:
                @block.vector
                def _(dve):
                    link = Chain(dve, sem("dve"))
                    for q in range(4):
                        dve.tensor_tensor(yb[:, 4 * q:4 * q + 4, :], yb[:, 4 * q:4 * q + 4, :], z[:, 4 * q:4 * q + 4, :], ALU.mult
                                          ).then_inc(sem("gated"), 1)
                    dve.wait_ge(sem("root"), 1)
                    link(dve.reciprocal(rstd[:, :], rstd[:, :]))
                    for b in range(16):
                        dve.scalar_tensor_tensor(yb[:, b, :], yb[:, b, :], pr("ssm_g", b, b + 1), rstd[:, :], ALU.mult, ALU.mult
                                                 ).then_inc(sem("y"), 1)

                @block.scalar
                def _(act):
                    for q in range(4):
                        act.wait_ge(sem("gated"), q + 1)
                        act.activation(z[:, 4 * q:4 * q + 4, :], yb[:, 4 * q:4 * q + 4, :], ACT.Square).then_inc(sem("squares"), 1)
                    act.wait_ge(sem("square_sums"), 1)
                    act.activation(rstd[:, :], PS[:, 0, 0:T], ACT.Sqrt, bias=eps, scale=1.0 / 2048).then_inc(sem("root"), 1)

                @block.tensor
                def _(pe):
                    for b in range(16):
                        pe.wait_ge(sem("squares"), b // 4 + 1)
                        mm = pe.matmul(PS[:, 0, 0:T], ones, z[:, b, :], start=(b == 0), stop=(b == 15))
                    mm.then_inc(sem("square_sums"), 1)
            stages.end()

    def attention(att):
        with ExitStack() as st:
            qkv = sb("qkv", [P, 40, T], st)
            acon = sb("acon", [48, 2, TWIDE], st)
            sem = stages.begin()
            a0, n = A_AT["hyqkv"]
            at0 = CON["bucket"][0]
            cst = ExitStack()
            ringC, acc = sb("ringC3", [P, NC, KC, 256], cst), sb("acc3", [P, NC, 256], cst)
            with nc.Block(no_gpsimd_drain=True) as block:
                @block.gpsimd
                def _(pool):
                    c_loads(pool, sem, ringC, "hyqkv")

                @block.sync
                def _(sp):
                    sp.dma_start(acon[:, :, :].rearrange("p a b -> p (a b)"), con_dram[0:48, at0:at0 + 2 * TWIDE]).then_inc(sem("acon"), 16)
                    refill_a(sp, a0, n)
                    sp.wait_ge(sem("rows"), 1)
                    sp.dma_start(bias_rows, acon[:, 0, :]).then_inc(sem("rows_out"), 16)
                    sp.wait_ge(sem("rows_out"), 16)

                @block.tensor
                def _(pe):
                    pe.wait_ge(sem("acon"), 16)
                    pe.matmul(PS[0:48, 4, 0:TWIDE], pr("rel")[0:32, :], acon[0:32, 0, :], start=True, stop=True).then_inc(sem("rows_done"), 1)
                    proj_pe(pe, sem, a0, n, dst_token=(16, 17, 18, 19), c_units=C_UNITS["hyqkv"], acc=acc)

                @block.scalar
                def _(act):
                    proj_evac(act, 0, act.copy, sem, a0, n, qkv)

                @block.vector
                def _(dve):
                    dve.wait_ge(sem("rows_done"), 1)
                    dve.tensor_tensor(acon[:, 0, :], PS[0:48, 4, 0:TWIDE], acon[:, 1, :], ALU.add).then_inc(sem("rows"), 1)
                    proj_evac(dve, 1, dve.tensor_copy, sem, a0, n, qkv, (ringC, acc, lambda m, i: cs[:, 1, :], C_UNITS["hyqkv"], 8))
                    mods_out(dve, sem, sem("c_summed"), 16, 5, 112, 144, [(2, 1, pr("norm_ffn2", 8, 16))])
            cst.close()
            stages.end()

            sem = stages.begin()
            NT = 4
            bias = sb("bias", [P, NT, 3, T], st)
            s_ = sb("s_", [P, 2, 3 * T], st)
            pt = xm[:, 0:2, :]
            pT = xm[:, 2:4, :]
            stat = sb("stat", [P, 2, 4], st)
            steps = [(hd, it) for hd in range(ATT_H) for it in range(2)]
            with nc.Block(no_gpsimd_drain=True) as block:
                @block.sync
                def _(sp):
                    for hd in range(ATT_H):
                        if hd >= NT:
                            sp.wait_ge(sem("biased"), 2 * (hd - NT) + 2)
                        src = bass.AP(tensor=bias_rows.tensor, offset=hd * TWIDE,
                                      ap=[[1, P], [ATT_H * TWIDE, 3], [1, T]])
                        sp.dma_start(bias[:, hd % NT, :, :], src).then_inc(sem(f"bias{hd % NT}"), 16)

                @block.tensor
                def _(pe):
                    def scores(n):
                        hd, it = steps[n]
                        W = P * (it + 1)
                        at = (hd % 2) * 64
                        if n >= 2:
                            pe.wait_ge(sem("biased"), n - 1)
                        for g in range(3):
                            mm = pe.matmul(PS[:, 2 * (n % 2) + g // 2, (g % 2) * T:(g % 2) * T + W],
                                           qkv[at:at + 64, 8 * g + hd // 2, it * P:(it + 1) * P],
                                           qkv[at:at + 64, 24 + hd // 2, 0:W], start=True, stop=True)
                        mm.then_inc(sem("scores"), 1)

                    def turn(n):
                        hd, it = steps[n]
                        pe.wait_ge(sem("normed"), n + 1)
                        if n >= 2:
                            pe.wait_ge(sem("pT"), n - 1)
                        for j in range(it + 1):
                            mm = pe.transpose(PS[:, 4 + n % 2, j * P:(j + 1) * P], pt[:, n % 2, j * P:(j + 1) * P], ident)
                        mm.then_inc(sem("turned"), 1)

                    def values(n):
                        hd, it = steps[n]
                        at = (hd % 2) * 64
                        pe.wait_ge(sem("pT"), n + 1)
                        if hd >= 4 and it == 0 and hd % 2 == 0:
                            pe.wait_ge(sem("att"), hd // 2 - 1)
                        for j in range(it + 1):
                            mm = pe.matmul(PS[at:at + 64, 6 + hd // 2 % 2, it * P:(it + 1) * P],
                                           qkv[:, 32 + 2 * (hd // 4) + j, (hd % 4) * 64:(hd % 4 + 1) * 64],
                                           pT[:, n % 2, j * P:(j + 1) * P], start=(j == 0), stop=(j == it))
                        mm.then_inc(sem("values"), 1)

                    scores(0)
                    for n in range(len(steps)):
                        if n + 1 < len(steps):
                            scores(n + 1)
                        turn(n)
                        if n >= 1:
                            values(n - 1)
                    values(len(steps) - 1)

                @block.scalar
                def _(act):
                    def turn_out(n):
                        W = P * (steps[n][1] + 1)
                        act.wait_ge(sem("turned"), n + 1)
                        if n >= 2:
                            act.wait_ge(sem("values"), n - 1)
                        act.copy(pT[:, n % 2, 0:W], PS[:, 4 + n % 2, 0:W]).then_inc(sem("pT"), 1)

                    def pair_out(b):
                        act.wait_ge(sem("values"), 4 * b + 4)
                        act.copy(att[:, b, :], PS[:, 6 + b % 2, 0:T]).then_inc(sem("att"), 1)

                    for n, (hd, it) in enumerate(steps):
                        W3 = 3 * P * (it + 1)
                        act.wait_ge(sem("max"), n + 1)
                        act.activation(s_[:, n % 2, 0:W3], s_[:, n % 2, 0:W3], ACT.Exp, bias=stat[:, n % 2, 0:1],
                                       accum_out=stat[:, n % 2, 1:2]).then_inc(sem("exps"), 1)
                        if n >= 1:
                            turn_out(n - 1)
                        if n >= 6 and n % 4 == 2:
                            pair_out(n // 4 - 1)
                    turn_out(len(steps) - 1)
                    pair_out(ATT_H // 2 - 1)

                @block.vector
                def _(dve):
                    link = Chain(dve, sem("dve"))

                    def biased(n):
                        hd, it = steps[n]
                        W = P * (it + 1)
                        dve.wait_ge(sem("scores"), n + 1)
                        dve.wait_ge(sem(f"bias{hd % NT}"), 16 * (hd // NT + 1))
                        sc = s_[:, n % 2, 0:3 * W].rearrange("p (g c) -> p g c", g=3)
                        b_ = bias[:, hd % NT, :, W - 1:W]
                        keys_forward = bass.AP(tensor=b_.tensor, offset=b_.offset, ap=[list(b_.ap[0]), list(b_.ap[1]), [-1, W]])
                        psum = PS[:, 2 * (n % 2):2 * (n % 2) + 2, :].rearrange("p a (g c) -> p (a g) c", g=2)[:, 0:3, 0:W]
                        dve.scalar_tensor_tensor(sc, psum, 0.125, keys_forward, ALU.mult, ALU.add
                                                 ).then_inc(sem("biased"), 1)
                        dve.wait_ge(sem("biased"), n + 1)
                        dve.tensor_reduce(stat[:, n % 2, 0:1], s_[:, n % 2, 0:3 * W], AX_X, ALU.max, negate=True).then_inc(sem("max"), 1)

                    def normed(n):
                        hd, it = steps[n]
                        W = P * (it + 1)
                        p = s_[:, n % 2, :]
                        dve.wait_ge(sem("exps"), n + 1)
                        if n >= 2:
                            dve.wait_ge(sem("turned"), n - 1)
                        link(dve.reciprocal(stat[:, n % 2, 2:3], stat[:, n % 2, 1:2]))
                        link(dve.tensor_tensor(pt[:, n % 2, 0:W], p[:, 0:W], p[:, W:2 * W], ALU.add))
                        link(dve.tensor_tensor(pt[:, n % 2, 0:W], pt[:, n % 2, 0:W], p[:, 2 * W:3 * W], ALU.add))
                        dve.tensor_scalar(pt[:, n % 2, 0:W], pt[:, n % 2, 0:W], stat[:, n % 2, 2:3], None, ALU.mult
                                          ).then_inc(sem("normed"), 1)

                    biased(0)
                    for n in range(len(steps)):
                        if n + 1 < len(steps):
                            biased(n + 1)
                        normed(n)
            stages.end()

    def conformer():
        with ExitStack() as st:
            ag = sb("ag", [P, 16, T], st)
            cvo = sb("cvo", [P, KC, T], st)
            mean = sb("mean", [P, T], st)
            sem = stages.begin()
            a0, n = A_AT["cv1"]
            with nc.Block(no_gpsimd_drain=True) as block:
                @block.sync
                def _(sp):
                    refill_a(sp, a0, n)

                @block.tensor
                def _(pe):
                    proj_pe(pe, sem, a0, n)

                @block.scalar
                def _(act):
                    proj_evac(act, 0, act.copy, sem, a0, n, ag)

                @block.vector
                def _(dve):
                    proj_evac(dve, 1, dve.tensor_copy, sem, a0, n, ag)
            stages.end()
            sem = stages.begin()
            u, sg = ag[:, 0:8, :], ag[:, 8:16, :]
            TAPS_N = 31
            with nc.Block(no_gpsimd_drain=True) as block:
                @block.vector
                def _(dve):
                    link = Chain(dve, sem("dve"))
                    dw = pr("dw").rearrange("p (b i) -> p b i", b=KC)
                    for b in range(KC):
                        dve.wait_ge(sem("gate"), b + 1)
                        i = dve.scalar_tensor_tensor(u[:, b, :], u[:, b, :], pr("b1", b, b + 1), sg[:, b, :], ALU.add, ALU.mult)
                        i.then_inc(sem("u"), 1)
                    for tp in range(TAPS_N):
                        for b in range(KC):
                            x, o = u[:, b, :], cvo[:, b, :]
                            w = dw[:, b, TAPS_N - 1 - tp:TAPS_N - tp]
                            if tp == 0:
                                dve.wait_ge(sem("u"), b + 1)
                                i = dve.tensor_scalar(o, x, w, pr("dw_b", b, b + 1), ALU.mult, ALU.add)
                            else:
                                dve.wait_ge(sem("conv"), KC * (tp - 1) + b + 1)
                                i = dve.scalar_tensor_tensor(o[:, tp:T], x[:, 0:T - tp], w, o[:, tp:T], ALU.mult, ALU.add)
                            i.then_inc(sem("conv"), 1)
                    dve.wait_ge(sem("sums"), 1)
                    link(dve.tensor_scalar(mean[:, :], PS[:, 0, 0:T], 1.0 / D, None, ALU.mult))
                    dve.tensor_tensor(cvo[:, :, :], cvo[:, :, :], rep(mean[:, :], KC), ALU.subtract).then_inc(sem("centred"), 1)
                    dve.wait_ge(sem("root"), 1)
                    link(dve.reciprocal(rstd[:, :], rstd[:, :]))
                    dve.tensor_tensor(cvo[:, :, :], cvo[:, :, :], rep(rstd[:, :], KC), ALU.mult).then_inc(sem("normed"), 1)

                @block.scalar
                def _(act):
                    for b in range(KC):
                        act.activation(sg[:, b, :], sg[:, b, :], ACT.Sigmoid, bias=pr("b1", 8 + b, 9 + b)).then_inc(sem("gate"), 1)
                    act.wait_ge(sem("centred"), 1)
                    act.activation(sg, cvo[:, :, :], ACT.Square).then_inc(sem("squares"), 1)
                    act.wait_ge(sem("square_sums"), 1)
                    act.activation(rstd[:, :], PS[:, 1, 0:T], ACT.Sqrt, bias=eps, scale=1.0 / D).then_inc(sem("root"), 1)
                    act.wait_ge(sem("normed"), 1)
                    for b in range(KC):
                        act.activation(cvo[:, b, :], cvo[:, b, :], ACT.Silu, bias=pr("ln_b", b, b + 1), scale=pr("ln_g", b, b + 1)
                                       ).then_inc(sem("out"), 1)

                @block.tensor
                def _(pe):
                    for b in range(KC):
                        pe.wait_ge(sem("conv"), KC * (TAPS_N - 1) + b + 1)
                        mm = pe.matmul(PS[:, 0, 0:T], ones, cvo[:, b, :], start=(b == 0), stop=(b == KC - 1))
                    mm.then_inc(sem("sums"), 1)
                    pe.wait_ge(sem("squares"), 1)
                    for b in range(KC):
                        mm = pe.matmul(PS[:, 1, 0:T], ones, sg[:, b, :], start=(b == 0), stop=(b == KC - 1))
                    mm.then_inc(sem("square_sums"), 1)
            stages.end()
            out_proj("cv2", cvo, pr("b2"), 2)

    first_stage()
    norm_stage(0, 0)
    mixer_one()
    norm_stage(1, 0)
    moe()
    norm_h(pr("norm_out"), h)
    norm_stage(0, 1)
    mixer_two()
    norm_stage(1, 1)
    swiglu("ffn0", FF // 256, None, 1)
    norm_stage(0, 2)
    conformer()
    norm_stage(1, 2)
    swiglu("ffn1", FF // 256, None, 2)
    norm_h(pr("final"), xm)
    ctx.close()


def put_a(dst, w):
    n = w.shape[1] // 256
    dst.reshape(n, P, KC, 256)[...] = w.reshape(KC, P, n, 256).transpose(2, 1, 0, 3)


def put_b(dst, w):
    n = w.shape[0] // 256
    dst.reshape(n, P, 2, D)[...] = w.reshape(n, 2, P, D).transpose(0, 2, 1, 3)


def put_paired(dst, a, b):
    for j, w in enumerate((a, b)):
        n = w.shape[1] // 256
        dst[j::2].reshape(n, P, KC, 256)[...] = w.reshape(KC, P, n, 256).transpose(2, 1, 0, 3)


def cols(v):
    return np.asarray(v).reshape(-1, P).T


def everywhere(v):
    return np.broadcast_to(np.asarray(v).reshape(1, -1), (P, np.asarray(v).size))


def layout(i):
    i = {k: np.asarray(v) for k, v in i.items()}
    w_in = i["w_in"][0]
    hy = i["hy_w_in_2"][0]
    eg = i["w_gate"][0].reshape(N_EXP, D, FF_EXP)
    eu = i["w_up"][0].reshape(N_EXP, D, FF_EXP)
    ed = i["w_down"][0].reshape(N_EXP, FF_EXP, D)
    wa = np.empty((A_ALL, P, UNIT), w_in.dtype)
    wb = np.empty((B_ALL, P, UNIT), w_in.dtype)
    in_a = lambda name, a=0, b=None: wa[A_AT[name][0] + a:A_AT[name][0] + (A_AT[name][1] if b is None else b)]
    in_b = lambda name, a=0, b=None: wb[B_AT[name][0] + a:B_AT[name][0] + (B_AT[name][1] if b is None else b)]
    put_a(in_a("mod"), i["mod_w"][0][:, :2048])
    wc = np.empty((C_ALL, P, UNIT), w_in.dtype)
    put_a(wc[0:16], i["mod_w"][0][:, 2048:])
    put_a(wc[16:40], i["ada_w_2"][0])
    put_a(wc[40:64], i["ada_w_2"][1])
    put_a(in_a("win", 0, 24), w_in[:, :6144])
    put_a(in_a("win", 24), w_in[:, 6152:])
    put_a(in_a("wout"), i["w_out"][0])
    for e in range(N_EXP):
        put_paired(in_a("moe", 4 * e, 4 * e + 4), eg[e], eu[e])
        put_b(in_b("moe", 2 * e, 2 * e + 2), ed[e])
    put_a(in_a("hyin"), hy[:, :5120])
    put_a(in_a("hyqkv"), hy[:, 5152:])
    put_b(in_b("hyout"), i["hy_w_out_2"][0])
    put_a(in_a("cv1"), i["cv_w_pw1_2"][0])
    put_a(in_a("cv2"), i["cv_w_pw2_2"][0])
    for l in range(2):
        put_paired(in_a(f"ffn{l}"), i["ffn_w_gate_2"][l], i["ffn_w_up_2"][l])
        put_b(in_b(f"ffn{l}"), i["ffn_w_down_2"][l])
    f = wa.dtype
    par = np.zeros((P, N_PAR), f)

    def put(name, v):
        at, w = PAR[name]
        v = np.asarray(v)
        par[:v.shape[0], at:at + w] = v.reshape(v.shape[0], w)

    put("c", cols(i["c"][0]))
    put("c2", cols(i["c_2"][0]))
    put("mod_b", cols(i["mod_b"][0]))
    put("ada_b", cols(i["ada_b_2"]))
    put("norm_mix", cols(i["norm_mix_w"][0]))
    put("norm_ffn", cols(i["norm_ffn_w"][0]))
    put("norm_out", cols(i["norm_out_w"]))
    put("norm_mix2", cols(i["norm_mix_g_2"]))
    put("norm_ffn2", cols(i["norm_ffn_g_2"]))
    put("final", cols(i["final_norm_g_2"]))
    put("gconv", i["gdn_conv_w"][0].reshape(4, 16, P).transpose(2, 1, 0))
    put("a_log", everywhere(i["gdn_a_log"][0]))
    put("dt_bias", everywhere(i["gdn_dt_bias"][0]))
    put("gdn_w", cols(i["gdn_norm_w"][0]))
    put("b_route", everywhere(np.concatenate([i["b_group"][0], i["b_router"][0].reshape(-1)])))
    put("w_route", np.concatenate([i["w_group"][0], i["w_router"][0]], 1).reshape(KC, P, 20).transpose(1, 0, 2))
    put("w_ab", w_in[:, 6144:6152].reshape(KC, P, 8).transpose(1, 0, 2))
    put("hconv", i["hy_conv_w_2"][0].reshape(4, 24, P).transpose(2, 1, 0))
    put("hconv_b", cols(i["hy_conv_b_2"][0]))
    put("w_dt", hy[:, 5120:5152].reshape(KC, P, SSM_H).transpose(1, 0, 2))
    put("dt_bias2", i["hy_dt_bias_2"][0][:, None])
    put("a_log2", i["hy_a_log_2"][0][:, None])
    put("d_skip", cols(np.repeat(i["hy_d_skip_2"][0], 64)))
    put("ssm_g", cols(i["hy_ssm_norm_g_2"][0]))
    put("rel", i["rel_table_2"])
    put("b1", cols(i["cv_b_pw1_2"][0]))
    put("dw", i["cv_w_dw_2"][0].reshape(31, 8, P).transpose(2, 1, 0))
    put("dw_b", cols(i["cv_b_dw_2"][0]))
    put("ln_g", cols(i["cv_ln_g_2"][0]))
    put("ln_b", cols(i["cv_ln_b_2"][0]))
    put("b2", cols(i["cv_b_pw2_2"][0]))
    x = np.ascontiguousarray(i["x"][0].T.reshape(KC, P, T).transpose(1, 0, 2))
    return {"wa": wa, "wb": wb, "wc": wc, "par": par, "con": constants(), "xT": x}


def kernel(**inputs):
    import concourse.bacc as _bacc
    from concourse.bass_utils import run_bass_kernel_spmd as _run

    nc = _bacc.Bacc("TRN2", target_bir_lowering=False, num_devices=1)
    arrays = layout(inputs)
    ins = [nc.dram_tensor(n, a.shape, mybir.dt.from_np(a.dtype), kind="ExternalInput").ap() for n, a in arrays.items()]
    out = nc.dram_tensor("out", (P, KC, T), F32, kind="ExternalOutput").ap()
    program(nc, ins, out)
    r = _run(nc, [arrays], core_ids=[0])
    y = r.results[0]["out"]
    return y.transpose(1, 0, 2).reshape(D, T).T.reshape(1, T, D)
```

```python
from contextlib import ExitStack

import numpy as np
import concourse.bass as bass
from concourse import mybir

F32 = mybir.dt.float32
F32R = mybir.dt.float32r
ACT = mybir.ActivationFunctionType
ALU = mybir.AluOpType
AX_X = mybir.AxisListType.X

P = 128
D = 1024
T = 256
KC = D // P
NA, NB = 8, 2
UNIT = 2048
HEADS = 4
EPS = 1e-6
N_EXP = 16
FF_EXP = 512
FF = 2816
SSM_H = 32
ATT_H = 16
BIG = -1e30
TWIDE = 384

A_UNITS = [("mod", 8), ("win", 32), ("wout", 4), ("moe", 4 * N_EXP), ("hyin", 20), ("hyqkv", 20),
           ("ffn0", 2 * FF // 256), ("cv1", 8), ("cv2", 4), ("ffn1", 2 * FF // 256)]
B_UNITS = [("moe", 2 * N_EXP), ("hyout", 12), ("ffn0", FF // 256), ("ffn1", FF // 256)]


C_UNITS = {"win": (0, 16), "moe": (16, 32), "hyin": (48, 8), "hyqkv": (56, 8)}
C_ALL = 64


SPLIT_FROM = 8


def starts(units):
    at, n = {}, 0
    for name, k in units:
        at[name] = (n, k)
        n += k
    return at, n


A_AT, A_ALL = starts(A_UNITS)
B_AT, B_ALL = starts(B_UNITS)

PAR_WIDTHS = [("c", 8), ("c2", 8), ("mod_b", 48), ("ada_b", 96), ("norm_mix", 8), ("norm_ffn", 8), ("norm_out", 8),
              ("norm_mix2", 16), ("norm_ffn2", 16), ("final", 8), ("gconv", 64), ("a_log", 4),
              ("dt_bias", 4), ("gdn_w", 2), ("b_route", 20), ("w_route", 160), ("w_ab", 64),
              ("hconv", 96), ("hconv_b", 24), ("w_dt", 256), ("dt_bias2", 1), ("a_log2", 1), ("d_skip", 16),
              ("ssm_g", 16), ("rel", 48), ("b1", 16), ("dw", 248), ("dw_b", 8), ("ln_g", 8), ("ln_b", 8), ("b2", 8)]
PAR = {}
N_PAR = 0
for _name, _w in PAR_WIDTHS:
    PAR[_name] = (N_PAR, _w)
    N_PAR += _w

CON_WIDTHS = [("ident", 128), ("ones", 128), ("upto", 512), ("eps", 1),
              ("cos", 256), ("sin", 256), ("turn", 128), ("ret", 4 * 384),
              ("strict", 128), ("levels", 7 * 128),
              ("bucket", TWIDE), ("band", TWIDE)]
CON = {}
N_CON = 0
for _name, _w in CON_WIDTHS:
    CON[_name] = (N_CON, _w)
    N_CON += _w
N_KEPT = CON["cos"][0]


def constants():
    c = np.zeros((P, N_CON), np.float32)

    def put(name, a):
        at, w = CON[name]
        a = np.asarray(a, np.float32)
        c[:a.shape[0], at:at + w] = a.reshape(a.shape[0], w)

    p = np.arange(P)
    i = np.arange(T)
    put("ident", np.eye(P))
    put("ones", np.ones((P, P)))
    put("upto", np.stack([p[:, None] + P * t <= i[None, :] for t in range(2)], 1))
    put("eps", np.full((P, 1), EPS))
    half = 64
    inv = (1.0 / (np.float32(10000.0) ** (np.arange(half, dtype=np.float32) / np.float32(half)))).astype(np.float32)
    ang = (np.arange(T, dtype=np.float32)[:, None] * inv[None, :]).astype(np.float32)
    put("cos", np.tile(np.cos(ang).T, (2, 1)))
    put("sin", np.tile(np.sin(ang).T, (2, 1)))
    turn = np.zeros((P, P))
    for m in range(half):
        turn[m + half, m] = -1.0
        turn[m, m + half] = 1.0
    put("turn", turn)
    ret = np.zeros((P, HEADS, 384))
    for h in range(HEADS):
        lg = np.log(1.0 - 2.0 ** (-5.0 - h))
        rel = i[None, :] - p[:, None]
        dec = np.where(rel >= 0, np.exp(np.maximum(rel, 0) * lg), 0.0) * 128 ** -0.5
        ret[:, h, :T] = dec
        ret[:, h, T:] = dec[:, :P]
    put("ret", ret)
    put("strict", p[:, None] < p[None, :])
    lv = np.zeros((P, 7, P))
    for n in range(7):
        s = 1 << n
        lv[:, n] = (p[:, None] // (2 * s) == p[None, :] // (2 * s)) & ((p[:, None] // s) % 2 == 0) & ((p[None, :] // s) % 2 == 1)
    put("levels", lv)
    dist = np.arange(TWIDE) - 127
    n = np.maximum(dist, 1).astype(np.float32)
    large = 16 + np.log(n / np.float32(16)) / np.float32(np.log(2048 / 16)) * 16
    large = np.minimum(large.astype(np.int32), 31)
    bk = np.where(dist < 16, np.maximum(dist, 0), large)
    put("bucket", (bk[None, :] == np.arange(32)[:, None]) & (dist >= 0)[None, :])
    band = np.zeros((48, TWIDE))
    for g, dil in enumerate((1, 4, 16)):
        ok = (dist >= 0) & (dist % dil == 0) & (dist // dil <= 128)
        band[g * 16:(g + 1) * 16] = np.where(ok, 0.0, BIG)[None, :]
    put("band", band)
    return c


def rep(ap, n):
    return bass.AP(tensor=ap.tensor, offset=ap.offset, ap=[list(ap.ap[0]), [0, n]] + [list(x) for x in ap.ap[1:]])


def wide(ap, m):
    return bass.AP(tensor=ap.tensor, offset=ap.offset, ap=[list(x) for x in ap.ap] + [[0, m]])


class Chain:

    def __init__(self, engine, semaphore):
        self.engine, self.semaphore, self.count = engine, semaphore, 0

    def __call__(self, instruction):
        self.count += 1
        instruction.then_inc(self.semaphore, 1)
        self.engine.wait_ge(self.semaphore, self.count)


class Stages:

    SIZE = 66

    def __init__(self, nc):
        self.nc, self.k = nc, 0
        self.pools = [[nc.alloc_semaphore(f"stage{q}_{i}") for i in range(self.SIZE)] for q in range(2)]

    def begin(self):
        taken = {}
        pool = self.pools[self.k % 2]

        def sem(name):
            if name not in taken:
                taken[name] = pool[len(taken)]
            return taken[name]

        return sem

    def end(self):
        pool = self.pools[self.k % 2]
        self.nc.gpsimd.sem_clear(range(pool[0].num, pool[-1].num + 1))
        self.k += 1


def program(nc, ins, out):
    wa, wb, wc, par_dram, con_dram, x_dram = ins
    bias_rows = nc.dram_tensor("bias_rows", (48, TWIDE), F32, kind="Internal").ap()
    ctx = ExitStack()

    def sb(name, shape, on=ctx):
        return on.enter_context(nc.sbuf_tensor(name + "_sb", shape, F32))

    def sb2(name, shape, on=ctx):
        with nc.sbuf_tensor(name + "_sb", shape, F32) as plain:
            pass
        return plain, on.enter_context(nc.sbuf_tensor(name + "_r_sb", shape, F32R))

    ringA, lowA = sb2("ringA", [P, NA, KC, 256])
    ringB, lowB = sb2("ringB", [P, NB, 2, D])
    h = sb("h", [P, KC, T])
    xm, xl = sb2("xm", [P, KC, T])
    par = sb("par", [P, N_PAR])
    con = sb("con", [P, N_KEPT])
    mods3 = sb("mods", [P, 3, 48])
    normw3 = sb("normw", [P, 3, 2, KC])
    cs = sb("cs", [P, 2, KC])
    rstd = sb("rstd", [P, T])
    spare_xh, xh = sb2("xh", [P, KC, T])
    spare_highA, highA = sb2("highA", [P, 2, KC, 256])
    PS = ctx.enter_context(nc.psum_tensor("PS", [P, 8, 512], F32))

    a_full = [nc.alloc_semaphore(f"a_full{i}") for i in range(NA)]
    b_full = [nc.alloc_semaphore(f"b_full{i}") for i in range(NB)]
    c_full = nc.alloc_semaphore("c_full")
    a_high = nc.alloc_semaphore("a_high")
    a_low = nc.alloc_semaphore("a_low")
    b_high = nc.alloc_semaphore("b_high")
    b_low = nc.alloc_semaphore("b_low")
    a_used = nc.alloc_semaphore("a_used")
    b_used = nc.alloc_semaphore("b_used")
    stages = Stages(nc)

    def pr(name, a=0, b=None):
        at, w = PAR[name]
        return par[:, at + a:at + (w if b is None else b)]

    def cn(name):
        at, w = CON[name]
        return con[:, at:at + w]

    ident, ones, eps = cn("ident"), cn("ones"), cn("eps")
    upto = cn("upto").rearrange("p (t i) -> p t i", t=2)

    def load_a(sp, slot, n):
        sp.dma_start(ringA[:, slot].rearrange("p k c -> p (k c)"), wa[n]).then_inc(a_full[slot], 16)

    def load_b(sp, slot, n):
        sp.dma_start(ringB[:, slot].rearrange("p k c -> p (k c)"), wb[n]).then_inc(b_full[slot], 16)

    def refill_a(sp, first, n):
        n = min(n, A_ALL - NA - first)
        turns = n // NA
        if turns > 1:
            with sp.Fori(0, turns) as i:
                for j in range(NA):
                    sp.wait_ge(a_used, i * NA + (first + j + 1))
                    sp.dma_start(ringA[:, (first + j) % NA].rearrange("p k c -> p (k c)"),
                                 wa[bass.ds(i * NA + (first + j + NA), 1)].rearrange("a p c -> p (a c)")
                                 ).then_inc(a_full[(first + j) % NA], 16)
        else:
            turns = 0
        for m in range(first + turns * NA, first + n):
            sp.wait_ge(a_used, m + 1)
            load_a(sp, m % NA, m + NA)

    def refill_b(sp, first, n):
        for m in range(first, first + min(n, B_ALL - NB - first)):
            sp.wait_ge(b_used, m + 1)
            load_b(sp, m % NB, m + NB)

    def refill_ab(sp, a0, b0, steps):
        def step(s):
            for j in (0, 1):
                m = a0 + 2 * s + j
                if m + NA < A_ALL:
                    sp.wait_ge(a_used, m + 1)
                    load_a(sp, m % NA, m + NA)
            m = b0 + s - 1
            if s > 0 and m + NB < B_ALL:
                sp.wait_ge(b_used, m + 1)
                load_b(sp, m % NB, m + NB)

        last = min(steps, (A_ALL - NA - a0) // 2, B_ALL - NB - b0)
        turns = (last - 4) // 4
        for s in range(4):
            step(s)
        if turns > 1:
            with sp.Fori(1, turns + 1) as i:
                for s in range(4):
                    loop_step(sp, a0, b0, s, i)
            done = 4 + 4 * turns
        else:
            done = 4
        for s in range(done, steps):
            step(s)
        m = b0 + steps - 1
        if m + NB < B_ALL:
            sp.wait_ge(b_used, m + 1)
            load_b(sp, m % NB, m + NB)

    def loop_step(sp, a0, b0, s, i):
        for j in (0, 1):
            m = a0 + 2 * s + j
            sp.wait_ge(a_used, i * 8 + (m + 1))
            sp.dma_start(ringA[:, m % NA].rearrange("p k c -> p (k c)"),
                         wa[bass.ds(i * 8 + (m + NA), 1)].rearrange("a p c -> p (a c)")).then_inc(a_full[m % NA], 16)
        m = b0 + s - 1
        sp.wait_ge(b_used, i * 4 + (m + 1))
        sp.dma_start(ringB[:, m % NB].rearrange("p k c -> p (k c)"),
                     wb[bass.ds(i * 4 + (m + NB), 1)].rearrange("a p c -> p (a c)")).then_inc(b_full[m % NB], 16)

    def a_wait(pe, n, i=None):
        pe.wait_ge(a_full[n % NA], 16 * (n // NA + 1) if i is None else i * 16 + 16 * (n // NA + 1))

    plus = lambda v, i, per: v if i is None else i * per + v

    def high_a(act, n, i=None):
        act.wait_ge(a_full[n % NA], plus(16 * (n // NA + 1), i, 16))
        act.wait_ge(a_used, plus(n - 1, i, NA))
        act.copy(highA[:, n % 2, :, :], ringA[:, n % NA, :, :]).then_inc(a_high, 1)

    def low_a(dve, n, i=None):
        dve.wait_ge(a_high, plus(n + 1 - SPLIT_FROM, i, NA))
        dve.tensor_tensor(lowA[:, n % NA, :, :], ringA[:, n % NA, :, :], highA[:, n % 2, :, :].bitcast(F32), ALU.subtract
                          ).then_inc(a_low, 1)

    def split_a_wait(pe, n, i=None):
        pe.wait_ge(a_low, plus(n + 1 - SPLIT_FROM, i, NA))

    def high_b(act, highB, n, i=None):
        act.wait_ge(b_full[n % NB], plus(16 * (n // NB + 1), i, 64 // NB))
        if n >= 2:
            act.wait_ge(b_used, plus(n - 1, i, 4))
        act.copy(highB[:, n % 2, :, :], ringB[:, n % NB, :, :]).then_inc(b_high, 1)

    def low_b(dve, highB, n, i=None):
        dve.wait_ge(b_high, plus(n + 1, i, 4))
        dve.tensor_tensor(lowB[:, n % NB, :, :], ringB[:, n % NB, :, :], highB[:, n % 2, :, :].bitcast(F32), ALU.subtract
                          ).then_inc(b_low, 1)

    def high_x(act, sem, src, high, parts):
        n = src.shape[1] // parts
        for q in range(parts):
            act.copy(high[:, q * n:(q + 1) * n, :], src[:, q * n:(q + 1) * n, :]).then_inc(sem("x_high"), 1)

    def low_x(dve, sem, src, high, low, parts):
        n = src.shape[1] // parts
        for q in range(parts):
            dve.wait_ge(sem("x_high"), q + 1)
            dve.tensor_tensor(low[:, q * n:(q + 1) * n, :], src[:, q * n:(q + 1) * n, :], high[:, q * n:(q + 1) * n, :].bitcast(F32),
                              ALU.subtract).then_inc(sem("x_low"), 1)

    def mm3(pe, psum, high, low, moving_high, moving_low, start, stop, **kw):
        pe.matmul(psum, high, moving_high, start=start, stop=False, **kw)
        pe.matmul(psum, high, moving_low, start=False, stop=False, **kw)
        return pe.matmul(psum, low, moving_high, start=False, stop=stop, **kw)

    def rms_pe(pe, sem, squares, blocks, psum):
        pe.wait_ge(sem("squares"), 1)
        for k in range(blocks):
            mm = pe.matmul(psum, ones, squares[:, k, :], start=(k == 0), stop=(k == blocks - 1))
        mm.then_inc(sem("square_sums"), 1)

    def proj_pe(pe, sem, first, units, dst_token=(), low_src=xl, c_units=None, acc=None):
        def unit(u, j, token, i=None):
            if i is not None or u >= 4:
                done = (sem("evac_act"), sem("evac_dve"))[j % 2]
                n = (j - 4) // 2 + 1
                pe.wait_ge(done, plus(n, i, NA // 2))
            split_a_wait(pe, first + j, i)
            high, low = highA[:, (first + j) % 2], lowA[:, (first + j) % NA]
            bank = PS[:, j % 4, :]
            for b in range(2):
                at = slice(b * P, (b + 1) * P)
                for k in range(KC):
                    if token:
                        mm = mm3(pe, bank[:, b * 256:(b + 1) * 256], xh[:, k, at], low_src[:, k, at], high[:, k, :], low[:, k, :],
                                 start=(k == 0), stop=(k == KC - 1))
                    else:
                        mm = mm3(pe, bank[:, b * 256:(b + 1) * 256], high[:, k, at], low[:, k, at], xh[:, k, :], low_src[:, k, :],
                                 start=(k == 0), stop=(k == KC - 1))
            mm.then_inc(a_used, 1)
            if c_units and j % 2 and (i is not None or 2 <= u <= 2 * c_units[1] + 1):
                c_sum(pe, sem, acc, 16 + 2 * c_units[0] + (j - 3), (j - 3) // 2, i, NA // 2)

        turns = (units - NA) // NA
        for u in range(min(NA, units)):
            unit(u, u, u in dst_token)
        if turns > 0:
            with pe.Fori(1, turns + 1) as i:
                for j in range(NA):
                    unit(None, j, False, i)
        for u in range(NA + max(turns, 0) * NA, units):
            unit(u, u, u in dst_token)
        if c_units and units == 2 * c_units[1]:
            c_sum(pe, sem, acc, 16 + 2 * c_units[0] + 2 * (c_units[1] - 1), c_units[1] - 1)

    def proj_evac(eng, which, sem, first, units, dst, c=None):
        name = ("evac_act", "evac_dve")[which]
        copy, part = (eng.tensor_copy, low_a) if which else (eng.copy, high_a)
        turns = units // NA

        def one(j, i=None, ahead=True):
            if ahead:
                part(eng, first + j + 2, i)
            if j % 2 == which:
                eng.wait_ge(a_used, plus(first + j + 1, i, NA))
                to = dst[:, 2 * j:2 * j + 2, :] if i is None else dst[:, bass.ds(i * (2 * NA) + 2 * j, 2), :]
                copy(to, PS[:, j % 4, :].rearrange("p (b t) -> p b t", b=2)).then_inc(sem(name), 1)
            elif c and (i is not None or j < 2 * C_UNITS[c[2]][1]):
                c_scale(eng, sem, c[0], c[1], c[3], C_UNITS[c[2]][0], j // 2, i, NA // 2)

        last = turns - 1 if units % NA < 2 else turns
        if last > 1:
            for j in range(NA):
                one(j)
            with eng.Fori(1, last) as i:
                for j in range(NA):
                    one(j, i)
            done = last * NA
        else:
            done = 0
        for j in range(done, units):
            one(j, None, j + 2 < units)

    def mod_unit(pe, n, layer, bank, col):
        a_wait(pe, n)
        w = ringA[:, n % NA]
        for b in range(2):
            for k in range(KC):
                mm = pe.matmul(PS[:, bank, col + b:col + b + 1], w[:, k, b * P:(b + 1) * P],
                               cs[:, min(layer, 1), k:k + 1], start=(k == 0), stop=(k == KC - 1))
        mm.then_inc(a_used, 1)

    mods_flat = mods3[:, :, :].rearrange("p l c -> p (l c)")

    def mods_out(dve, sem, counter, count, src, lo, hi, scales):
        dve.wait_ge(counter, count)
        dve.tensor_tensor(mods_flat[:, lo:hi], src, par[:, PAR["mod_b"][0] + lo:PAR["mod_b"][0] + hi], ALU.add).then_inc(sem("mods"), 1)
        dve.wait_ge(sem("mods"), 1)
        for layer, q, w in scales:
            at = 8 + 24 * q
            dve.scalar_tensor_tensor(normw3[:, layer, q, :], mods3[:, layer, at:at + 8], 1.0, w, ALU.add, ALU.mult
                                     ).then_inc(sem("normw"), 1)

    def c_loads(pool, sem, bufC, name):
        first, n = C_UNITS[name]
        pool.dma_start(bufC.rearrange("p k c -> p (k c)"), wc[first]).then_inc(c_full, 16)
        with pool.Fori(1, n) as i:
            pool.wait_ge(sem("c_used"), i)
            pool.dma_start(bufC.rearrange("p k c -> p (k c)"),
                           wc[bass.ds(i + first, 1)].rearrange("a p c -> p (a c)")).then_inc(c_full, 16)

    def c_scale(dve, sem, bufC, acc, c_of, first, m, i=None, per=0):
        dve.wait_ge(c_full, plus(16 * (first + m + 1), i, 16 * per))
        if i is not None or m >= 2:
            dve.wait_ge(sem("c_summed"), plus(m - 1, i, per))
        for k in range(KC):
            col = cs[:, c_of, k:k + 1]
            if k == 0:
                ins_ = dve.tensor_scalar(acc[:, m % 2, :], bufC[:, k, :], col, None, ALU.mult)
            else:
                dve.wait_ge(sem("c_block"), plus((KC - 1) * m + k, i, (KC - 1) * per))
                ins_ = dve.scalar_tensor_tensor(acc[:, m % 2, :], bufC[:, k, :], col, acc[:, m % 2, :], ALU.mult, ALU.add)
            if k < KC - 1:
                ins_.then_inc(sem("c_block"), 1)
        ins_.then_inc(sem("c_used"), 1)

    def c_sum(pe, sem, acc, col, m, i=None, per=0, bank=5, fixed=False):
        pe.wait_ge(sem("c_used"), plus(m + 1, i, per))
        for b in range(2):
            to = PS[:, bank, col + b:col + b + 1] if i is None or fixed else PS[:, bank, bass.ds(i * (2 * per) + (col + b), 1)]
            mm = pe.matmul(to, acc[:, m % 2, b * P:(b + 1) * P], ones[:, 0:1], start=True, stop=True)
        mm.then_inc(sem("c_summed"), 1)

    def first_stage():
        sem = stages.begin()
        a0, n = A_AT["mod"]
        with nc.Block(no_gpsimd_drain=True) as block:
            @block.sync
            def _(sp):
                sp.dma_start(par[:, :], par_dram).then_inc(sem("par"), 16)
                for m in range(NA):
                    load_a(sp, m, m)
                sp.dma_start(h[:, :, :], x_dram).then_inc(sem("x"), 16)
                sp.dma_start(con[:, :], con_dram[:, 0:N_KEPT]).then_inc(sem("con"), 16)
                refill_a(sp, a0, n)
                for m in range(NB):
                    load_b(sp, m, m)
                sp.wait_ge(sem("con"), 16)
                sp.wait_ge(sem("x"), 16)

            @block.scalar
            def _(act):
                act.wait_ge(sem("par"), 16)
                act.activation(cs[:, 0, :], pr("c"), ACT.Silu).then_inc(sem("cs"), 1)
                act.activation(cs[:, 1, :], pr("c2"), ACT.Silu).then_inc(sem("cs"), 1)

            @block.tensor
            def _(pe):
                pe.wait_ge(sem("cs"), 2)
                for j in range(n):
                    mod_unit(pe, a0 + j, 0, 0, 2 * j)

            @block.vector
            def _(dve):
                dve.wait_ge(sem("par"), 16)
                mods_out(dve, sem, a_used, a0 + n, PS[:, 0, 0:16], 0, 16, [(0, 0, pr("norm_mix"))])
        stages.end()

    def norm_stage(which, layer, following, small=None):
        first = A_AT[following][0]
        sem = stages.begin()
        with ExitStack() as st:
            squares = sb(f"squares{stages.k}", [P, KC, T], st)
            with nc.Block(no_gpsimd_drain=True) as block:
                @block.scalar
                def _(act):
                    act.activation(squares[:, :, :], h[:, :, :], ACT.Square).then_inc(sem("squares"), 1)
                    high_a(act, first)
                    act.wait_ge(sem("square_sums"), 1)
                    act.activation(rstd[:, :], PS[:, 0, 0:T], ACT.Sqrt, bias=eps, scale=1.0 / D).then_inc(sem("root"), 1)
                    high_a(act, first + 1)
                    for q in range(2):
                        act.wait_ge(sem("xm"), 4 * q + 4)
                        act.copy(xh[:, 4 * q:4 * q + 4, :], xm[:, 4 * q:4 * q + 4, :]).then_inc(sem("x_high"), 1)

                @block.tensor
                def _(pe):
                    rms_pe(pe, sem, squares, KC, PS[:, 0, 0:T])
                    if small is not None:
                        pe.wait_ge(sem("xm"), KC)
                        small(pe).then_inc(sem("small"), 1)

                @block.vector
                def _(dve):
                    link = Chain(dve, sem("dve"))
                    low_a(dve, first)
                    dve.wait_ge(sem("root"), 1)
                    link(dve.reciprocal(rstd[:, :], rstd[:, :]))
                    link(dve.tensor_tensor(squares[:, :, :], h[:, :, :], rep(rstd[:, :], KC), ALU.mult))
                    for k in range(KC):
                        dve.tensor_scalar(xm[:, k, :], squares[:, k, :], normw3[:, layer, which, k:k + 1],
                                          mods3[:, layer, 24 * which + k:24 * which + k + 1], ALU.mult, ALU.add
                                          ).then_inc(sem("xm"), 1)
                    low_a(dve, first + 1)
                    if small is not None:
                        dve.wait_ge(sem("small"), 1)
                    low_x(dve, sem, xm, xh, xl, 2)
        stages.end()

    def norm_h(w, dst):
        sem = stages.begin()
        with ExitStack() as st:
            squares = sb(f"squares{stages.k}", [P, KC, T], st)
            with nc.Block(no_gpsimd_drain=True) as block:
                @block.scalar
                def _(act):
                    act.activation(squares[:, :, :], h[:, :, :], ACT.Square).then_inc(sem("squares"), 1)
                    act.wait_ge(sem("square_sums"), 1)
                    act.activation(rstd[:, :], PS[:, 0, 0:T], ACT.Sqrt, bias=eps, scale=1.0 / D).then_inc(sem("root"), 1)

                @block.tensor
                def _(pe):
                    rms_pe(pe, sem, squares, KC, PS[:, 0, 0:T])

                @block.vector
                def _(dve):
                    link = Chain(dve, sem("dve"))
                    dve.wait_ge(sem("root"), 1)
                    link(dve.reciprocal(rstd[:, :], rstd[:, :]))
                    link(dve.tensor_tensor(squares[:, :, :], h[:, :, :], rep(rstd[:, :], KC), ALU.mult))
                    for k in range(KC):
                        dve.tensor_scalar(dst[:, k, :], squares[:, k, :], w[:, k:k + 1], None, ALU.mult
                                          ).then_inc(sem("normed"), 1)

                if dst is not h:
                    @block.sync
                    def _(sp):
                        sp.wait_ge(sem("normed"), KC)
                        sp.dma_start(out, dst[:, :, :]).then_inc(sem("stored"), 16)
                        sp.wait_ge(sem("stored"), 16)
        stages.end()

    def small_ab(pe):
        w_ab = pr("w_ab").rearrange("p (k c) -> p k c", k=KC)
        for t in range(2):
            for k in range(KC):
                mm = pe.matmul(PS[:, 4, t * 8:t * 8 + 8], xm[:, k, t * P:(t + 1) * P], w_ab[:, k, :],
                               start=(k == 0), stop=(k == KC - 1))
        return mm

    def small_dt(pe):
        w_dt = pr("w_dt").rearrange("p (k c) -> p k c", k=KC)
        for k in range(KC):
            mm = pe.matmul(PS[0:SSM_H, 4, 0:T], w_dt[:, k, :], xm[:, k, :], start=(k == 0), stop=(k == KC - 1))
        return mm

    def small_route(pe):
        wr = pr("w_route").rearrange("p (k c) -> p k c", k=KC)
        for t in range(2):
            for k in range(KC):
                mm = pe.matmul(PS[:, 4, t * 20:(t + 1) * 20], xm[:, k, t * P:(t + 1) * P], wr[:, k, :],
                               start=(k == 0), stop=(k == KC - 1))
        return mm

    def mixer_one():
        with ExitStack() as st:
            proj = sb("proj", [P, 64, T], st)
            gab = sb("gab", [P, 2, 8], st)
            sem = stages.begin()
            a0, n = A_AT["win"]
            cst = ExitStack()
            bufC, acc = sb("bufC1", [P, KC, 256], cst), sb("acc1", [P, 2, 256], cst)
            with nc.Block(no_gpsimd_drain=True) as block:
                @block.gpsimd
                def _(pool):
                    c_loads(pool, sem, bufC[:, :, :], "win")

                @block.sync
                def _(sp):
                    refill_a(sp, a0, n)

                @block.tensor
                def _(pe):
                    proj_pe(pe, sem, a0, n, dst_token=(4, 5, 6, 7), c_units=C_UNITS["win"], acc=acc)

                @block.scalar
                def _(act):
                    proj_evac(act, 0, sem, a0, n, proj)

                @block.vector
                def _(dve):
                    dve.tensor_copy(gab[:, :, :], PS[:, 4, 0:16].rearrange("p (t c) -> p t c", t=2)).then_inc(sem("gab"), 1)
                    proj_evac(dve, 1, sem, a0, n, proj, (bufC[:, :, :], acc, "win", 0))
                    mods_out(dve, sem, sem("c_summed"), 16, PS[:, 5, 16:48], 16, 48, [(0, 1, pr("norm_ffn"))])
            cst.close()
            stages.end()
            mix, mix_low = sb2("mix", [P, KC, T], st)
            retention(proj, mix)
            delta_rule(proj, gab, mix)
            out_proj("wout", mix, mix_low, None, 0)

    def out_proj(name, src, low_src, bias, layer):
        sem = stages.begin()
        a0, n = A_AT[name]
        with ExitStack() as st:
            biased = sb(f"biased{stages.k}", [P, KC, T], st) if bias is not None else None
            with nc.Block(no_gpsimd_drain=True) as block:
                @block.sync
                def _(sp):
                    refill_a(sp, a0, n)

                @block.tensor
                def _(pe):
                    pe.wait_ge(sem("x_low"), 2)
                    proj_pe(pe, sem, a0, n, low_src=low_src)

                @block.scalar
                def _(act):
                    high_x(act, sem, src, xh, 2)
                    for u in range(2, n):
                        high_a(act, a0 + u)

                @block.vector
                def _(dve):
                    low_x(dve, sem, src, xh, low_src, 2)
                    for b in range(KC):
                        if b % 2 == 0 and b < 4:
                            low_a(dve, a0 + 2 + b // 2)
                        dve.wait_ge(a_used, a0 + b // 2 + 1)
                        psum = PS[:, b // 2, (b % 2) * T:(b % 2 + 1) * T]
                        gate = mods3[:, layer, 16 + b:17 + b]
                        if bias is None:
                            dve.scalar_tensor_tensor(h[:, b, :], psum, gate, h[:, b, :], ALU.mult, ALU.add
                                                     ).then_inc(sem("h"), 1)
                        else:
                            dve.tensor_scalar(biased[:, b, :], psum, bias[:, b:b + 1], gate, ALU.add, ALU.mult
                                              ).then_inc(sem("biased"), 1)
                            dve.wait_ge(sem("biased"), b + 1)
                            dve.tensor_tensor(h[:, b, :], h[:, b, :], biased[:, b, :], ALU.add).then_inc(sem("h"), 1)
            stages.end()

    def retention(proj, mix):
        sem = stages.begin()
        with ExitStack() as st:
            at0 = CON["cos"][0]
            n_rc = CON["strict"][0] - at0
            rcon = spare_highA[:, :, :, :].rearrange("p a k c -> p (a k c)")[:, 0:n_rc]

            def rc(name):
                at, w = CON[name]
                return rcon[:, at - at0:at - at0 + w]

            cos, sin, turn = rc("cos"), rc("sin"), rc("turn")
            ret = rc("ret").rearrange("p (h i) -> p h i", h=HEADS)
            turned = xm
            qk = proj[:, 0:8, :]
            S = proj[:, 0:6, :].rearrange("p a b -> p (a b)").rearrange("p (h i) -> p h i", h=HEADS)
            with nc.Block(no_gpsimd_drain=True) as block:
                @block.sync
                def _(sp):
                    sp.dma_start(rcon, con_dram[:, at0:CON["strict"][0]]).then_inc(sem("rcon"), 16)

                @block.tensor
                def _(pe):
                    pe.wait_ge(sem("rcon"), 16)
                    for b in range(8):
                        mm = pe.matmul(PS[:, b // 2, (b % 2) * T:(b % 2 + 1) * T], turn, qk[:, b, :], start=True, stop=True)
                    mm.then_inc(sem("halves_swapped"), 1)
                    pe.wait_ge(sem("roped"), 1)
                    for hd in range(HEADS):
                        q, k = qk[:, hd, :], qk[:, 4 + hd, :]
                        pe.matmul(PS[:, 4 + hd, 0:T], k[:, 0:P], q, start=True, stop=True)
                        pe.matmul(PS[:, 4 + hd, T:384], k[:, P:T], q[:, P:T], start=True, stop=True
                                  ).then_inc(sem("scores"), 1)
                    for hd in range(HEADS):
                        pe.wait_ge(sem("decayed"), hd + 1)
                        for b in range(2):
                            o = PS[:, hd, b * T:(b + 1) * T]
                            v = [proj[:, 8 + 2 * hd + t, b * P:(b + 1) * P] for t in range(2)]
                            pe.matmul(o, v[0], S[:, hd, 0:T], start=True, stop=False, skip_group_check=True)
                            mm = pe.matmul(o[:, P:T], v[1], S[:, hd, T:384], start=False, stop=True, skip_group_check=True)
                        mm.then_inc(sem("outputs"), 1)
                    for hd in range(HEADS):
                        pe.wait_ge(sem("squares"), hd + 1)
                        for b in range(2):
                            mm = pe.matmul(PS[:, 4 + hd // 2, (hd % 2) * T:(hd % 2 + 1) * T], ones, turned[:, 2 * hd + b, :],
                                           start=(b == 0), stop=(b == 1))
                        mm.then_inc(sem("square_sums"), 1)

                @block.scalar
                def _(act):
                    act.activation(proj[:, 16:24, :], proj[:, 16:24, :], ACT.Silu).then_inc(sem("silu"), 1)
                    for hd in range(HEADS):
                        act.wait_ge(sem("outputs"), hd + 1)
                        act.activation(turned[:, 2 * hd:2 * hd + 2, :], PS[:, hd, :].rearrange("p (b t) -> p b t", b=2),
                                       ACT.Square).then_inc(sem("squares"), 1)
                    act.wait_ge(sem("square_sums"), HEADS)
                    act.activation(S[:, :, 0:T].rearrange("p h i -> p h i"), PS[:, 4:6, :].rearrange("p a (b t) -> p (a b) t", b=2),
                                   ACT.Sqrt, bias=eps, scale=1.0 / 256).then_inc(sem("root"), 1)

                @block.vector
                def _(dve):
                    link = Chain(dve, sem("dve"))
                    dve.wait_ge(sem("halves_swapped"), 1)
                    dve.tensor_tensor(turned[:, :, :], PS[:, 0:4, :].rearrange("p a (b t) -> p (a b) t", b=2), rep(sin, 8),
                                      ALU.mult).then_inc(sem("turned"), 1)
                    link(dve.tensor_tensor(qk, qk, rep(cos, 8), ALU.mult))
                    dve.wait_ge(sem("turned"), 1)
                    dve.tensor_tensor(qk, qk, turned[:, :, :], ALU.add).then_inc(sem("roped"), 1)
                    dve.wait_ge(sem("scores"), HEADS)
                    for hd in range(HEADS):
                        dve.tensor_tensor(S[:, hd, :], PS[:, 4 + hd, 0:384], ret[:, hd, :], ALU.mult).then_inc(sem("decayed"), 1)
                    dve.wait_ge(sem("root"), 1)
                    link(dve.reciprocal(S[:, :, 0:T], S[:, :, 0:T]))
                    dve.wait_ge(sem("silu"), 1)
                    for hd in range(HEADS):
                        link(dve.tensor_tensor(mix[:, 2 * hd:2 * hd + 2, :], PS[:, hd, :].rearrange("p (b t) -> p b t", b=2),
                                               rep(S[:, hd, 0:T], 2), ALU.mult))
                    dve.tensor_tensor(mix[:, :, :], mix[:, :, :], proj[:, 16:24, :], ALU.mult).then_inc(sem("mix"), 1)
        stages.end()

    def delta_rule(proj, gab, mix):
        C8 = 2 * HEADS
        with ExitStack() as st:
            cv = proj[:, 0:16, :]
            sem = stages.begin()
            squares = proj[:, 16:24, :]
            vtok = xm[:, :, :]
            ktok = sb("ktok", [P, HEADS, P], st)
            small = sb("small", [P, 120], st)
            ld = small[:, 0:8]
            beta = small[:, 8:16]
            t0, t1, t2, t3, t4 = [small[:, 16 + 8 * i:24 + 8 * i] for i in range(5)]
            nea = small[:, 56:60]
            gcc = small[:, 64:72]
            nbe = small[:, 72:80]
            ekd = small[:, 80:88]
            with nc.Block(no_gpsimd_drain=True) as block:
                @block.vector
                def _(dve):
                    link = Chain(dve, sem("dve"))
                    cw = pr("gconv").rearrange("p (b i) -> p b i", b=16)
                    for tap in range(4):
                        for b in range(16):
                            x = proj[:, 24 + b, :]
                            if tap == 0:
                                i = dve.tensor_scalar(cv[:, b, :], x, cw[:, b, 3:4], None, ALU.mult)
                            else:
                                dve.wait_ge(sem("conv"), 16 * (tap - 1) + b + 1)
                                i = dve.scalar_tensor_tensor(cv[:, b, tap:T], x[:, 0:T - tap], cw[:, b, 3 - tap:4 - tap],
                                                             cv[:, b, tap:T], ALU.mult, ALU.add)
                            i.then_inc(sem("conv"), 1)
                    ga = gab[:, :, 0:4].rearrange("p t c -> p t c")
                    s2 = lambda a: a.rearrange("p (t c) -> p t c", t=2)
                    link(dve.tensor_tensor(s2(t0), ga, rep(pr("dt_bias"), 2), ALU.add))
                    link(dve.tensor_scalar(t1, t0, -1.0, None, ALU.mult))
                    link(dve.tensor_tensor(t1, t0, t1, ALU.min))
                    dve.tensor_scalar(t4, t0, 0.0, None, ALU.max).then_inc(sem("minus_abs"), 1)
                    dve.wait_ge(sem("exp_minus_abs"), 1)
                    link(dve.tensor_scalar(t2, t1, 1.0, None, ALU.add))
                    link(dve.tensor_scalar(t3, t2, -1.0, None, ALU.add))
                    link(dve.tensor_scalar(t0, t3, 0.0, None, ALU.is_equal))
                    dve.tensor_tensor(t3, t3, t0, ALU.add).then_inc(sem("u_minus_1"), 1)
                    dve.wait_ge(sem("ln_u"), 1)
                    link(dve.tensor_tensor(t2, t2, t0, ALU.add))
                    link(dve.reciprocal(t3, t3))
                    link(dve.tensor_tensor(t2, t2, t3, ALU.mult))
                    link(dve.tensor_tensor(t2, t2, t1, ALU.mult))
                    link(dve.tensor_tensor(t2, t2, t4, ALU.add))
                    link(dve.tensor_scalar(nea, nea, -1.0, None, ALU.mult))
                    dve.tensor_tensor(s2(ld), s2(t2), rep(nea, 2), ALU.mult).then_inc(sem("ld"), 1)
                    for q in range(2):
                        dve.wait_ge(sem("root"), q + 1)
                        link(dve.reciprocal(squares[:, 4 * q:4 * q + 4, :], squares[:, 4 * q:4 * q + 4, :]))
                        if q == 0:
                            i = dve.scalar_tensor_tensor(cv[:, 0:4, :], cv[:, 0:4, :], float(P) ** -0.5, squares[:, 0:4, :],
                                                         ALU.mult, ALU.mult)
                        else:
                            i = dve.tensor_tensor(cv[:, 4:8, :], cv[:, 4:8, :], squares[:, 4:8, :], ALU.mult)
                        i.then_inc(sem("qk_normed"), 1)
                    for c in range(2):
                        for hd in range(HEADS):
                            if hd % 2 == 0:
                                dve.wait_ge(sem("v_turned"), 2 * c + hd // 2 + 1)
                            dve.tensor_scalar(vtok[:, 4 * c + hd, :], PS[:, 4 + 2 * c + hd // 2, (hd % 2) * 256:(hd % 2 + 1) * 256],
                                              beta[:, 4 * c + hd:4 * c + hd + 1], None, ALU.mult).then_inc(sem("vtok"), 1)
                    dve.wait_ge(sem("gcc_done"), 1)
                    dve.tensor_copy(gcc, PS[:, 3, 0:8]).then_inc(sem("gcc"), 1)
                    dve.wait_ge(sem("k_turned"), 1)
                    dve.tensor_copy(ktok[:, :, :], PS[:, 0, :].rearrange("p (h d) -> p h d", h=HEADS)).then_inc(sem("ktok"), 1)

                @block.scalar
                def _(act):
                    act.activation(proj[:, 48:64, :], proj[:, 48:64, :], ACT.Sigmoid).then_inc(sem("act"), 1)
                    act.activation(beta.rearrange("p (t c) -> p t c", t=2), gab[:, :, 4:8], ACT.Sigmoid).then_inc(sem("beta"), 1)
                    act.activation(proj[:, 40:48, :], proj[:, 40:48, :], ACT.Silu).then_inc(sem("act"), 1)
                    act.wait_ge(sem("conv"), 64)
                    act.activation(cv, cv, ACT.Silu).then_inc(sem("silu"), 1)
                    act.wait_ge(sem("silu"), 1)
                    act.activation(squares, cv[:, 0:8, :], ACT.Square).then_inc(sem("squares"), 1)
                    act.activation(nea, pr("a_log"), ACT.Exp).then_inc(sem("act"), 1)
                    act.wait_ge(sem("minus_abs"), 1)
                    act.activation(t1, t1, ACT.Exp).then_inc(sem("exp_minus_abs"), 1)
                    act.wait_ge(sem("u_minus_1"), 1)
                    act.activation(t2, t2, ACT.Ln).then_inc(sem("ln_u"), 1)
                    for q in range(2):
                        act.wait_ge(sem("square_sums"), 4 * q + 4)
                        act.activation(squares[:, 4 * q:4 * q + 4, :], PS[:, 2 * q:2 * q + 2, :].rearrange("p a (b t) -> p (a b) t", b=2),
                                       ACT.Sqrt, bias=eps).then_inc(sem("root"), 1)

                @block.tensor
                def _(pe):
                    pe.wait_ge(sem("squares"), 1)
                    for b in range(8):
                        pe.matmul(PS[:, b // 2, (b % 2) * T:(b % 2 + 1) * T], ones, squares[:, b, :], start=True, stop=True
                                  ).then_inc(sem("square_sums"), 1)
                    for c in range(2):
                        for hd in range(HEADS):
                            for b in range(2):
                                mm = pe.transpose(PS[:, 4 + 2 * c + hd // 2, (hd % 2) * 256 + b * P:(hd % 2) * 256 + (b + 1) * P],
                                                  cv[:, 8 + 2 * hd + b, c * P:(c + 1) * P], ident)
                            if hd % 2:
                                mm.then_inc(sem("v_turned"), 1)
                    pe.wait_ge(sem("root"), 2)
                    pe.wait_ge(sem("ld"), 1)
                    pe.matmul(PS[:, 3, 0:8], upto[:, 0, 0:P], ld, start=True, stop=True).then_inc(sem("gcc_done"), 1)
                    pe.wait_ge(sem("qk_normed"), 2)
                    for hd in range(HEADS):
                        mm = pe.transpose(PS[:, 0, hd * P:(hd + 1) * P], cv[:, 4 + hd, 0:P], ident)
                    mm.then_inc(sem("k_turned"), 1)
            stages.end()

            sem = stages.begin()
            at0 = CON["strict"][0]
            free = spare_xh[:, :, :].rearrange("p k t -> p (k t)")
            gcon = free[:, 0:CON["bucket"][0] - at0]
            strict = gcon[:, 0:P]
            levels = gcon[:, P:].rearrange("p (n i) -> p n i", n=7)
            V4 = lambda a: proj[:, a:a + 4, :].rearrange("p a (b i) -> p (a b) i", b=2)
            dec, LT, M, MT = V4(24), V4(28), V4(32), V4(36)
            QK = V4(16)
            Loff, Pm = V4(20), free[:, 1024:2048].rearrange("p (a i) -> p a i", a=C8)
            egB = sb("egB", [P, HEADS, P], st)
            two = lambda b: PS[:, b:b + 2, :].rearrange("p a (c i) -> p (a c) i", c=4)
            with nc.Block(no_gpsimd_drain=True) as block:
                @block.sync
                def _(sp):
                    sp.dma_start(gcon, con_dram[:, at0:CON["bucket"][0]]).then_inc(sem("gcon"), 16)

                @block.tensor
                def _(pe):
                    for q in range(C8):
                        c, hd = q // 4, q % 4
                        kc = cv[:, 4 + hd, c * P:(c + 1) * P]
                        at = slice((q % 4) * P, (q % 4 + 1) * P)
                        pe.matmul(PS[:, c, at], ld[:, q:q + 1].to_broadcast([P, P]), upto[:, 0, 0:P], start=True, stop=True)
                        pe.matmul(PS[:, 2 + c, at], beta[:, q:q + 1].to_broadcast([P, P]), ident, start=True, stop=True)
                        pe.matmul(PS[:, 4 + c, at], kc, kc, start=True, stop=True)
                        mm = pe.matmul(PS[:, 6 + c, at], kc, cv[:, hd, c * P:(c + 1) * P], start=True, stop=True)
                    mm.then_inc(sem("products"), 1)
                    pe.wait_ge(sem("MT"), 1)
                    for q in range(C8):
                        mm = pe.transpose(PS[:, q // 4, (q % 4) * P:(q % 4 + 1) * P], MT[:, q, :], ident)
                    mm.then_inc(sem("M_turned"), 1)
                    for n in range(1, 7):
                        pe.wait_ge(sem("M"), n)
                        pe.wait_ge(sem("MT"), n)
                        pe.wait_ge(sem("Loff"), n)
                        for q in range(C8):
                            mm = pe.matmul(PS[:, 2 + q // 4, (q % 4) * P:(q % 4 + 1) * P], Loff[:, q, :], M[:, q, :],
                                           start=True, stop=True)
                        mm.then_inc(sem("P_done"), 1)
                        pe.wait_ge(sem("P"), n)
                        for q in range(C8):
                            mm = pe.matmul(PS[:, 4 + q // 4, (q % 4) * P:(q % 4 + 1) * P], Pm[:, q, :], MT[:, q, :],
                                           start=True, stop=True)
                        mm.then_inc(sem("N2_done"), 1)
                        if n < 6:
                            for q in range(C8):
                                mm = pe.matmul(PS[:, 6 + q // 4, (q % 4) * P:(q % 4 + 1) * P], MT[:, q, :], Pm[:, q, :],
                                               start=True, stop=True)
                            mm.then_inc(sem("N1_done"), 1)

                @block.scalar
                def _(act):
                    act.wait_ge(sem("products"), 1)
                    act.activation(egB[:, :, :], PS[:, 1, :].rearrange("p (h i) -> p h i", h=HEADS), ACT.Exp).then_inc(sem("egB"), 1)
                    act.activation(ekd[:, 4:8], gcc[:, 4:8], ACT.Exp).then_inc(sem("egc"), 1)
                    act.wait_ge(sem("last_less"), 1)
                    act.activation(ekd[:, 0:4], ekd[:, 0:4], ACT.Exp).then_inc(sem("act"), 1)
                    act.wait_ge(sem("less"), C8)
                    act.activation(dec, dec, ACT.Exp).then_inc(sem("decays"), 1)
                    for n in range(1, 7):
                        act.wait_ge(sem("P_done"), n)
                        if n > 1:
                            act.wait_ge(sem("N2_done"), n - 1)
                            act.wait_ge(sem("N1_done"), n - 1)
                        act.copy(Pm, two(2)).then_inc(sem("P"), 1)

                @block.vector
                def _(dve):
                    link = Chain(dve, sem("dve"))
                    dve.wait_ge(sem("products"), 1)
                    for q in range(C8):
                        if q == 4:
                            dve.wait_ge(sem("egB"), 1)
                        dve.tensor_scalar(dec[:, q, :], PS[:, q // 4, (q % 4) * P:(q % 4 + 1) * P], gcc[:, q:q + 1], 0.0,
                                          ALU.subtract, ALU.min).then_inc(sem("less"), 1)
                    dve.tensor_tensor(ekd[:, 0:4], PS[:, 0, P - 1:512:P], gcc[:, 0:4], ALU.subtract).then_inc(sem("last_less"), 1)
                    dve.wait_ge(sem("egc"), 1)
                    dve.scalar_tensor_tensor(nbe[:, 4:8], ekd[:, 4:8], -1.0, beta[:, 4:8], ALU.mult, ALU.mult).then_inc(sem("nbe"), 1)
                    dve.wait_ge(sem("decays"), 1)
                    link(dve.tensor_tensor(dec, dec, rep(upto[:, 0, 0:P], C8), ALU.mult))
                    dve.tensor_tensor(QK, two(6), dec, ALU.mult).then_inc(sem("QK"), 1)
                    link(dve.tensor_tensor(LT, two(4), dec, ALU.mult))
                    link(dve.tensor_tensor(LT, LT, two(2), ALU.mult))
                    dve.wait_ge(sem("gcon"), 16)
                    link(dve.tensor_tensor(LT, LT, rep(strict, C8), ALU.mult))
                    link(dve.tensor_tensor(MT, LT, rep(levels[:, 0, :], C8), ALU.mult))
                    dve.scalar_tensor_tensor(MT, MT, -1.0, rep(ident, C8), ALU.mult, ALU.add).then_inc(sem("MT"), 1)
                    dve.tensor_tensor(Loff, LT, rep(levels[:, 1, :], C8), ALU.mult).then_inc(sem("Loff"), 1)
                    dve.wait_ge(sem("M_turned"), 1)
                    dve.tensor_copy(M, two(0)).then_inc(sem("M"), 1)
                    for n in range(1, 7):
                        if n < 6:
                            dve.wait_ge(sem("P_done"), n)
                            dve.tensor_tensor(Loff, LT, rep(levels[:, n + 1, :], C8), ALU.mult).then_inc(sem("Loff"), 1)
                            dve.wait_ge(sem("N1_done"), n)
                            dve.wait_ge(sem("M"), n)
                            dve.tensor_tensor(M, M, two(6), ALU.subtract).then_inc(sem("M"), 1)
                        dve.wait_ge(sem("N2_done"), n)
                        dve.wait_ge(sem("MT"), n)
                        dve.tensor_tensor(MT, MT, two(4), ALU.subtract).then_inc(sem("MT"), 1)
            stages.end()

            sem = stages.begin()
            vn = Pm.rearrange("p a b -> p (a b)").rearrange("p (h v) -> p h v", h=HEADS)
            vs = dec.rearrange("p a b -> p (a b)").rearrange("p (h v) -> p h v", h=HEADS)
            state = M.rearrange("p a b -> p (a b)").rearrange("p (h v) -> p h v", h=HEADS)
            rhs = Loff.rearrange("p a b -> p (a b)").rearrange("p (h v) -> p h v", h=HEADS)
            qg = LT[:, 0:4, :]
            sq = cv[:, 8:16, :]
            r4 = proj[:, 24:28, :]
            y = cv[:, 0:8, :]
            heads2 = lambda b: PS[:, b:b + 2, :].rearrange("p a (c v) -> p (a c) v", c=2)
            o_of = lambda hd, b, c: PS[:, 4 + hd, b * T + c * P:b * T + (c + 1) * P]
            with nc.Block(no_gpsimd_drain=True) as block:
                @block.tensor
                def _(pe):
                    for hd in range(HEADS):
                        mm = pe.matmul(PS[:, hd // 2, (hd % 2) * 256:(hd % 2 + 1) * 256], MT[:, hd, :], vtok[:, hd, :], start=True, stop=True)
                    mm.then_inc(sem("u_done"), 1)
                    pe.wait_ge(sem("vs"), HEADS)
                    for hd in range(HEADS):
                        mm = pe.matmul(PS[:, 2 + hd // 2, (hd % 2) * 256:(hd % 2 + 1) * 256], ktok[:, hd, :], vs[:, hd, :], start=True, stop=True)
                    mm.then_inc(sem("state_done"), 1)
                    pe.wait_ge(sem("vn"), 1)
                    for hd in range(HEADS):
                        for b in range(2):
                            mm = pe.matmul(o_of(hd, b, 0), vn[:, hd, b * P:(b + 1) * P], QK[:, hd, :], start=True, stop=True)
                    mm.then_inc(sem("o0_done"), 1)
                    pe.wait_ge(sem("state"), 1)
                    for hd in range(HEADS):
                        mm = pe.matmul(PS[:, hd // 2, (hd % 2) * 256:(hd % 2 + 1) * 256], cv[:, 4 + hd, P:T], state[:, hd, :], start=True, stop=True)
                    mm.then_inc(sem("ks_done"), 1)
                    pe.wait_ge(sem("rhs"), HEADS)
                    for hd in range(HEADS):
                        mm = pe.matmul(PS[:, 2 + hd // 2, (hd % 2) * 256:(hd % 2 + 1) * 256], MT[:, 4 + hd, :], rhs[:, hd, :], start=True, stop=True)
                    mm.then_inc(sem("u1_done"), 1)
                    pe.wait_ge(sem("vn"), 2)
                    pe.wait_ge(sem("qg"), 1)
                    for hd in range(HEADS):
                        for b in range(2):
                            pe.matmul(o_of(hd, b, 1), vn[:, hd, b * P:(b + 1) * P], QK[:, 4 + hd, :], start=True, stop=False)
                            mm = pe.matmul(o_of(hd, b, 1), state[:, hd, b * P:(b + 1) * P], qg[:, hd, :], start=False, stop=True)
                        mm.then_inc(sem("o_done"), 1)
                    for hd in range(HEADS):
                        pe.wait_ge(sem("squares"), hd + 1)
                        for b in range(2):
                            mm = pe.matmul(PS[:, hd // 2, (hd % 2) * T:(hd % 2 + 1) * T], ones, sq[:, 2 * hd + b, :],
                                           start=(b == 0), stop=(b == 1))
                        mm.then_inc(sem("square_sums"), 1)

                @block.scalar
                def _(act):
                    act.wait_ge(sem("u_done"), 1)
                    act.copy(vn[:, :, :], heads2(0)).then_inc(sem("vn"), 1)
                    act.wait_ge(sem("state_done"), 1)
                    act.copy(state, heads2(2)).then_inc(sem("state"), 1)
                    for u in range(2):
                        high_a(act, A_AT["wout"][0] + u)
                    act.wait_ge(sem("u1_done"), 1)
                    act.wait_ge(sem("o0_done"), 1)
                    act.wait_ge(sem("vs"), HEADS)
                    act.copy(vn[:, :, :], heads2(2)).then_inc(sem("vn"), 1)
                    for hd in range(HEADS):
                        act.wait_ge(sem("o_done"), hd + 1)
                        act.activation(sq[:, 2 * hd:2 * hd + 2, :], PS[:, 4 + hd, :].rearrange("p (b t) -> p b t", b=2),
                                       ACT.Square).then_inc(sem("squares"), 1)
                    act.wait_ge(sem("square_sums"), HEADS)
                    act.activation(r4, PS[:, 0:2, :].rearrange("p a (b t) -> p (a b) t", b=2), ACT.Sqrt, bias=eps, scale=1.0 / 256
                                   ).then_inc(sem("root"), 1)

                @block.vector
                def _(dve):
                    link = Chain(dve, sem("dve"))
                    dve.tensor_tensor(qg, cv[:, 0:4, P:T], egB[:, :, :], ALU.mult).then_inc(sem("qg"), 1)
                    dve.wait_ge(sem("vn"), 1)
                    for hd in range(HEADS):
                        dve.tensor_scalar(vs[:, hd, :], vn[:, hd, :], ekd[:, hd:hd + 1], None, ALU.mult).then_inc(sem("vs"), 1)
                    dve.wait_ge(sem("ks_done"), 1)
                    for hd in range(HEADS):
                        dve.scalar_tensor_tensor(rhs[:, hd, :], PS[:, hd // 2, (hd % 2) * 256:(hd % 2 + 1) * 256],
                                                 nbe[:, 4 + hd:5 + hd], vtok[:, 4 + hd, :], ALU.mult, ALU.add).then_inc(sem("rhs"), 1)
                    for u in range(2):
                        low_a(dve, A_AT["wout"][0] + u)
                    dve.wait_ge(sem("root"), 1)
                    link(dve.reciprocal(r4, r4))
                    for hd in range(HEADS):
                        for b in range(2):
                            i = dve.scalar_tensor_tensor(y[:, 2 * hd + b, :], PS[:, 4 + hd, b * T:(b + 1) * T],
                                                         pr("gdn_w", b, b + 1), r4[:, hd, :], ALU.mult, ALU.mult)
                    link(i)
                    link(dve.tensor_tensor(y, y, proj[:, 40:48, :], ALU.mult))
                    link(dve.tensor_tensor(y, y, proj[:, 56:64, :], ALU.mult))
                    link(dve.tensor_tensor(mix[:, :, :], mix[:, :, :], proj[:, 48:56, :], ALU.mult))
                    dve.tensor_tensor(mix[:, :, :], mix[:, :, :], y, ALU.add).then_inc(sem("mix"), 1)
            stages.end()

    def down_pe(pe, highB, n, hidden, first, last):
        for kf in range(2):
            for ob in range(KC):
                at = slice(ob * P, (ob + 1) * P)
                mm = mm3(pe, PS[:, 4 + ob // 2, (ob % 2) * T:(ob % 2 + 1) * T], highB[:, n % 2, kf, at], lowB[:, n % NB, kf, at],
                         hidden[kf][0], hidden[kf][1], start=(first and kf == 0 and ob % 2 == 0), stop=last, skip_group_check=True)
        mm.then_inc(b_used, 1)

    def swiglu(name, steps, combB, layer):
        sem = stages.begin()
        a0, b0 = A_AT[name][0], B_AT[name][0]
        modulate = name in C_UNITS
        with ExitStack() as st:
            silu = sb(f"silu{stages.k}", [P, 2, 512], st)
            hid_, hid_low = sb2(f"hid{stages.k}", [P, 2, 2, T], st)
            hid_high = st.enter_context(nc.sbuf_tensor(f"hid_high{stages.k}", [P, 2, 2, T], F32R))
            highB = st.enter_context(nc.sbuf_tensor(f"highB{stages.k}", [P, 2, 2, D], F32R))
            if modulate:
                bufC, acc = sb(f"bufC{stages.k}", [P, KC, 256], st), sb(f"acc{stages.k}", [P, 2, 256], st)
                sums = sb(f"sums{stages.k}", [P, 2 * C_UNITS[name][1]], st)
            turns = steps // 4

            with nc.Block(no_gpsimd_drain=True) as block:
                if modulate:
                    @block.gpsimd
                    def _(pool):
                        c_loads(pool, sem, bufC[:, :, :], name)

                @block.sync
                def _(sp):
                    refill_ab(sp, a0, b0, steps)

                def down(pe, s, i, first, last):
                    pe.wait_ge(b_low, plus(b0 + s + 1, i, 4))
                    pe.wait_ge(sem("hid_low"), plus(s + 1, i, 4))
                    down_pe(pe, highB, b0 + s, [(hid_high[:, s % 2, kf, :], hid_low[:, s % 2, kf, :]) for kf in range(2)], first, last)

                @block.tensor
                def _(pe):
                    def step(s, i=None):
                        if i is not None or s >= 2:
                            pe.wait_ge(sem("hidden"), plus(s - 1, i, 4))
                            if modulate and (i is not None or s >= 3):
                                pe.wait_ge(sem("c_out"), plus(s - 2, i, 4))
                        for j in range(2):
                            m = a0 + 2 * s + j
                            split_a_wait(pe, m, i)
                            for b in range(2):
                                at = slice(b * P, (b + 1) * P)
                                for k in range(KC):
                                    mm = mm3(pe, PS[:, 2 * (s % 2) + j, b * T:(b + 1) * T], highA[:, m % 2, k, at], lowA[:, m % NA, k, at],
                                             xh[:, k, :], xl[:, k, :], start=(k == 0), stop=(k == KC - 1))
                            mm.then_inc(a_used, 1)
                        if i is not None or s >= 1:
                            down(pe, s - 1, i, first=(i is None and s == 1), last=False)
                        if modulate and (i is not None or s >= 1):
                            pe.wait_ge(sem("silu"), plus(s + 1, i, 4))
                            c_sum(pe, sem, acc, 0, s - 1, i, 4, bank=2 * (s % 2), fixed=True)
                    for s in range(4):
                        step(s)
                    if turns > 1:
                        with pe.Fori(1, turns) as i:
                            for s in range(4):
                                step(s, i)
                    for s in range(4 * turns, steps):
                        step(s)
                    down(pe, steps - 1, None, False, True)
                    if modulate:
                        c_sum(pe, sem, acc, 0, steps - 1, bank=2 * (steps % 2))

                @block.scalar
                def _(act):
                    def step(s, i=None, ahead=True):
                        act.wait_ge(a_used, plus(a0 + 2 * s + 1, i, 8))
                        if i is not None or s >= 2:
                            act.wait_ge(sem("hidden"), plus(s - 1, i, 4))
                        act.activation(silu[:, s % 2, :], PS[:, 2 * (s % 2), :], ACT.Silu).then_inc(sem("silu"), 1)
                        if ahead:
                            high_a(act, a0 + 2 * s + 2, i)
                        act.wait_ge(sem("hidden"), plus(s + 1, i, 4))
                        if i is not None or s >= 2:
                            act.wait_ge(b_used, plus(b0 + s - 1, i, 4))
                        act.copy(hid_high[:, s % 2, :, :], hid_[:, s % 2, :, :]).then_inc(sem("hid_high"), 1)
                        if ahead:
                            high_a(act, a0 + 2 * s + 3, i)
                        high_b(act, highB, b0 + s, i)

                    for s in range(4):
                        step(s)
                    last = turns if steps % 4 else turns - 1
                    with act.Fori(1, last) as i:
                        for s in range(4):
                            step(s, i)
                    for s in range(4 * last, steps):
                        step(s, None, s + 1 < steps)

                @block.vector
                def _(dve):
                    def sums_out(m, i=None):
                        dve.wait_ge(sem("c_summed"), plus(m + 1, i, 4))
                        to = sums[:, 2 * m:2 * m + 2] if i is None else sums[:, bass.ds(i * 8 + 2 * m, 2)]
                        dve.tensor_copy(to, PS[:, 2 * ((m + 1) % 2), 0:2]).then_inc(sem("c_out"), 1)

                    def step(s, i=None, ahead=True):
                        hid = hid_[:, s % 2, :, :]
                        if ahead:
                            low_a(dve, a0 + 2 * s + 2, i)
                        dve.wait_ge(a_used, plus(a0 + 2 * s + 2, i, 8))
                        dve.wait_ge(sem("silu"), plus(s + 1, i, 4))
                        if i is not None or s >= 2:
                            dve.wait_ge(b_used, plus(b0 + s - 1, i, 4))
                        up = PS[:, 2 * (s % 2) + 1, :].rearrange("p (b t) -> p b t", b=2)
                        ins_ = dve.tensor_tensor(hid, silu[:, s % 2, :].rearrange("p (b t) -> p b t", b=2), up, ALU.mult)
                        if combB is not None:
                            ins_.then_inc(sem("unweighted"), 1)
                            dve.wait_ge(sem("unweighted"), plus(s + 1, i, 4))
                            comb = combB[:, s // 2, :] if i is None else combB[:, bass.ds(i * 2 + s // 2, 1), :].rearrange("p a t -> p (a t)")
                            ins_ = dve.tensor_tensor(hid, hid, rep(comb, 2), ALU.mult)
                        ins_.then_inc(sem("hidden"), 1)
                        dve.wait_ge(sem("hid_high"), plus(s + 1, i, 4))
                        dve.tensor_tensor(hid_low[:, s % 2, :, :], hid, hid_high[:, s % 2, :, :].bitcast(F32), ALU.subtract
                                          ).then_inc(sem("hid_low"), 1)
                        if modulate:
                            if i is not None or s >= 2:
                                sums_out(s - 2, i)
                            c_scale(dve, sem, bufC[:, :, :], acc, 1, C_UNITS[name][0], s, i, 4)
                        if ahead:
                            low_a(dve, a0 + 2 * s + 3, i)
                        low_b(dve, highB, b0 + s, i)

                    for s in range(4):
                        step(s)
                    last = turns if steps % 4 else turns - 1
                    with dve.Fori(1, last) as i:
                        for s in range(4):
                            step(s, i)
                    for s in range(4 * last, steps):
                        step(s, None, s + 1 < steps)
                    if modulate:
                        sums_out(steps - 2)
                        sums_out(steps - 1)
                        mods_out(dve, sem, sem("c_out"), steps, sums[:, :], 48, 112,
                                 [(1, 0, pr("norm_mix2", 0, 8)), (1, 1, pr("norm_ffn2", 0, 8)), (2, 0, pr("norm_mix2", 8, 16))])
                    dve.wait_ge(b_used, b0 + steps)
                    for b in range(KC):
                        dve.scalar_tensor_tensor(h[:, b, :], PS[:, 4 + b // 2, (b % 2) * T:(b % 2 + 1) * T], mods3[:, layer, 40 + b:41 + b],
                                                 h[:, b, :], ALU.mult, ALU.add).then_inc(sem("h"), 1)
            stages.end()

    def moe():
        with ExitStack() as st:
            combB = sb("combB", [P, N_EXP, T], st)
            w = sb("route", [P, 2, 80], st)
            sem = stages.begin()
            lg = w[:, :, 0:20]
            eq, pre, oh = w[:, :, 20:24], w[:, :, 24:28], w[:, :, 28:32]
            el, pe_, oh1, oh2 = w[:, :, 32:36], w[:, :, 36:40], w[:, :, 40:44], w[:, :, 44:48]
            m1, m2, s1, gt = w[:, :, 48:49], w[:, :, 49:50], w[:, :, 50:51], w[:, :, 51:52]
            comb = sb("comb", [P, 2, N_EXP], st)
            prod = sb("prod", [P, 2, N_EXP], st)
            spread = lambda a, n: bass.AP(tensor=a.tensor, offset=a.offset, ap=[list(a.ap[0]), list(a.ap[1]), [0, n]])
            with nc.Block(no_gpsimd_drain=True) as block:
                @block.tensor
                def _(pe):
                    pe.wait_ge(sem("comb"), 1)
                    for e in range(N_EXP):
                        if e >= 8 and e % 2 == 0:
                            pe.wait_ge(sem("combB"), (e - 8) // 2 + 1)
                        for t in range(2):
                            mm = pe.matmul(PS[:, 4 + e // 2 % 4, (e % 2) * T + t * P:(e % 2) * T + (t + 1) * P],
                                           comb[:, t, e:e + 1].to_broadcast([P, P]), ident, start=True, stop=True)
                        if e % 2:
                            mm.then_inc(sem("combB_done"), 1)

                @block.scalar
                def _(act):
                    act.wait_ge(sem("less_max"), 1)
                    act.activation(pre, eq, ACT.Exp).then_inc(sem("group_exp"), 1)
                    act.wait_ge(sem("less_max2"), 1)
                    act.activation(pe_, el, ACT.Exp).then_inc(sem("expert_exp"), 1)
                    for n in range(N_EXP // 2):
                        act.wait_ge(sem("combB_done"), n + 1)
                        act.copy(combB[:, 2 * n:2 * n + 2, :], PS[:, 4 + n % 4, :].rearrange("p (e t) -> p e t", e=2)
                                 ).then_inc(sem("combB"), 1)

                @block.vector
                def _(dve):
                    link = Chain(dve, sem("dve"))

                    def first_of(dst, hit, at):
                        link(dve.tensor_copy(at, hit))
                        link(dve.tensor_tensor(at[:, :, 1:4], at[:, :, 1:4], hit[:, :, 0:3], ALU.add))
                        link(dve.tensor_tensor(at[:, :, 2:4], at[:, :, 2:4], hit[:, :, 0:2], ALU.add))
                        link(dve.tensor_tensor(at[:, :, 3:4], at[:, :, 3:4], hit[:, :, 0:1], ALU.add))
                        link(dve.tensor_scalar(at, at, 1.0, None, ALU.is_equal))
                        link(dve.tensor_tensor(dst, at, hit, ALU.mult))

                    link(dve.tensor_tensor(lg, PS[:, 4, 0:40].rearrange("p (t c) -> p t c", t=2), rep(pr("b_route"), 2), ALU.add))
                    link(dve.tensor_reduce(m1, lg[:, :, 0:4], AX_X, ALU.max))
                    dve.tensor_tensor(eq, lg[:, :, 0:4], spread(m1, 4), ALU.subtract).then_inc(sem("less_max"), 1)
                    dve.wait_ge(sem("group_exp"), 1)
                    link(dve.tensor_reduce(gt, pre, AX_X, ALU.add))
                    link(dve.reciprocal(gt, gt))
                    link(dve.tensor_tensor(pre, pre, spread(gt, 4), ALU.mult))
                    link(dve.tensor_reduce(gt, pre, AX_X, ALU.max))
                    link(dve.tensor_tensor(eq, pre, spread(gt, 4), ALU.is_equal))
                    first_of(oh, eq, pre)
                    for g in range(4):
                        link(dve.tensor_tensor(prod[:, :, 4 * g:4 * g + 4], lg[:, :, 4 + 4 * g:8 + 4 * g], spread(oh[:, :, g:g + 1], 4), ALU.mult))
                    link(dve.tensor_tensor(prod[:, :, 0:8], prod[:, :, 0:8], prod[:, :, 8:16], ALU.add))
                    link(dve.tensor_tensor(el, prod[:, :, 0:4], prod[:, :, 4:8], ALU.add))
                    link(dve.tensor_reduce(m1, el, AX_X, ALU.max))
                    dve.tensor_tensor(el, el, spread(m1, 4), ALU.subtract).then_inc(sem("less_max2"), 1)
                    dve.wait_ge(sem("expert_exp"), 1)
                    link(dve.tensor_reduce(s1, pe_, AX_X, ALU.add))
                    link(dve.reciprocal(s1, s1))
                    link(dve.tensor_tensor(pe_, pe_, spread(s1, 4), ALU.mult))
                    link(dve.tensor_reduce(m1, pe_, AX_X, ALU.max))
                    link(dve.tensor_tensor(eq, pe_, spread(m1, 4), ALU.is_equal))
                    first_of(oh1, eq, pre)
                    link(dve.scalar_tensor_tensor(pe_, oh1, -2.0, pe_, ALU.mult, ALU.add))
                    link(dve.tensor_reduce(m2, pe_, AX_X, ALU.max))
                    link(dve.tensor_tensor(eq, pe_, spread(m2, 4), ALU.is_equal))
                    first_of(oh2, eq, pre)
                    link(dve.tensor_tensor(s1, m1, m2, ALU.add))
                    link(dve.reciprocal(s1, s1))
                    link(dve.tensor_tensor(oh1, oh1, spread(m1, 4), ALU.mult))
                    link(dve.tensor_tensor(oh2, oh2, spread(m2, 4), ALU.mult))
                    link(dve.tensor_tensor(oh1, oh1, oh2, ALU.add))
                    link(dve.tensor_tensor(oh1, oh1, spread(s1, 4), ALU.mult))
                    link(dve.tensor_tensor(oh1, oh1, spread(gt, 4), ALU.mult))
                    for g in range(4):
                        i = dve.tensor_tensor(comb[:, :, 4 * g:4 * g + 4], oh1, spread(oh[:, :, g:g + 1], 4), ALU.mult)
                    i.then_inc(sem("comb"), 1)
            stages.end()
            swiglu("moe", 2 * N_EXP, combB, 0)

    def mixer_two():
        with ExitStack() as st:
            yb, yb_low = sb2("yb", [P, 16, T], st)
            state_space(yb)
            att, att_low = sb2("att", [P, KC, T], st)
            attention(att)
            sem = stages.begin()
            b0, n = B_AT["hyout"]
            high = st.enter_context(nc.sbuf_tensor("out_high", [P, 24, T], F32R))
            highB = st.enter_context(nc.sbuf_tensor("out_highB", [P, 2, 2, D], F32R))
            pair = lambda u: yb[:, 2 * u:2 * u + 2, :] if u < 8 else att[:, 2 * u - 16:2 * u - 14, :]
            low_pair = lambda u: yb_low[:, 2 * u:2 * u + 2, :] if u < 8 else att_low[:, 2 * u - 16:2 * u - 14, :]
            with nc.Block(no_gpsimd_drain=True) as block:
                @block.sync
                def _(sp):
                    refill_b(sp, b0, n)

                @block.scalar
                def _(act):
                    for u in range(n):
                        act.copy(high[:, 2 * u:2 * u + 2, :], pair(u)).then_inc(sem("x_high"), 1)
                        high_b(act, highB, b0 + u)

                @block.tensor
                def _(pe):
                    for u in range(n):
                        pe.wait_ge(sem("x_low"), u + 1)
                        pe.wait_ge(b_low, b0 + u + 1)
                        low = low_pair(u)
                        down_pe(pe, highB, b0 + u, [(high[:, 2 * u + kf, :], low[:, kf, :]) for kf in range(2)], u == 0, u == n - 1)

                @block.vector
                def _(dve):
                    for u in range(n):
                        dve.wait_ge(sem("x_high"), u + 1)
                        dve.tensor_tensor(low_pair(u), pair(u), high[:, 2 * u:2 * u + 2, :].bitcast(F32), ALU.subtract
                                          ).then_inc(sem("x_low"), 1)
                        low_b(dve, highB, b0 + u)
                    dve.wait_ge(b_used, b0 + n)
                    for b in range(KC):
                        dve.scalar_tensor_tensor(h[:, b, :], PS[:, 4 + b // 2, (b % 2) * T:(b % 2 + 1) * T], mods3[:, 1, 16 + b:17 + b],
                                                 h[:, b, :], ALU.mult, ALU.add).then_inc(sem("h"), 1)
            stages.end()

    def state_space(yb):
        with ExitStack() as st:
            zx = sb("zx", [P, 40, T], st)
            dts = sb("dts", [SSM_H, 7, T], st)
            sem = stages.begin()
            a0, n = A_AT["hyin"]
            cst = ExitStack()
            bufC, acc = sb("bufC2", [P, KC, 256], cst), sb("acc2", [P, 2, 256], cst)
            with nc.Block(no_gpsimd_drain=True) as block:
                @block.gpsimd
                def _(pool):
                    c_loads(pool, sem, bufC[:, :, :], "hyin")

                @block.sync
                def _(sp):
                    refill_a(sp, a0, n)

                @block.tensor
                def _(pe):
                    proj_pe(pe, sem, a0, n, c_units=C_UNITS["hyin"], acc=acc)

                @block.scalar
                def _(act):
                    proj_evac(act, 0, sem, a0, n, zx)

                @block.vector
                def _(dve):
                    dve.tensor_scalar(dts[:, 0, :], PS[0:SSM_H, 4, 0:T], pr("dt_bias2")[0:SSM_H, :], None, ALU.add).then_inc(sem("dt"), 1)
                    proj_evac(dve, 1, sem, a0, n, zx, (bufC[:, :, :], acc, "hyin", 1))
                    mods_out(dve, sem, sem("c_summed"), 8, PS[:, 5, 112:128], 112, 128, [])
            cst.close()
            stages.end()

            spare = spare_highA[:, :, :, :]
            bc = spare[:, 0, :, :]
            sem = stages.begin()
            xdt = zx[:, 16:32, :].rearrange("p a b -> p (a b)").rearrange("p (t c) -> p t c", t=2)
            tok = sb("tok", [P, 3, 2, SSM_H], st)
            cbm = sb("cbm", [P, 4, 384], st)
            na = sb("na", [SSM_H, 1], st)
            conv_to = lambda b: yb[:, b, :] if b < 16 else bc[:, b - 16, :]
            with nc.Block(no_gpsimd_drain=True) as block:
                @block.vector
                def _(dve):
                    link = Chain(dve, sem("dve"))
                    y, e, u, um, m0, dt, dA = [dts[:, i, :] for i in range(7)]
                    link(dve.tensor_scalar(e, y, -1.0, None, ALU.mult))
                    link(dve.tensor_tensor(e, y, e, ALU.min))
                    dve.tensor_scalar(m0, y, 0.0, None, ALU.max).then_inc(sem("minus_abs"), 1)
                    dve.wait_ge(sem("exp_minus_abs"), 1)
                    link(dve.tensor_scalar(u, e, 1.0, None, ALU.add))
                    link(dve.tensor_scalar(um, u, -1.0, None, ALU.add))
                    link(dve.tensor_scalar(y, um, 0.0, None, ALU.is_equal))
                    dve.tensor_tensor(um, um, y, ALU.add).then_inc(sem("u_minus_1"), 1)
                    dve.wait_ge(sem("ln_u"), 1)
                    link(dve.tensor_tensor(u, u, y, ALU.add))
                    link(dve.reciprocal(um, um))
                    link(dve.tensor_tensor(u, u, um, ALU.mult))
                    link(dve.tensor_tensor(u, u, e, ALU.mult))
                    link(dve.tensor_tensor(dt, u, m0, ALU.add))
                    link(dve.tensor_scalar(na[:, :], na[:, :], -1.0, None, ALU.mult))
                    dve.tensor_scalar(dA, dt, na[:, 0:1], None, ALU.mult).then_inc(sem("dA"), 1)
                    cw = pr("hconv").rearrange("p (b i) -> p b i", b=24)
                    for tap_ in range(4):
                        for b in range(24):
                            x, o = zx[:, 16 + b, :], conv_to(b)
                            if tap_ == 0:
                                i = dve.tensor_scalar(o, x, cw[:, b, 3:4], pr("hconv_b", b, b + 1), ALU.mult, ALU.add)
                            else:
                                dve.wait_ge(sem("conv"), 24 * (tap_ - 1) + b + 1)
                                i = dve.scalar_tensor_tensor(o[:, tap_:T], x[:, 0:T - tap_], cw[:, b, 3 - tap_:4 - tap_],
                                                             o[:, tap_:T], ALU.mult, ALU.add)
                            i.then_inc(sem("conv"), 1)
                    dve.wait_ge(sem("turned"), 1)
                    dve.tensor_copy(tok[:, 0:2, :, :], PS[:, 0, 0:128].rearrange("p (a t c) -> p a t c", a=2, t=2)).then_inc(sem("tok"), 1)
                    dve.wait_ge(sem("sums_done"), 1)
                    dve.tensor_copy(tok[:, 2, :, :], PS[:, 1, 0:64].rearrange("p (t c) -> p t c", t=2)).then_inc(sem("acs"), 1)
                    dve.tensor_copy(dA, PS[0:SSM_H, 1, 128:384]).then_inc(sem("acs"), 1)
                    dve.wait_ge(sem("cb_done"), 1)
                    dve.tensor_tensor(cbm[:, :, 0:T], PS[:, 4:8, 0:T], rep(upto[:, 0, :], 4), ALU.mult).then_inc(sem("cbm"), 1)
                    dve.tensor_tensor(cbm[:, :, T:384], PS[:, 4:8, T:384], rep(upto[:, 0, 0:P], 4), ALU.mult).then_inc(sem("cbm"), 1)
                    for n8 in range(8):
                        t, c4 = n8 // 4, n8 % 4
                        dve.wait_ge(sem("x_turned"), n8 + 1)
                        dve.tensor_tensor(xdt[:, t, c4 * 512:(c4 + 1) * 512].rearrange("p (h d) -> p h d", h=8),
                                          PS[:, n8 % 4, :].rearrange("p (h d) -> p h d", h=8),
                                          wide(tok[:, 0, t, 8 * c4:8 * c4 + 8], 64), ALU.mult).then_inc(sem("xdt"), 1)

                @block.scalar
                def _(act):
                    act.activation(na[:, :], pr("a_log2")[0:SSM_H, :], ACT.Exp).then_inc(sem("act"), 1)
                    act.wait_ge(sem("minus_abs"), 1)
                    act.activation(dts[:, 1, :], dts[:, 1, :], ACT.Exp).then_inc(sem("exp_minus_abs"), 1)
                    act.wait_ge(sem("u_minus_1"), 1)
                    act.activation(dts[:, 2, :], dts[:, 2, :], ACT.Ln).then_inc(sem("ln_u"), 1)
                    act.activation(zx[:, 0:16, :], zx[:, 0:16, :], ACT.Silu).then_inc(sem("act"), 1)
                    act.wait_ge(sem("conv"), 96)
                    act.activation(yb[:, :, :], yb[:, :, :], ACT.Silu).then_inc(sem("silu"), 1)
                    act.activation(bc, bc, ACT.Silu).then_inc(sem("silu"), 1)

                @block.tensor
                def _(pe):
                    pe.wait_ge(sem("dA"), 1)
                    for a in range(2):
                        for t in range(2):
                            mm = pe.transpose(PS[:, 0, (2 * a + t) * 32:(2 * a + t + 1) * 32], dts[:, 5 + a, t * P:(t + 1) * P], ident[0:SSM_H, 0:SSM_H])
                    mm.then_inc(sem("turned"), 1)
                    pe.wait_ge(sem("tok"), 1)
                    pe.matmul(PS[:, 1, 0:32], upto[:, 0, 0:P], tok[:, 1, 0, :], start=True, stop=True)
                    pe.matmul(PS[:, 1, 32:64], upto[:, 0, P:T], tok[:, 1, 0, :], start=True, stop=False)
                    pe.matmul(PS[:, 1, 32:64], upto[:, 1, P:T], tok[:, 1, 1, :], start=False, stop=True)
                    pe.matmul(PS[0:SSM_H, 1, 128:384], tok[:, 1, 0, :], upto[:, 0, :], start=True, stop=False)
                    pe.matmul(PS[0:SSM_H, 1, 128:384], tok[:, 1, 1, :], upto[:, 1, :], start=False, stop=True).then_inc(sem("sums_done"), 1)
                    pe.wait_ge(sem("silu"), 2)
                    for g in range(4):
                        pe.matmul(PS[:, 4 + g, 0:T], bc[:, g, 0:P], bc[:, 4 + g, :], start=True, stop=True)
                        mm = pe.matmul(PS[:, 4 + g, T:384], bc[:, g, P:T], bc[:, 4 + g, P:T], start=True, stop=True)
                    mm.then_inc(sem("cb_done"), 1)
                    pe.wait_ge(sem("acs"), 2)
                    for n8 in range(8):
                        t, c4 = n8 // 4, n8 % 4
                        if n8 >= 4:
                            pe.wait_ge(sem("xdt"), n8 - 3)
                        for j in range(4):
                            mm = pe.transpose(PS[:, n8 % 4, j * P:(j + 1) * P], yb[:, 4 * c4 + j, t * P:(t + 1) * P], ident)
                        mm.then_inc(sem("x_turned"), 1)
            stages.end()

            sem = stages.begin()
            mt_dl = spare[:, 1, :, :].rearrange("p k c -> p (k c)")[:, 0:1536].rearrange("p (a b i) -> p a b i", a=2, b=2)
            mt, dl = mt_dl[:, 0], mt_dl[:, 1]
            acsT, acs = dts[:, 6, :], tok[:, 2, :, :]
            with nc.Block(no_gpsimd_drain=True) as block:
                @block.tensor
                def _(pe):
                    def spread_head(hd):
                        if hd >= 2:
                            pe.wait_ge(sem("less"), 2 * (hd - 1))
                        pe.matmul(PS[:, hd % 2, 0:T], ident[0:SSM_H, hd:hd + 1].to_broadcast([SSM_H, P]), acsT,
                                  start=True, stop=True).then_inc(sem("spread"), 1)

                    spread_head(0)
                    for hd in range(SSM_H):
                        if hd + 1 < SSM_H:
                            spread_head(hd + 1)
                        pe.wait_ge(sem("mt"), hd + 1)
                        if hd >= 8:
                            pe.wait_ge(sem("y"), hd // 2 - 3)
                        at = (hd % 2) * 64
                        o = PS[at:at + 64, 4 + hd // 2 % 4, 0:T]
                        pe.matmul(o, xdt[:, 0, hd * 64:(hd + 1) * 64], mt[:, hd % 2, 0:T], start=True, stop=False, skip_group_check=True)
                        pe.matmul(o[:, P:T], xdt[:, 1, hd * 64:(hd + 1) * 64], mt[:, hd % 2, T:384], start=False, stop=True,
                                  skip_group_check=True).then_inc(sem("y_done"), 1)

                @block.scalar
                def _(act):
                    for hd in range(SSM_H):
                        act.wait_ge(sem("less"), 2 * hd + 2)
                        act.activation(dl[:, hd % 2, :], dl[:, hd % 2, :], ACT.Exp).then_inc(sem("decay"), 1)

                @block.vector
                def _(dve):
                    def out_pair(b):
                        dve.wait_ge(sem("y_done"), 2 * b + 2)
                        dve.scalar_tensor_tensor(yb[:, b, :], yb[:, b, :], pr("d_skip", b, b + 1), PS[:, 4 + b % 4, 0:T],
                                                 ALU.mult, ALU.add).then_inc(sem("y"), 1)

                    def less(hd):
                        dve.wait_ge(sem("spread"), hd + 1)
                        if hd >= 2:
                            dve.wait_ge(sem("mt"), hd - 1)
                        dve.tensor_scalar(dl[:, hd % 2, 0:T], PS[:, hd % 2, 0:T], acs[:, 0, hd:hd + 1], 0.0, ALU.subtract, ALU.min
                                          ).then_inc(sem("less"), 1)
                        dve.tensor_scalar(dl[:, hd % 2, T:384], PS[:, hd % 2, P:T], acs[:, 1, hd:hd + 1], 0.0, ALU.subtract, ALU.min
                                          ).then_inc(sem("less"), 1)

                    less(0)
                    for hd in range(SSM_H):
                        if hd + 1 < SSM_H:
                            less(hd + 1)
                        dve.wait_ge(sem("decay"), hd + 1)
                        if hd >= 2:
                            dve.wait_ge(sem("y_done"), hd - 1)
                        dve.tensor_tensor(mt[:, hd % 2, :], dl[:, hd % 2, :], cbm[:, hd // 8, :], ALU.mult).then_inc(sem("mt"), 1)
                        if hd % 2 and hd > 1:
                            out_pair(hd // 2 - 1)
                    out_pair(SSM_H // 2 - 1)
            stages.end()

            sem = stages.begin()
            z = zx[:, 0:16, :]
            with nc.Block(no_gpsimd_drain=True) as block:
                @block.vector
                def _(dve):
                    link = Chain(dve, sem("dve"))
                    for q in range(4):
                        dve.tensor_tensor(yb[:, 4 * q:4 * q + 4, :], yb[:, 4 * q:4 * q + 4, :], z[:, 4 * q:4 * q + 4, :], ALU.mult
                                          ).then_inc(sem("gated"), 1)
                    for u in range(2):
                        low_a(dve, A_AT["hyqkv"][0] + u)
                    dve.wait_ge(sem("root"), 1)
                    link(dve.reciprocal(rstd[:, :], rstd[:, :]))
                    for b in range(16):
                        dve.scalar_tensor_tensor(yb[:, b, :], yb[:, b, :], pr("ssm_g", b, b + 1), rstd[:, :], ALU.mult, ALU.mult
                                                 ).then_inc(sem("y"), 1)

                @block.scalar
                def _(act):
                    for u in range(2):
                        high_a(act, A_AT["hyqkv"][0] + u)
                    for q in range(4):
                        act.wait_ge(sem("gated"), q + 1)
                        act.activation(z[:, 4 * q:4 * q + 4, :], yb[:, 4 * q:4 * q + 4, :], ACT.Square).then_inc(sem("squares"), 1)
                    act.wait_ge(sem("square_sums"), 1)
                    act.activation(rstd[:, :], PS[:, 0, 0:T], ACT.Sqrt, bias=eps, scale=1.0 / 2048).then_inc(sem("root"), 1)

                @block.tensor
                def _(pe):
                    for b in range(16):
                        pe.wait_ge(sem("squares"), b // 4 + 1)
                        mm = pe.matmul(PS[:, 0, 0:T], ones, z[:, b, :], start=(b == 0), stop=(b == 15))
                    mm.then_inc(sem("square_sums"), 1)
            stages.end()

    def attention(att):
        with ExitStack() as st:
            qkv = sb("qkv", [P, 40, T], st)
            acon = sb("acon", [48, 2, TWIDE], st)
            sem = stages.begin()
            a0, n = A_AT["hyqkv"]
            at0 = CON["bucket"][0]
            cst = ExitStack()
            bufC, acc = sb("bufC3", [P, KC, 256], cst), sb("acc3", [P, 2, 256], cst)
            with nc.Block(no_gpsimd_drain=True) as block:
                @block.gpsimd
                def _(pool):
                    c_loads(pool, sem, bufC[:, :, :], "hyqkv")

                @block.sync
                def _(sp):
                    sp.dma_start(acon[:, :, :].rearrange("p a b -> p (a b)"), con_dram[0:48, at0:at0 + 2 * TWIDE]).then_inc(sem("acon"), 16)
                    refill_a(sp, a0, n)
                    sp.wait_ge(sem("rows"), 1)
                    sp.dma_start(bias_rows, acon[:, 0, :]).then_inc(sem("rows_out"), 16)
                    sp.wait_ge(sem("rows_out"), 16)

                @block.tensor
                def _(pe):
                    pe.wait_ge(sem("acon"), 16)
                    pe.matmul(PS[0:48, 4, 0:TWIDE], pr("rel")[0:32, :], acon[0:32, 0, :], start=True, stop=True).then_inc(sem("rows_done"), 1)
                    proj_pe(pe, sem, a0, n, dst_token=(16, 17, 18, 19), c_units=C_UNITS["hyqkv"], acc=acc)

                @block.scalar
                def _(act):
                    proj_evac(act, 0, sem, a0, n, qkv)

                @block.vector
                def _(dve):
                    dve.wait_ge(sem("rows_done"), 1)
                    dve.tensor_tensor(acon[:, 0, :], PS[0:48, 4, 0:TWIDE], acon[:, 1, :], ALU.add).then_inc(sem("rows"), 1)
                    proj_evac(dve, 1, sem, a0, n, qkv, (bufC[:, :, :], acc, "hyqkv", 1))
                    mods_out(dve, sem, sem("c_summed"), 8, PS[:, 5, 128:144], 128, 144, [(2, 1, pr("norm_ffn2", 8, 16))])
            cst.close()
            stages.end()

            sem = stages.begin()
            NT = 4
            bias = spare_highA[:, :, :, :].rearrange("p a k c -> p (a k c)")[:, 0:NT * 3 * T].rearrange("p (n g c) -> p n g c", n=NT, g=3)
            s_ = spare_xh[:, :, :].rearrange("p k t -> p (k t)")[:, 0:6 * T].rearrange("p (a c) -> p a c", a=2)
            pt = xm[:, 0:2, :]
            pT = xm[:, 2:4, :]
            stat = sb("stat", [P, 2, 4], st)
            steps = [(hd, it) for hd in range(ATT_H) for it in range(2)]
            with nc.Block(no_gpsimd_drain=True) as block:
                @block.sync
                def _(sp):
                    for hd in range(ATT_H):
                        if hd >= NT:
                            sp.wait_ge(sem("biased"), 2 * (hd - NT) + 2)
                        src = bass.AP(tensor=bias_rows.tensor, offset=hd * TWIDE,
                                      ap=[[1, P], [ATT_H * TWIDE, 3], [1, T]])
                        sp.dma_start(bias[:, hd % NT, :, :], src).then_inc(sem(f"bias{hd % NT}"), 16)

                @block.tensor
                def _(pe):
                    def scores(n):
                        hd, it = steps[n]
                        W = P * (it + 1)
                        at = (hd % 2) * 64
                        if n >= 2:
                            pe.wait_ge(sem("biased"), n - 1)
                        for g in range(3):
                            mm = pe.matmul(PS[:, 2 * (n % 2) + g // 2, (g % 2) * T:(g % 2) * T + W],
                                           qkv[at:at + 64, 8 * g + hd // 2, it * P:(it + 1) * P],
                                           qkv[at:at + 64, 24 + hd // 2, 0:W], start=True, stop=True)
                        mm.then_inc(sem("scores"), 1)

                    def turn(n):
                        hd, it = steps[n]
                        pe.wait_ge(sem("normed"), n + 1)
                        if n >= 2:
                            pe.wait_ge(sem("pT"), n - 1)
                        for j in range(it + 1):
                            mm = pe.transpose(PS[:, 4 + n % 2, j * P:(j + 1) * P], pt[:, n % 2, j * P:(j + 1) * P], ident)
                        mm.then_inc(sem("turned"), 1)

                    def values(n):
                        hd, it = steps[n]
                        at = (hd % 2) * 64
                        pe.wait_ge(sem("pT"), n + 1)
                        if hd >= 4 and it == 0 and hd % 2 == 0:
                            pe.wait_ge(sem("att"), hd // 2 - 1)
                        for j in range(it + 1):
                            mm = pe.matmul(PS[at:at + 64, 6 + hd // 2 % 2, it * P:(it + 1) * P],
                                           qkv[:, 32 + 2 * (hd // 4) + j, (hd % 4) * 64:(hd % 4 + 1) * 64],
                                           pT[:, n % 2, j * P:(j + 1) * P], start=(j == 0), stop=(j == it))
                        mm.then_inc(sem("values"), 1)

                    scores(0)
                    for n in range(len(steps)):
                        if n + 1 < len(steps):
                            scores(n + 1)
                        turn(n)
                        if n >= 1:
                            values(n - 1)
                    values(len(steps) - 1)

                @block.scalar
                def _(act):
                    def turn_out(n):
                        W = P * (steps[n][1] + 1)
                        act.wait_ge(sem("turned"), n + 1)
                        if n >= 2:
                            act.wait_ge(sem("values"), n - 1)
                        act.copy(pT[:, n % 2, 0:W], PS[:, 4 + n % 2, 0:W]).then_inc(sem("pT"), 1)

                    def pair_out(b):
                        act.wait_ge(sem("values"), 4 * b + 4)
                        act.copy(att[:, b, :], PS[:, 6 + b % 2, 0:T]).then_inc(sem("att"), 1)

                    for n, (hd, it) in enumerate(steps):
                        W3 = 3 * P * (it + 1)
                        act.wait_ge(sem("max"), n + 1)
                        act.activation(s_[:, n % 2, 0:W3], s_[:, n % 2, 0:W3], ACT.Exp, bias=stat[:, n % 2, 0:1],
                                       accum_out=stat[:, n % 2, 1:2]).then_inc(sem("exps"), 1)
                        if n >= 1:
                            turn_out(n - 1)
                        if n >= 6 and n % 4 == 2:
                            pair_out(n // 4 - 1)
                    turn_out(len(steps) - 1)
                    pair_out(ATT_H // 2 - 1)

                @block.vector
                def _(dve):
                    link = Chain(dve, sem("dve"))

                    def biased(n):
                        hd, it = steps[n]
                        W = P * (it + 1)
                        dve.wait_ge(sem("scores"), n + 1)
                        dve.wait_ge(sem(f"bias{hd % NT}"), 16 * (hd // NT + 1))
                        sc = s_[:, n % 2, 0:3 * W].rearrange("p (g c) -> p g c", g=3)
                        b_ = bias[:, hd % NT, :, W - 1:W]
                        keys_forward = bass.AP(tensor=b_.tensor, offset=b_.offset, ap=[list(b_.ap[0]), list(b_.ap[1]), [-1, W]])
                        psum = PS[:, 2 * (n % 2):2 * (n % 2) + 2, :].rearrange("p a (g c) -> p (a g) c", g=2)[:, 0:3, 0:W]
                        dve.scalar_tensor_tensor(sc, psum, 0.125, keys_forward, ALU.mult, ALU.add
                                                 ).then_inc(sem("biased"), 1)
                        dve.wait_ge(sem("biased"), n + 1)
                        dve.tensor_reduce(stat[:, n % 2, 0:1], s_[:, n % 2, 0:3 * W], AX_X, ALU.max, negate=True).then_inc(sem("max"), 1)

                    def normed(n):
                        hd, it = steps[n]
                        W = P * (it + 1)
                        p = s_[:, n % 2, :]
                        dve.wait_ge(sem("exps"), n + 1)
                        if n >= 2:
                            dve.wait_ge(sem("turned"), n - 1)
                        link(dve.reciprocal(stat[:, n % 2, 2:3], stat[:, n % 2, 1:2]))
                        link(dve.tensor_tensor(pt[:, n % 2, 0:W], p[:, 0:W], p[:, W:2 * W], ALU.add))
                        link(dve.tensor_tensor(pt[:, n % 2, 0:W], pt[:, n % 2, 0:W], p[:, 2 * W:3 * W], ALU.add))
                        dve.tensor_scalar(pt[:, n % 2, 0:W], pt[:, n % 2, 0:W], stat[:, n % 2, 2:3], None, ALU.mult
                                          ).then_inc(sem("normed"), 1)

                    biased(0)
                    for n in range(len(steps)):
                        if n + 1 < len(steps):
                            biased(n + 1)
                        normed(n)
            stages.end()

    def conformer():
        with ExitStack() as st:
            ag = sb("ag", [P, 16, T], st)
            cvo, cvo_low = sb2("cvo", [P, KC, T], st)
            mean = sb("mean", [P, T], st)
            sem = stages.begin()
            a0, n = A_AT["cv1"]
            with nc.Block(no_gpsimd_drain=True) as block:
                @block.sync
                def _(sp):
                    refill_a(sp, a0, n)

                @block.tensor
                def _(pe):
                    proj_pe(pe, sem, a0, n)

                @block.scalar
                def _(act):
                    proj_evac(act, 0, sem, a0, n, ag)

                @block.vector
                def _(dve):
                    proj_evac(dve, 1, sem, a0, n, ag)
            stages.end()
            sem = stages.begin()
            u, sg = ag[:, 0:8, :], ag[:, 8:16, :]
            TAPS_N = 31
            with nc.Block(no_gpsimd_drain=True) as block:
                @block.vector
                def _(dve):
                    link = Chain(dve, sem("dve"))
                    dw = pr("dw").rearrange("p (b i) -> p b i", b=KC)
                    for b in range(KC):
                        dve.wait_ge(sem("gate"), b + 1)
                        i = dve.scalar_tensor_tensor(u[:, b, :], u[:, b, :], pr("b1", b, b + 1), sg[:, b, :], ALU.add, ALU.mult)
                        i.then_inc(sem("u"), 1)
                    for tp in range(TAPS_N):
                        for b in range(KC):
                            x, o = u[:, b, :], cvo[:, b, :]
                            w = dw[:, b, TAPS_N - 1 - tp:TAPS_N - tp]
                            if tp == 0:
                                dve.wait_ge(sem("u"), b + 1)
                                i = dve.tensor_scalar(o, x, w, pr("dw_b", b, b + 1), ALU.mult, ALU.add)
                            else:
                                dve.wait_ge(sem("conv"), KC * (tp - 1) + b + 1)
                                i = dve.scalar_tensor_tensor(o[:, tp:T], x[:, 0:T - tp], w, o[:, tp:T], ALU.mult, ALU.add)
                            i.then_inc(sem("conv"), 1)
                    for n in range(2):
                        low_a(dve, A_AT["cv2"][0] + n)
                    dve.wait_ge(sem("sums"), 1)
                    link(dve.tensor_scalar(mean[:, :], PS[:, 0, 0:T], 1.0 / D, None, ALU.mult))
                    dve.tensor_tensor(cvo[:, :, :], cvo[:, :, :], rep(mean[:, :], KC), ALU.subtract).then_inc(sem("centred"), 1)
                    dve.wait_ge(sem("root"), 1)
                    link(dve.reciprocal(rstd[:, :], rstd[:, :]))
                    dve.tensor_tensor(cvo[:, :, :], cvo[:, :, :], rep(rstd[:, :], KC), ALU.mult).then_inc(sem("normed"), 1)

                @block.scalar
                def _(act):
                    for b in range(KC):
                        act.activation(sg[:, b, :], sg[:, b, :], ACT.Sigmoid, bias=pr("b1", 8 + b, 9 + b)).then_inc(sem("gate"), 1)
                    for n in range(2):
                        high_a(act, A_AT["cv2"][0] + n)
                    act.wait_ge(sem("centred"), 1)
                    act.activation(sg, cvo[:, :, :], ACT.Square).then_inc(sem("squares"), 1)
                    act.wait_ge(sem("square_sums"), 1)
                    act.activation(rstd[:, :], PS[:, 1, 0:T], ACT.Sqrt, bias=eps, scale=1.0 / D).then_inc(sem("root"), 1)
                    act.wait_ge(sem("normed"), 1)
                    for b in range(KC):
                        act.activation(cvo[:, b, :], cvo[:, b, :], ACT.Silu, bias=pr("ln_b", b, b + 1), scale=pr("ln_g", b, b + 1)
                                       ).then_inc(sem("out"), 1)

                @block.tensor
                def _(pe):
                    for b in range(KC):
                        pe.wait_ge(sem("conv"), KC * (TAPS_N - 1) + b + 1)
                        mm = pe.matmul(PS[:, 0, 0:T], ones, cvo[:, b, :], start=(b == 0), stop=(b == KC - 1))
                    mm.then_inc(sem("sums"), 1)
                    pe.wait_ge(sem("squares"), 1)
                    for b in range(KC):
                        mm = pe.matmul(PS[:, 1, 0:T], ones, sg[:, b, :], start=(b == 0), stop=(b == KC - 1))
                    mm.then_inc(sem("square_sums"), 1)
            stages.end()
            out_proj("cv2", cvo, cvo_low, pr("b2"), 2)

    first_stage()
    norm_stage(0, 0, "win", small_ab)
    mixer_one()
    norm_stage(1, 0, "moe", small_route)
    moe()
    norm_h(pr("norm_out"), h)
    norm_stage(0, 1, "hyin", small_dt)
    mixer_two()
    norm_stage(1, 1, "ffn0")
    swiglu("ffn0", FF // 256, None, 1)
    norm_stage(0, 2, "cv1")
    conformer()
    norm_stage(1, 2, "ffn1")
    swiglu("ffn1", FF // 256, None, 2)
    norm_h(pr("final"), xm)
    ctx.close()


def put_a(dst, w):
    n = w.shape[1] // 256
    dst.reshape(n, P, KC, 256)[...] = w.reshape(KC, P, n, 256).transpose(2, 1, 0, 3)


def put_b(dst, w):
    n = w.shape[0] // 256
    dst.reshape(n, P, 2, D)[...] = w.reshape(n, 2, P, D).transpose(0, 2, 1, 3)


def put_paired(dst, a, b):
    for j, w in enumerate((a, b)):
        n = w.shape[1] // 256
        dst[j::2].reshape(n, P, KC, 256)[...] = w.reshape(KC, P, n, 256).transpose(2, 1, 0, 3)


def cols(v):
    return np.asarray(v).reshape(-1, P).T


def everywhere(v):
    return np.broadcast_to(np.asarray(v).reshape(1, -1), (P, np.asarray(v).size))


def layout(i):
    i = {k: np.asarray(v) for k, v in i.items()}
    w_in = i["w_in"][0]
    hy = i["hy_w_in_2"][0]
    eg = i["w_gate"][0].reshape(N_EXP, D, FF_EXP)
    eu = i["w_up"][0].reshape(N_EXP, D, FF_EXP)
    ed = i["w_down"][0].reshape(N_EXP, FF_EXP, D)
    wa = np.empty((A_ALL, P, UNIT), w_in.dtype)
    wb = np.empty((B_ALL, P, UNIT), w_in.dtype)
    in_a = lambda name, a=0, b=None: wa[A_AT[name][0] + a:A_AT[name][0] + (A_AT[name][1] if b is None else b)]
    in_b = lambda name, a=0, b=None: wb[B_AT[name][0] + a:B_AT[name][0] + (B_AT[name][1] if b is None else b)]
    put_a(in_a("mod"), i["mod_w"][0][:, :2048])
    wc = np.empty((C_ALL, P, UNIT), w_in.dtype)
    put_a(wc[0:16], i["mod_w"][0][:, 2048:])
    put_a(wc[16:40], i["ada_w_2"][0])
    put_a(wc[40:64], i["ada_w_2"][1])
    put_a(in_a("win", 0, 24), w_in[:, :6144])
    put_a(in_a("win", 24), w_in[:, 6152:])
    put_a(in_a("wout"), i["w_out"][0])
    for e in range(N_EXP):
        put_paired(in_a("moe", 4 * e, 4 * e + 4), eg[e], eu[e])
        put_b(in_b("moe", 2 * e, 2 * e + 2), ed[e])
    put_a(in_a("hyin"), hy[:, :5120])
    put_a(in_a("hyqkv"), hy[:, 5152:])
    put_b(in_b("hyout"), i["hy_w_out_2"][0])
    put_a(in_a("cv1"), i["cv_w_pw1_2"][0])
    put_a(in_a("cv2"), i["cv_w_pw2_2"][0])
    for l in range(2):
        put_paired(in_a(f"ffn{l}"), i["ffn_w_gate_2"][l], i["ffn_w_up_2"][l])
        put_b(in_b(f"ffn{l}"), i["ffn_w_down_2"][l])
    f = wa.dtype
    par = np.zeros((P, N_PAR), f)

    def put(name, v):
        at, w = PAR[name]
        v = np.asarray(v)
        par[:v.shape[0], at:at + w] = v.reshape(v.shape[0], w)

    put("c", cols(i["c"][0]))
    put("c2", cols(i["c_2"][0]))
    put("mod_b", cols(i["mod_b"][0]))
    put("ada_b", cols(i["ada_b_2"]))
    put("norm_mix", cols(i["norm_mix_w"][0]))
    put("norm_ffn", cols(i["norm_ffn_w"][0]))
    put("norm_out", cols(i["norm_out_w"]))
    put("norm_mix2", cols(i["norm_mix_g_2"]))
    put("norm_ffn2", cols(i["norm_ffn_g_2"]))
    put("final", cols(i["final_norm_g_2"]))
    put("gconv", i["gdn_conv_w"][0].reshape(4, 16, P).transpose(2, 1, 0))
    put("a_log", everywhere(i["gdn_a_log"][0]))
    put("dt_bias", everywhere(i["gdn_dt_bias"][0]))
    put("gdn_w", cols(i["gdn_norm_w"][0]))
    put("b_route", everywhere(np.concatenate([i["b_group"][0], i["b_router"][0].reshape(-1)])))
    put("w_route", np.concatenate([i["w_group"][0], i["w_router"][0]], 1).reshape(KC, P, 20).transpose(1, 0, 2))
    put("w_ab", w_in[:, 6144:6152].reshape(KC, P, 8).transpose(1, 0, 2))
    put("hconv", i["hy_conv_w_2"][0].reshape(4, 24, P).transpose(2, 1, 0))
    put("hconv_b", cols(i["hy_conv_b_2"][0]))
    put("w_dt", hy[:, 5120:5152].reshape(KC, P, SSM_H).transpose(1, 0, 2))
    put("dt_bias2", i["hy_dt_bias_2"][0][:, None])
    put("a_log2", i["hy_a_log_2"][0][:, None])
    put("d_skip", cols(np.repeat(i["hy_d_skip_2"][0], 64)))
    put("ssm_g", cols(i["hy_ssm_norm_g_2"][0]))
    put("rel", i["rel_table_2"])
    put("b1", cols(i["cv_b_pw1_2"][0]))
    put("dw", i["cv_w_dw_2"][0].reshape(31, 8, P).transpose(2, 1, 0))
    put("dw_b", cols(i["cv_b_dw_2"][0]))
    put("ln_g", cols(i["cv_ln_g_2"][0]))
    put("ln_b", cols(i["cv_ln_b_2"][0]))
    put("b2", cols(i["cv_b_pw2_2"][0]))
    x = np.ascontiguousarray(i["x"][0].T.reshape(KC, P, T).transpose(1, 0, 2))
    return {"wa": wa, "wb": wb, "wc": wc, "par": par, "con": constants(), "xT": x}


def kernel(**inputs):
    import concourse.bacc as _bacc
    from concourse.bass_utils import run_bass_kernel_spmd as _run

    nc = _bacc.Bacc("TRN2", target_bir_lowering=False, num_devices=1)
    arrays = layout(inputs)
    ins = [nc.dram_tensor(n, a.shape, mybir.dt.from_np(a.dtype), kind="ExternalInput").ap() for n, a in arrays.items()]
    out = nc.dram_tensor("out", (P, KC, T), F32, kind="ExternalOutput").ap()
    program(nc, ins, out)
    r = _run(nc, [arrays], core_ids=[0])
    y = r.results[0]["out"]
    return y.transpose(1, 0, 2).reshape(D, T).T.reshape(1, T, D)
```

```python
from contextlib import ExitStack

import numpy as np
import concourse.bass as bass
from concourse import mybir

F32 = mybir.dt.float32
F32R = mybir.dt.float32r
ACT = mybir.ActivationFunctionType
ALU = mybir.AluOpType
AX_X = mybir.AxisListType.X

P = 128
D = 1024
T = 256
KC = D // P
NA, NB = 8, 2
UNIT = 2048
HEADS = 4
EPS = 1e-6
N_EXP = 16
FF_EXP = 512
FF = 2816
SSM_H = 32
ATT_H = 16
BIG = -1e30
TWIDE = 384

A_UNITS = [("mod", 8), ("win", 32), ("wout", 4), ("moe", 4 * N_EXP), ("hyin", 20), ("hyqkv", 20), ("hyout", 12),
           ("ffn0", 2 * FF // 256), ("cv1", 8), ("cv2", 4), ("ffn1", 2 * FF // 256)]
B_UNITS = [("moe", 2 * N_EXP), ("ffn0", FF // 256), ("ffn1", FF // 256)]


C_UNITS = {"win": (0, 16), "moe": (16, 32), "hyin": (48, 8), "hyqkv": (56, 8)}
C_ALL = 64


SPLIT_FROM = 8


def starts(units):
    at, n = {}, 0
    for name, k in units:
        at[name] = (n, k)
        n += k
    return at, n


A_AT, A_ALL = starts(A_UNITS)
B_AT, B_ALL = starts(B_UNITS)

PAR_WIDTHS = [("c", 8), ("c2", 8), ("mod_b", 48), ("ada_b", 96), ("norm_mix", 8), ("norm_ffn", 8), ("norm_out", 8),
              ("norm_mix2", 16), ("norm_ffn2", 16), ("final", 8), ("gconv", 64), ("a_log", 4),
              ("dt_bias", 4), ("gdn_w", 2), ("b_route", 20), ("w_route", 160), ("w_ab", 64),
              ("hconv", 96), ("hconv_b", 24), ("w_dt", 256), ("dt_bias2", 1), ("a_log2", 1), ("d_skip", 16),
              ("ssm_g", 16), ("rel", 48), ("b1", 16), ("dw", 248), ("dw_b", 8), ("ln_g", 8), ("ln_b", 8), ("b2", 8)]
PAR = {}
N_PAR = 0
for _name, _w in PAR_WIDTHS:
    PAR[_name] = (N_PAR, _w)
    N_PAR += _w

CON_WIDTHS = [("ident", 128), ("ones", 128), ("upto", 512), ("eps", 1),
              ("cos", 256), ("sin", 256), ("turn", 128), ("ret", 4 * 384),
              ("strict", 128), ("levels", 7 * 128),
              ("bucket", TWIDE), ("band", TWIDE)]
CON = {}
N_CON = 0
for _name, _w in CON_WIDTHS:
    CON[_name] = (N_CON, _w)
    N_CON += _w
N_KEPT = CON["cos"][0]


def constants():
    c = np.zeros((P, N_CON), np.float32)

    def put(name, a):
        at, w = CON[name]
        a = np.asarray(a, np.float32)
        c[:a.shape[0], at:at + w] = a.reshape(a.shape[0], w)

    p = np.arange(P)
    i = np.arange(T)
    put("ident", np.eye(P))
    put("ones", np.ones((P, P)))
    put("upto", np.stack([p[:, None] + P * t <= i[None, :] for t in range(2)], 1))
    put("eps", np.full((P, 1), EPS))
    half = 64
    inv = (1.0 / (np.float32(10000.0) ** (np.arange(half, dtype=np.float32) / np.float32(half)))).astype(np.float32)
    ang = (np.arange(T, dtype=np.float32)[:, None] * inv[None, :]).astype(np.float32)
    put("cos", np.tile(np.cos(ang).T, (2, 1)))
    put("sin", np.tile(np.sin(ang).T, (2, 1)))
    turn = np.zeros((P, P))
    for m in range(half):
        turn[m + half, m] = -1.0
        turn[m, m + half] = 1.0
    put("turn", turn)
    ret = np.zeros((P, HEADS, 384))
    for h in range(HEADS):
        lg = np.log(1.0 - 2.0 ** (-5.0 - h))
        rel = i[None, :] - p[:, None]
        dec = np.where(rel >= 0, np.exp(np.maximum(rel, 0) * lg), 0.0) * 128 ** -0.5
        ret[:, h, :T] = dec
        ret[:, h, T:] = dec[:, :P]
    put("ret", ret)
    put("strict", p[:, None] < p[None, :])
    lv = np.zeros((P, 7, P))
    for n in range(7):
        s = 1 << n
        lv[:, n] = (p[:, None] // (2 * s) == p[None, :] // (2 * s)) & ((p[:, None] // s) % 2 == 0) & ((p[None, :] // s) % 2 == 1)
    put("levels", lv)
    dist = np.arange(TWIDE) - 127
    n = np.maximum(dist, 1).astype(np.float32)
    large = 16 + np.log(n / np.float32(16)) / np.float32(np.log(2048 / 16)) * 16
    large = np.minimum(large.astype(np.int32), 31)
    bk = np.where(dist < 16, np.maximum(dist, 0), large)
    put("bucket", (bk[None, :] == np.arange(32)[:, None]) & (dist >= 0)[None, :])
    band = np.zeros((48, TWIDE))
    for g, dil in enumerate((1, 4, 16)):
        ok = (dist >= 0) & (dist % dil == 0) & (dist // dil <= 128)
        band[g * 16:(g + 1) * 16] = np.where(ok, 0.0, BIG)[None, :]
    put("band", band)
    return c


def rep(ap, n):
    return bass.AP(tensor=ap.tensor, offset=ap.offset, ap=[list(ap.ap[0]), [0, n]] + [list(x) for x in ap.ap[1:]])


def wide(ap, m):
    return bass.AP(tensor=ap.tensor, offset=ap.offset, ap=[list(x) for x in ap.ap] + [[0, m]])


class Chain:

    def __init__(self, engine, semaphore):
        self.engine, self.semaphore, self.count = engine, semaphore, 0

    def __call__(self, instruction):
        self.count += 1
        instruction.then_inc(self.semaphore, 1)
        self.engine.wait_ge(self.semaphore, self.count)


class Stages:

    SIZE = 66

    def __init__(self, nc):
        self.nc, self.k = nc, 0
        self.pools = [[nc.alloc_semaphore(f"stage{q}_{i}") for i in range(self.SIZE)] for q in range(2)]

    def begin(self):
        taken = {}
        pool = self.pools[self.k % 2]

        def sem(name):
            if name not in taken:
                taken[name] = pool[len(taken)]
            return taken[name]

        return sem

    def end(self):
        pool = self.pools[self.k % 2]
        self.nc.gpsimd.sem_clear(range(pool[0].num, pool[-1].num + 1))
        self.k += 1


def program(nc, ins, out):
    wa, wb, wc, par_dram, con_dram, x_dram = ins
    bias_rows = nc.dram_tensor("bias_rows", (48, TWIDE), F32, kind="Internal").ap()
    ctx = ExitStack()

    def sb(name, shape, on=ctx):
        return on.enter_context(nc.sbuf_tensor(name + "_sb", shape, F32))

    def sb2(name, shape, on=ctx):
        with nc.sbuf_tensor(name + "_sb", shape, F32) as plain:
            pass
        return plain, on.enter_context(nc.sbuf_tensor(name + "_r_sb", shape, F32R))

    ringA, lowA = sb2("ringA", [P, NA, KC, 256])
    ringB, lowB = sb2("ringB", [P, NB, 2, D])
    h = sb("h", [P, KC, T])
    xm, xl = sb2("xm", [P, KC, T])
    par = sb("par", [P, N_PAR])
    con = sb("con", [P, N_KEPT])
    mods3 = sb("mods", [P, 3, 48])
    normw3 = sb("normw", [P, 3, 2, KC])
    cs = sb("cs", [P, 2, KC])
    rstd = sb("rstd", [P, T])
    spare_xh, xh = sb2("xh", [P, KC, T])
    spare_highA, highA = sb2("highA", [P, 2, KC, 256])
    PS = ctx.enter_context(nc.psum_tensor("PS", [P, 8, 512], F32))

    a_full = [nc.alloc_semaphore(f"a_full{i}") for i in range(NA)]
    b_full = [nc.alloc_semaphore(f"b_full{i}") for i in range(NB)]
    c_full = nc.alloc_semaphore("c_full")
    a_high = nc.alloc_semaphore("a_high")
    a_low = nc.alloc_semaphore("a_low")
    b_high = nc.alloc_semaphore("b_high")
    b_low = nc.alloc_semaphore("b_low")
    a_used = nc.alloc_semaphore("a_used")
    b_used = nc.alloc_semaphore("b_used")
    stages = Stages(nc)

    def pr(name, a=0, b=None):
        at, w = PAR[name]
        return par[:, at + a:at + (w if b is None else b)]

    def cn(name):
        at, w = CON[name]
        return con[:, at:at + w]

    ident, ones, eps = cn("ident"), cn("ones"), cn("eps")
    upto = cn("upto").rearrange("p (t i) -> p t i", t=2)

    def load_a(sp, slot, n):
        sp.dma_start(ringA[:, slot].rearrange("p k c -> p (k c)"), wa[n]).then_inc(a_full[slot], 16)

    def load_b(sp, slot, n):
        sp.dma_start(ringB[:, slot].rearrange("p k c -> p (k c)"), wb[n]).then_inc(b_full[slot], 16)

    def refill_a(sp, first, n):
        n = min(n, A_ALL - NA - first)
        turns = n // NA
        if turns > 1:
            with sp.Fori(0, turns) as i:
                for j in range(NA):
                    sp.wait_ge(a_used, i * NA + (first + j + 1))
                    sp.dma_start(ringA[:, (first + j) % NA].rearrange("p k c -> p (k c)"),
                                 wa[bass.ds(i * NA + (first + j + NA), 1)].rearrange("a p c -> p (a c)")
                                 ).then_inc(a_full[(first + j) % NA], 16)
        else:
            turns = 0
        for m in range(first + turns * NA, first + n):
            sp.wait_ge(a_used, m + 1)
            load_a(sp, m % NA, m + NA)

    def refill_ab(sp, a0, b0, steps):
        def step(s):
            for j in (0, 1):
                m = a0 + 2 * s + j
                if m + NA < A_ALL:
                    sp.wait_ge(a_used, m + 1)
                    load_a(sp, m % NA, m + NA)
            m = b0 + s - 1
            if s > 0 and m + NB < B_ALL:
                sp.wait_ge(b_used, m + 1)
                load_b(sp, m % NB, m + NB)

        last = min(steps, (A_ALL - NA - a0) // 2, B_ALL - NB - b0)
        turns = (last - 4) // 4
        for s in range(4):
            step(s)
        if turns > 1:
            with sp.Fori(1, turns + 1) as i:
                for s in range(4):
                    loop_step(sp, a0, b0, s, i)
            done = 4 + 4 * turns
        else:
            done = 4
        for s in range(done, steps):
            step(s)
        m = b0 + steps - 1
        if m + NB < B_ALL:
            sp.wait_ge(b_used, m + 1)
            load_b(sp, m % NB, m + NB)

    def loop_step(sp, a0, b0, s, i):
        for j in (0, 1):
            m = a0 + 2 * s + j
            sp.wait_ge(a_used, i * 8 + (m + 1))
            sp.dma_start(ringA[:, m % NA].rearrange("p k c -> p (k c)"),
                         wa[bass.ds(i * 8 + (m + NA), 1)].rearrange("a p c -> p (a c)")).then_inc(a_full[m % NA], 16)
        m = b0 + s - 1
        sp.wait_ge(b_used, i * 4 + (m + 1))
        sp.dma_start(ringB[:, m % NB].rearrange("p k c -> p (k c)"),
                     wb[bass.ds(i * 4 + (m + NB), 1)].rearrange("a p c -> p (a c)")).then_inc(b_full[m % NB], 16)

    plus = lambda v, i, per: v if i is None else i * per + v

    def high_a(act, n, i=None):
        act.wait_ge(a_full[n % NA], plus(16 * (n // NA + 1), i, 16))
        act.wait_ge(a_used, plus(n - 1, i, NA))
        act.copy(highA[:, n % 2, :, :], ringA[:, n % NA, :, :]).then_inc(a_high, 1)

    def low_a(dve, n, i=None):
        dve.wait_ge(a_high, plus(n + 1 - SPLIT_FROM, i, NA))
        dve.tensor_tensor(lowA[:, n % NA, :, :], ringA[:, n % NA, :, :], highA[:, n % 2, :, :].bitcast(F32), ALU.subtract
                          ).then_inc(a_low, 1)

    def split_a_wait(pe, n, i=None):
        pe.wait_ge(a_low, plus(n + 1 - SPLIT_FROM, i, NA))

    def high_b(act, highB, n, i=None):
        act.wait_ge(b_full[n % NB], plus(16 * (n // NB + 1), i, 64 // NB))
        if n >= 2:
            act.wait_ge(b_used, plus(n - 1, i, 4))
        act.copy(highB[:, n % 2, :, :], ringB[:, n % NB, :, :]).then_inc(b_high, 1)

    def low_b(dve, highB, n, i=None):
        dve.wait_ge(b_high, plus(n + 1, i, 4))
        dve.tensor_tensor(lowB[:, n % NB, :, :], ringB[:, n % NB, :, :], highB[:, n % 2, :, :].bitcast(F32), ALU.subtract
                          ).then_inc(b_low, 1)

    def high_x(act, sem, src, high, parts):
        n = src.shape[1] // parts
        for q in range(parts):
            act.copy(high[:, q * n:(q + 1) * n, :], src[:, q * n:(q + 1) * n, :]).then_inc(sem("x_high"), 1)

    def low_x(dve, sem, src, high, low, parts):
        n = src.shape[1] // parts
        for q in range(parts):
            dve.wait_ge(sem("x_high"), q + 1)
            dve.tensor_tensor(low[:, q * n:(q + 1) * n, :], src[:, q * n:(q + 1) * n, :], high[:, q * n:(q + 1) * n, :].bitcast(F32),
                              ALU.subtract).then_inc(sem("x_low"), 1)

    def mm3(pe, psum, high, low, moving_high, moving_low, start, stop, **kw):
        pe.matmul(psum, high, moving_high, start=start, stop=False, **kw)
        pe.matmul(psum, high, moving_low, start=False, stop=False, **kw)
        return pe.matmul(psum, low, moving_high, start=False, stop=stop, **kw)

    def update_h(dve, sem, update):
        bank, layer, col, bias = update
        for b in range(KC):
            psum = PS[:, bank + b // 2, (b % 2) * T:(b % 2 + 1) * T]
            gate = mods3[:, layer, col + b:col + b + 1]
            if bias is None:
                dve.scalar_tensor_tensor(h[:, b, :], psum, gate, h[:, b, :], ALU.mult, ALU.add).then_inc(sem("h"), 1)
            else:
                dve.tensor_scalar(xm[:, b, :], psum, bias[:, b:b + 1], gate, ALU.add, ALU.mult).then_inc(sem("biased"), 1)
                dve.wait_ge(sem("biased"), b + 1)
                dve.tensor_tensor(h[:, b, :], h[:, b, :], xm[:, b, :], ALU.add).then_inc(sem("h"), 1)

    def squares_act(act, sem, squares, update):
        for b in range(KC):
            if update is not None:
                act.wait_ge(sem("h"), b + 1)
            act.activation(squares[:, b, :], h[:, b, :], ACT.Square).then_inc(sem("squares"), 1)

    def sums_bank(update):
        return 5 if update is None or update[0] == 0 else 0

    def rms_pe(pe, sem, squares, psum):
        for b in range(KC):
            pe.wait_ge(sem("squares"), b + 1)
            mm = pe.matmul(psum, ones, squares[:, b, :], start=(b == 0), stop=(b == KC - 1))
        mm.then_inc(sem("square_sums"), 1)

    def proj_pe(pe, sem, first, units, dst_token=(), low_src=xl, c_units=None, acc=None):
        def unit(u, j, token, i=None):
            if i is not None or u >= 4:
                done = (sem("evac_act"), sem("evac_dve"))[j % 2]
                n = (j - 4) // 2 + 1
                pe.wait_ge(done, plus(n, i, NA // 2))
            split_a_wait(pe, first + j, i)
            high, low = highA[:, (first + j) % 2], lowA[:, (first + j) % NA]
            bank = PS[:, j % 4, :]
            for b in range(2):
                at = slice(b * P, (b + 1) * P)
                for k in range(KC):
                    if token:
                        mm = mm3(pe, bank[:, b * 256:(b + 1) * 256], xh[:, k, at], low_src[:, k, at], high[:, k, :], low[:, k, :],
                                 start=(k == 0), stop=(k == KC - 1))
                    else:
                        mm = mm3(pe, bank[:, b * 256:(b + 1) * 256], high[:, k, at], low[:, k, at], xh[:, k, :], low_src[:, k, :],
                                 start=(k == 0), stop=(k == KC - 1))
            mm.then_inc(a_used, 1)
            if c_units and j % 2 and (i is not None or 2 <= u <= 2 * c_units[1] + 1):
                c_sum(pe, sem, acc, 16 + 2 * c_units[0] + (j - 3), (j - 3) // 2, i, NA // 2)

        turns = (units - NA) // NA
        for u in range(min(NA, units)):
            unit(u, u, u in dst_token)
        if turns > 0:
            with pe.Fori(1, turns + 1) as i:
                for j in range(NA):
                    unit(None, j, False, i)
        for u in range(NA + max(turns, 0) * NA, units):
            unit(u, u, u in dst_token)
        if c_units and units == 2 * c_units[1]:
            c_sum(pe, sem, acc, 16 + 2 * c_units[0] + 2 * (c_units[1] - 1), c_units[1] - 1)

    def proj_evac(eng, which, sem, first, units, dst, c=None, second=True):
        name = ("evac_act", "evac_dve")[which]
        copy, part = (eng.tensor_copy, low_a) if which else (eng.copy, high_a)
        turns = units // NA
        if which and second:
            low_a(eng, first + 1)

        def one(j, i=None, ahead=True):
            if ahead:
                part(eng, first + j + 2, i)
            if j % 2 == which:
                eng.wait_ge(a_used, plus(first + j + 1, i, NA))
                to = dst[:, 2 * j:2 * j + 2, :] if i is None else dst[:, bass.ds(i * (2 * NA) + 2 * j, 2), :]
                copy(to, PS[:, j % 4, :].rearrange("p (b t) -> p b t", b=2)).then_inc(sem(name), 1)
            elif c and (i is not None or j < 2 * C_UNITS[c[2]][1]):
                c_scale(eng, sem, c[0], c[1], c[3], C_UNITS[c[2]][0], j // 2, i, NA // 2)

        last = turns - 1 if units % NA < 2 else turns
        if last > 1:
            for j in range(NA):
                one(j)
            with eng.Fori(1, last) as i:
                for j in range(NA):
                    one(j, i)
            done = last * NA
        else:
            done = 0
        for j in range(done, units):
            one(j, None, j + 2 < units)

    mods_flat = mods3[:, :, :].rearrange("p l c -> p (l c)")

    def mods_out(dve, sem, counter, count, src, lo, hi, scales):
        dve.wait_ge(counter, count)
        dve.tensor_tensor(mods_flat[:, lo:hi], src, par[:, PAR["mod_b"][0] + lo:PAR["mod_b"][0] + hi], ALU.add).then_inc(sem("mods"), 1)
        dve.wait_ge(sem("mods"), 1)
        for layer, q, w in scales:
            at = 8 + 24 * q
            dve.scalar_tensor_tensor(normw3[:, layer, q, :], mods3[:, layer, at:at + 8], 1.0, w, ALU.add, ALU.mult
                                     ).then_inc(sem("normw"), 1)

    def c_loads(pool, sem, bufC, name):
        first, n = C_UNITS[name]
        pool.dma_start(bufC.rearrange("p k c -> p (k c)"), wc[first]).then_inc(c_full, 16)
        with pool.Fori(1, n) as i:
            pool.wait_ge(sem("c_used"), i)
            pool.dma_start(bufC.rearrange("p k c -> p (k c)"),
                           wc[bass.ds(i + first, 1)].rearrange("a p c -> p (a c)")).then_inc(c_full, 16)

    def c_scale(dve, sem, bufC, acc, c_of, first, m, i=None, per=0):
        dve.wait_ge(c_full, plus(16 * (first + m + 1), i, 16 * per))
        scale_rows(dve, sem, bufC, acc, c_of, m, i, per)

    def scale_rows(dve, sem, buf, acc, c_of, m, i=None, per=0):
        if i is not None or m >= 2:
            dve.wait_ge(sem("c_summed"), plus(m - 1, i, per))
        for k in range(KC):
            col = cs[:, c_of, k:k + 1]
            if k == 0:
                ins_ = dve.tensor_scalar(acc[:, m % 2, :], buf[:, k, :], col, None, ALU.mult)
            else:
                dve.wait_ge(sem("c_block"), plus((KC - 1) * m + k, i, (KC - 1) * per))
                ins_ = dve.scalar_tensor_tensor(acc[:, m % 2, :], buf[:, k, :], col, acc[:, m % 2, :], ALU.mult, ALU.add)
            if k < KC - 1:
                ins_.then_inc(sem("c_block"), 1)
        ins_.then_inc(sem("c_used"), 1)

    def c_sum(pe, sem, acc, col, m, i=None, per=0, bank=5, fixed=False, used=None):
        pe.wait_ge(sem("c_used"), plus(m + 1, i, per))
        for b in range(2):
            if b and used is not None:
                mm.then_inc(used, 1)
            to = PS[:, bank, col + b:col + b + 1] if i is None or fixed else PS[:, bank, bass.ds(i * (2 * per) + (col + b), 1)]
            mm = pe.matmul(to, acc[:, m % 2, b * P:(b + 1) * P], ones[:, 0:1], start=True, stop=True)
        mm.then_inc(sem("c_summed"), 1)

    def first_stage():
        sem = stages.begin()
        a0, n = A_AT["mod"]
        acc_ = ExitStack()
        acc = sb("acc0", [P, 2, 256], acc_)
        with nc.Block(no_gpsimd_drain=True) as block:
            @block.sync
            def _(sp):
                sp.dma_start(par[:, :], par_dram).then_inc(sem("par"), 16)
                sp.dma_start(h[:, :, :], x_dram).then_inc(sem("x"), 16)
                sp.dma_start(con[:, :], con_dram[:, 0:N_KEPT]).then_inc(sem("con"), 16)
                for m in range(NA):
                    load_a(sp, m, m)
                refill_a(sp, a0, n)
                for m in range(NB):
                    load_b(sp, m, m)
                sp.wait_ge(sem("con"), 16)
                sp.wait_ge(sem("x"), 16)

            @block.scalar
            def _(act):
                act.wait_ge(sem("par"), 16)
                act.activation(cs[:, 0, :], pr("c"), ACT.Silu).then_inc(sem("cs"), 1)
                act.activation(cs[:, 1, :], pr("c2"), ACT.Silu).then_inc(sem("cs"), 1)

            @block.tensor
            def _(pe):
                pe.wait_ge(sem("con"), 16)
                for m in range(n):
                    c_sum(pe, sem, acc, 2 * m, m, used=a_used)

            @block.vector
            def _(dve):
                dve.wait_ge(sem("cs"), 2)
                for m in range(n):
                    dve.wait_ge(a_full[(a0 + m) % NA], 16)
                    scale_rows(dve, sem, ringA[:, (a0 + m) % NA, :, :], acc, 0, m)
                mods_out(dve, sem, sem("c_summed"), n, PS[:, 5, 0:16], 0, 16, [(0, 0, pr("norm_mix"))])
        acc_.close()
        stages.end()

    def norm_stage(which, layer, following, small=None, update=None):
        first = A_AT[following][0]
        sem = stages.begin()
        with ExitStack() as st:
            squares = sb(f"squares{stages.k}", [P, KC, T], st)
            with nc.Block(no_gpsimd_drain=True) as block:
                @block.scalar
                def _(act):
                    high_a(act, first)
                    squares_act(act, sem, squares, update)
                    act.wait_ge(sem("square_sums"), 1)
                    act.activation(rstd[:, :], PS[:, sums_bank(update), 0:T], ACT.Sqrt, bias=eps, scale=1.0 / D).then_inc(sem("root"), 1)
                    high_a(act, first + 1)
                    for q in range(2):
                        act.wait_ge(sem("xm"), 4 * q + 4)
                        act.copy(xh[:, 4 * q:4 * q + 4, :], xm[:, 4 * q:4 * q + 4, :]).then_inc(sem("x_high"), 1)

                @block.tensor
                def _(pe):
                    rms_pe(pe, sem, squares, PS[:, sums_bank(update), 0:T])
                    if small is not None:
                        pe.wait_ge(sem("xm"), KC)
                        small(pe).then_inc(sem("small"), 1)

                @block.vector
                def _(dve):
                    link = Chain(dve, sem("dve"))
                    if update is not None:
                        update_h(dve, sem, update)
                    low_a(dve, first)
                    dve.wait_ge(sem("root"), 1)
                    link(dve.reciprocal(rstd[:, :], rstd[:, :]))
                    link(dve.tensor_tensor(squares[:, :, :], h[:, :, :], rep(rstd[:, :], KC), ALU.mult))
                    for k in range(KC):
                        dve.tensor_scalar(xm[:, k, :], squares[:, k, :], normw3[:, layer, which, k:k + 1],
                                          mods3[:, layer, 24 * which + k:24 * which + k + 1], ALU.mult, ALU.add
                                          ).then_inc(sem("xm"), 1)
                    if small is not None:
                        dve.wait_ge(sem("small"), 1)
                    low_x(dve, sem, xm, xh, xl, 2)
        stages.end()

    def norm_h(w, dst, update):
        sem = stages.begin()
        with ExitStack() as st:
            squares = sb(f"squares{stages.k}", [P, KC, T], st)
            with nc.Block(no_gpsimd_drain=True) as block:
                @block.scalar
                def _(act):
                    squares_act(act, sem, squares, update)
                    act.wait_ge(sem("square_sums"), 1)
                    act.activation(rstd[:, :], PS[:, sums_bank(update), 0:T], ACT.Sqrt, bias=eps, scale=1.0 / D).then_inc(sem("root"), 1)

                @block.tensor
                def _(pe):
                    rms_pe(pe, sem, squares, PS[:, sums_bank(update), 0:T])

                @block.vector
                def _(dve):
                    link = Chain(dve, sem("dve"))
                    if update is not None:
                        update_h(dve, sem, update)
                    dve.wait_ge(sem("root"), 1)
                    link(dve.reciprocal(rstd[:, :], rstd[:, :]))
                    link(dve.tensor_tensor(squares[:, :, :], h[:, :, :], rep(rstd[:, :], KC), ALU.mult))
                    for k in range(KC):
                        dve.tensor_scalar(dst[:, k, :], squares[:, k, :], w[:, k:k + 1], None, ALU.mult
                                          ).then_inc(sem("normed"), 1)

                if dst is not h:
                    @block.sync
                    def _(sp):
                        sp.wait_ge(sem("normed"), KC)
                        sp.dma_start(out, dst[:, :, :]).then_inc(sem("stored"), 16)
                        sp.wait_ge(sem("stored"), 16)
        stages.end()

    def conv_pe(pe, sem, diag, src, blocks, bank0):
        for b in range(blocks):
            pe.wait_ge(sem("diag"), b + 1)
            for tp in range(4):
                at = (b % 2) * T
                mm = pe.matmul(PS[:, bank0 + b // 2, at + tp:at + T], diag[:, b % 2, tp, :], src(b)[:, 0:T - tp],
                               start=(tp == 0 and b % 2 == 0), stop=(tp == 3), skip_group_check=True)
            mm.then_inc(sem("block_conved"), 1)

    def conv_act(act, sem, diag, tap_of, blocks, bank0, dst, bias_of):
        def pair_out(p):
            act.wait_ge(sem("block_conved"), 2 * p + 2)
            for b in (2 * p, 2 * p + 1):
                act.activation(dst(b), PS[:, bank0 + p, (b % 2) * T:(b % 2 + 1) * T], ACT.Silu, bias=bias_of(b)
                               ).then_inc(sem("block_out"), 1)

        for b in range(blocks):
            if b >= 2:
                act.wait_ge(sem("block_conved"), b - 1)
            for tp in range(4):
                i = act.activation(diag[:, b % 2, tp, :], ident, ACT.Copy, scale=tap_of(b, tp))
            i.then_inc(sem("diag"), 1)
            if b % 2 and b >= 3:
                pair_out(b // 2 - 1)
        pair_out(blocks // 2 - 1)

    def small_ab(pe):
        w_ab = pr("w_ab").rearrange("p (k c) -> p k c", k=KC)
        for t in range(2):
            for k in range(KC):
                mm = pe.matmul(PS[:, 4, t * 8:t * 8 + 8], xm[:, k, t * P:(t + 1) * P], w_ab[:, k, :],
                               start=(k == 0), stop=(k == KC - 1))
        return mm

    def small_dt(pe):
        w_dt = pr("w_dt").rearrange("p (k c) -> p k c", k=KC)
        for k in range(KC):
            mm = pe.matmul(PS[0:SSM_H, 4, 0:T], w_dt[:, k, :], xm[:, k, :], start=(k == 0), stop=(k == KC - 1))
        return mm

    def small_route(pe):
        wr = pr("w_route").rearrange("p (k c) -> p k c", k=KC)
        for t in range(2):
            for k in range(KC):
                mm = pe.matmul(PS[:, 4, t * 20:(t + 1) * 20], xm[:, k, t * P:(t + 1) * P], wr[:, k, :],
                               start=(k == 0), stop=(k == KC - 1))
        return mm

    def mixer_one():
        with ExitStack() as st:
            proj = sb("proj", [P, 64, T], st)
            gab = sb("gab", [P, 2, 8], st)
            sem = stages.begin()
            a0, n = A_AT["win"]
            cst = ExitStack()
            bufC, acc = sb("bufC1", [P, KC, 256], cst), sb("acc1", [P, 2, 256], cst)
            with nc.Block(no_gpsimd_drain=True) as block:
                @block.gpsimd
                def _(pool):
                    c_loads(pool, sem, bufC[:, :, :], "win")

                @block.sync
                def _(sp):
                    refill_a(sp, a0, n)

                @block.tensor
                def _(pe):
                    proj_pe(pe, sem, a0, n, dst_token=(4, 5, 6, 7), c_units=C_UNITS["win"], acc=acc)

                @block.scalar
                def _(act):
                    proj_evac(act, 0, sem, a0, n, proj)

                @block.vector
                def _(dve):
                    dve.tensor_copy(gab[:, :, :], PS[:, 4, 0:16].rearrange("p (t c) -> p t c", t=2)).then_inc(sem("gab"), 1)
                    proj_evac(dve, 1, sem, a0, n, proj, (bufC[:, :, :], acc, "win", 0))
                    mods_out(dve, sem, sem("c_summed"), 16, PS[:, 5, 16:48], 16, 48, [(0, 1, pr("norm_ffn"))])
            cst.close()
            stages.end()
            mix, mix_low = sb2("mix", [P, KC, T], st)
            retention(proj, mix)
            delta_rule(proj, gab, mix)
            out_proj("wout", mix, mix_low)

    def out_proj(name, src, low_src):
        sem = stages.begin()
        a0, n = A_AT[name]
        with nc.Block(no_gpsimd_drain=True) as block:
            @block.sync
            def _(sp):
                refill_a(sp, a0, n)

            @block.tensor
            def _(pe):
                pe.wait_ge(sem("x_low"), 2)
                proj_pe(pe, sem, a0, n, low_src=low_src)

            @block.scalar
            def _(act):
                high_x(act, sem, src, xh, 2)
                for u in range(2, n):
                    high_a(act, a0 + u)

            @block.vector
            def _(dve):
                low_x(dve, sem, src, xh, low_src, 2)
                for u in range(2, n):
                    low_a(dve, a0 + u)
        stages.end()

    def retention(proj, mix):
        sem = stages.begin()
        with ExitStack() as st:
            at0 = CON["cos"][0]
            n_rc = CON["strict"][0] - at0
            rcon = spare_highA[:, :, :, :].rearrange("p a k c -> p (a k c)")[:, 0:n_rc]

            def rc(name):
                at, w = CON[name]
                return rcon[:, at - at0:at - at0 + w]

            cos, sin, turn = rc("cos"), rc("sin"), rc("turn")
            ret = rc("ret").rearrange("p (h i) -> p h i", h=HEADS)
            turned = xm
            qk = proj[:, 0:8, :]
            S = proj[:, 0:6, :].rearrange("p a b -> p (a b)").rearrange("p (h i) -> p h i", h=HEADS)
            with nc.Block(no_gpsimd_drain=True) as block:
                @block.sync
                def _(sp):
                    n_rope = CON["ret"][0] - at0
                    sp.dma_start(rcon[:, 0:n_rope], con_dram[:, at0:CON["ret"][0]]).then_inc(sem("rope_con"), 16)
                    sp.dma_start(rcon[:, n_rope:], con_dram[:, CON["ret"][0]:CON["strict"][0]]).then_inc(sem("ret_con"), 16)

                @block.tensor
                def _(pe):
                    pe.wait_ge(sem("rope_con"), 16)
                    for b in range(8):
                        mm = pe.matmul(PS[:, b // 2, (b % 2) * T:(b % 2 + 1) * T], turn, qk[:, b, :], start=True, stop=True)
                    mm.then_inc(sem("halves_swapped"), 1)
                    pe.wait_ge(sem("roped"), 1)
                    for hd in range(HEADS):
                        q, k = qk[:, hd, :], qk[:, 4 + hd, :]
                        pe.matmul(PS[:, 4 + hd, 0:T], k[:, 0:P], q, start=True, stop=True)
                        pe.matmul(PS[:, 4 + hd, T:384], k[:, P:T], q[:, P:T], start=True, stop=True
                                  ).then_inc(sem("scores"), 1)
                    for hd in range(HEADS):
                        pe.wait_ge(sem("decayed"), hd + 1)
                        for b in range(2):
                            o = PS[:, hd, b * T:(b + 1) * T]
                            v = [proj[:, 8 + 2 * hd + t, b * P:(b + 1) * P] for t in range(2)]
                            pe.matmul(o, v[0], S[:, hd, 0:T], start=True, stop=False, skip_group_check=True)
                            mm = pe.matmul(o[:, P:T], v[1], S[:, hd, T:384], start=False, stop=True, skip_group_check=True)
                        mm.then_inc(sem("outputs"), 1)
                    for hd in range(HEADS):
                        pe.wait_ge(sem("squares"), hd + 1)
                        for b in range(2):
                            mm = pe.matmul(PS[:, 4 + hd // 2, (hd % 2) * T:(hd % 2 + 1) * T], ones, turned[:, 2 * hd + b, :],
                                           start=(b == 0), stop=(b == 1))
                        mm.then_inc(sem("square_sums"), 1)

                @block.scalar
                def _(act):
                    act.activation(proj[:, 16:24, :], proj[:, 16:24, :], ACT.Silu).then_inc(sem("silu"), 1)
                    for hd in range(HEADS):
                        act.wait_ge(sem("outputs"), hd + 1)
                        act.activation(turned[:, 2 * hd:2 * hd + 2, :], PS[:, hd, :].rearrange("p (b t) -> p b t", b=2),
                                       ACT.Square).then_inc(sem("squares"), 1)
                    act.wait_ge(sem("square_sums"), HEADS)
                    act.activation(S[:, :, 0:T].rearrange("p h i -> p h i"), PS[:, 4:6, :].rearrange("p a (b t) -> p (a b) t", b=2),
                                   ACT.Ln, bias=eps, scale=1.0 / 256).then_inc(sem("ln"), 1)
                    act.wait_ge(sem("ln"), 1)
                    act.activation(S[:, :, 0:T], S[:, :, 0:T], ACT.Exp, scale=-0.5).then_inc(sem("root"), 1)

                @block.vector
                def _(dve):
                    link = Chain(dve, sem("dve"))
                    dve.wait_ge(sem("halves_swapped"), 1)
                    dve.tensor_tensor(turned[:, :, :], PS[:, 0:4, :].rearrange("p a (b t) -> p (a b) t", b=2), rep(sin, 8),
                                      ALU.mult).then_inc(sem("turned"), 1)
                    link(dve.tensor_tensor(qk, qk, rep(cos, 8), ALU.mult))
                    dve.wait_ge(sem("turned"), 1)
                    dve.tensor_tensor(qk, qk, turned[:, :, :], ALU.add).then_inc(sem("roped"), 1)
                    dve.wait_ge(sem("scores"), HEADS)
                    dve.wait_ge(sem("ret_con"), 16)
                    for hd in range(HEADS):
                        dve.tensor_tensor(S[:, hd, :], PS[:, 4 + hd, 0:384], ret[:, hd, :], ALU.mult).then_inc(sem("decayed"), 1)
                    dve.wait_ge(sem("root"), 1)
                    dve.wait_ge(sem("silu"), 1)
                    for hd in range(HEADS):
                        link(dve.tensor_tensor(mix[:, 2 * hd:2 * hd + 2, :], PS[:, hd, :].rearrange("p (b t) -> p b t", b=2),
                                               rep(S[:, hd, 0:T], 2), ALU.mult))
                    dve.tensor_tensor(mix[:, :, :], mix[:, :, :], proj[:, 16:24, :], ALU.mult).then_inc(sem("mix"), 1)
        stages.end()

    def delta_rule(proj, gab, mix):
        C8 = 2 * HEADS
        with ExitStack() as st:
            cv = proj[:, 0:16, :]
            sem = stages.begin()
            squares = proj[:, 16:24, :]
            diag = spare_xh[:, 0:4, :].rearrange("p k t -> p (k t)").rearrange("p (a t i) -> p a t i", a=2, t=4)
            vtok = xm[:, :, :]
            ktok = sb("ktok", [P, HEADS, P], st)
            small = sb("small", [P, 120], st)
            ld = small[:, 0:8]
            beta = small[:, 8:16]
            t0, t1, t2, t3, t4 = [small[:, 16 + 8 * i:24 + 8 * i] for i in range(5)]
            nea = small[:, 56:60]
            gcc = small[:, 64:72]
            nbe = small[:, 72:80]
            ekd = small[:, 80:88]
            with nc.Block(no_gpsimd_drain=True) as block:
                @block.vector
                def _(dve):
                    link = Chain(dve, sem("dve"))
                    cw = pr("gconv").rearrange("p (b i) -> p b i", b=16)
                    for tap in range(4):
                        for b in range(8):
                            x = proj[:, 24 + b, :]
                            if tap == 0:
                                i = dve.tensor_scalar(cv[:, b, :], x, cw[:, b, 3:4], None, ALU.mult)
                            else:
                                dve.wait_ge(sem("conv"), 8 * (tap - 1) + b + 1)
                                i = dve.scalar_tensor_tensor(cv[:, b, tap:T], x[:, 0:T - tap], cw[:, b, 3 - tap:4 - tap],
                                                             cv[:, b, tap:T], ALU.mult, ALU.add)
                            i.then_inc(sem("conv"), 1)
                    ga = gab[:, :, 0:4].rearrange("p t c -> p t c")
                    s2 = lambda a: a.rearrange("p (t c) -> p t c", t=2)
                    link(dve.tensor_tensor(s2(t0), ga, rep(pr("dt_bias"), 2), ALU.add))
                    link(dve.tensor_scalar(t1, t0, -1.0, None, ALU.mult))
                    link(dve.tensor_tensor(t1, t0, t1, ALU.min))
                    dve.tensor_scalar(t4, t0, 0.0, None, ALU.max).then_inc(sem("minus_abs"), 1)
                    dve.wait_ge(sem("exp_minus_abs"), 1)
                    link(dve.tensor_scalar(t2, t1, 1.0, None, ALU.add))
                    link(dve.tensor_scalar(t3, t2, -1.0, None, ALU.add))
                    link(dve.tensor_scalar(t0, t3, 0.0, None, ALU.is_equal))
                    dve.tensor_tensor(t3, t3, t0, ALU.add).then_inc(sem("u_minus_1"), 1)
                    dve.wait_ge(sem("ln_u"), 1)
                    link(dve.tensor_tensor(t2, t2, t0, ALU.add))
                    link(dve.reciprocal(t3, t3))
                    link(dve.tensor_tensor(t2, t2, t3, ALU.mult))
                    link(dve.tensor_tensor(t2, t2, t1, ALU.mult))
                    link(dve.tensor_tensor(t2, t2, t4, ALU.add))
                    link(dve.tensor_scalar(nea, nea, -1.0, None, ALU.mult))
                    dve.tensor_tensor(s2(ld), s2(t2), rep(nea, 2), ALU.mult).then_inc(sem("ld"), 1)
                    for q in range(2):
                        dve.wait_ge(sem("root"), q + 1)
                        if q == 0:
                            i = dve.scalar_tensor_tensor(cv[:, 0:4, :], cv[:, 0:4, :], float(P) ** -0.5, squares[:, 0:4, :],
                                                         ALU.mult, ALU.mult)
                        else:
                            i = dve.tensor_tensor(cv[:, 4:8, :], cv[:, 4:8, :], squares[:, 4:8, :], ALU.mult)
                        i.then_inc(sem("qk_normed"), 1)
                    for c in range(2):
                        for hd in range(HEADS):
                            if hd % 2 == 0:
                                dve.wait_ge(sem("v_turned"), 2 * c + hd // 2 + 1)
                            dve.tensor_scalar(vtok[:, 4 * c + hd, :], PS[:, 4 + 2 * c + hd // 2, (hd % 2) * 256:(hd % 2 + 1) * 256],
                                              beta[:, 4 * c + hd:4 * c + hd + 1], None, ALU.mult).then_inc(sem("vtok"), 1)
                    dve.wait_ge(sem("gcc_done"), 1)
                    dve.tensor_copy(gcc, PS[:, 3, 0:8]).then_inc(sem("gcc"), 1)
                    dve.wait_ge(sem("k_turned"), 1)
                    dve.tensor_copy(ktok[:, :, :], PS[:, 0, :].rearrange("p (h d) -> p h d", h=HEADS)).then_inc(sem("ktok"), 1)

                @block.scalar
                def _(act):
                    act.activation(beta.rearrange("p (t c) -> p t c", t=2), gab[:, :, 4:8], ACT.Sigmoid).then_inc(sem("beta"), 1)
                    cw = pr("gconv").rearrange("p (b i) -> p b i", b=16)
                    conv_act(act, sem, diag, lambda b, tp: cw[:, 8 + b, 3 - tp:4 - tp], 8, 4, lambda b: cv[:, 8 + b, :], lambda b: 0.0)
                    act.wait_ge(sem("conv"), 32)
                    act.activation(cv[:, 0:8, :], cv[:, 0:8, :], ACT.Silu).then_inc(sem("silu"), 1)
                    act.wait_ge(sem("silu"), 1)
                    act.activation(squares, cv[:, 0:8, :], ACT.Square).then_inc(sem("squares"), 1)
                    act.activation(nea, pr("a_log"), ACT.Exp).then_inc(sem("act"), 1)
                    act.wait_ge(sem("minus_abs"), 1)
                    act.activation(t1, t1, ACT.Exp).then_inc(sem("exp_minus_abs"), 1)
                    act.wait_ge(sem("u_minus_1"), 1)
                    act.activation(t2, t2, ACT.Ln).then_inc(sem("ln_u"), 1)
                    for q in range(2):
                        act.wait_ge(sem("square_sums"), 4 * q + 4)
                        act.activation(squares[:, 4 * q:4 * q + 4, :], PS[:, 2 * q:2 * q + 2, :].rearrange("p a (b t) -> p (a b) t", b=2),
                                       ACT.Ln, bias=eps).then_inc(sem("ln"), 1)
                    for q in range(2):
                        act.wait_ge(sem("ln"), q + 1)
                        act.activation(squares[:, 4 * q:4 * q + 4, :], squares[:, 4 * q:4 * q + 4, :], ACT.Exp, scale=-0.5
                                       ).then_inc(sem("root"), 1)

                @block.tensor
                def _(pe):
                    conv_pe(pe, sem, diag, lambda b: proj[:, 32 + b, :], 8, 4)
                    pe.wait_ge(sem("squares"), 1)
                    for b in range(8):
                        pe.matmul(PS[:, b // 2, (b % 2) * T:(b % 2 + 1) * T], ones, squares[:, b, :], start=True, stop=True
                                  ).then_inc(sem("square_sums"), 1)
                    pe.wait_ge(sem("block_out"), 8)
                    for c in range(2):
                        for hd in range(HEADS):
                            for b in range(2):
                                mm = pe.transpose(PS[:, 4 + 2 * c + hd // 2, (hd % 2) * 256 + b * P:(hd % 2) * 256 + (b + 1) * P],
                                                  cv[:, 8 + 2 * hd + b, c * P:(c + 1) * P], ident)
                            if hd % 2:
                                mm.then_inc(sem("v_turned"), 1)
                    pe.wait_ge(sem("root"), 2)
                    pe.wait_ge(sem("ld"), 1)
                    pe.matmul(PS[:, 3, 0:8], upto[:, 0, 0:P], ld, start=True, stop=True).then_inc(sem("gcc_done"), 1)
                    pe.wait_ge(sem("qk_normed"), 2)
                    for hd in range(HEADS):
                        mm = pe.transpose(PS[:, 0, hd * P:(hd + 1) * P], cv[:, 4 + hd, 0:P], ident)
                    mm.then_inc(sem("k_turned"), 1)
            stages.end()

            sem = stages.begin()
            at0 = CON["strict"][0]
            free = spare_xh[:, :, :].rearrange("p k t -> p (k t)")
            gcon = free[:, 0:CON["bucket"][0] - at0]
            strict = gcon[:, 0:P]
            levels = gcon[:, P:].rearrange("p (n i) -> p n i", n=7)
            V4 = lambda a: proj[:, a:a + 4, :].rearrange("p a (b i) -> p (a b) i", b=2)
            dec, LT, M, MT = V4(24), V4(28), V4(32), V4(36)
            QK = V4(16)
            Loff, Pm = V4(20), free[:, 1024:2048].rearrange("p (a i) -> p a i", a=C8)
            egB = sb("egB", [P, HEADS, P], st)
            two = lambda b: PS[:, b:b + 2, :].rearrange("p a (c i) -> p (a c) i", c=4)
            four = lambda b: PS[:, b, :].rearrange("p (c i) -> p c i", c=4)
            with nc.Block(no_gpsimd_drain=True) as block:
                @block.sync
                def _(sp):
                    sp.dma_start(gcon, con_dram[:, at0:CON["bucket"][0]]).then_inc(sem("gcon"), 16)

                @block.tensor
                def _(pe):
                    for q in range(C8):
                        c, hd = q // 4, q % 4
                        kc = cv[:, 4 + hd, c * P:(c + 1) * P]
                        at = slice((q % 4) * P, (q % 4 + 1) * P)
                        pe.matmul(PS[:, c, at], ld[:, q:q + 1].to_broadcast([P, P]), upto[:, 0, 0:P], start=True, stop=True)
                        pe.matmul(PS[:, 2 + c, at], beta[:, q:q + 1].to_broadcast([P, P]), ident, start=True, stop=True)
                        pe.matmul(PS[:, 4 + c, at], kc, kc, start=True, stop=True)
                        mm = pe.matmul(PS[:, 6 + c, at], kc, cv[:, hd, c * P:(c + 1) * P], start=True, stop=True)
                    mm.then_inc(sem("products"), 1)
                    pe.wait_ge(sem("MT"), 1)
                    for q in range(C8):
                        mm = pe.transpose(PS[:, q // 4, (q % 4) * P:(q % 4 + 1) * P], MT[:, q, :], ident)
                    mm.then_inc(sem("M_turned"), 1)
                    for n in range(1, 7):
                        for c in range(2):
                            pe.wait_ge(sem(f"M{c}"), n)
                            if n > 1:
                                pe.wait_ge(sem(f"MT{c}"), n - 1)
                            pe.wait_ge(sem(f"Loff{c}"), n)
                            for j in range(4):
                                mm = pe.matmul(PS[:, 2 + c, j * P:(j + 1) * P], Loff[:, 4 * c + j, :], M[:, 4 * c + j, :], start=True, stop=True)
                            mm.then_inc(sem(f"P_done{c}"), 1)
                        for c in range(2):
                            pe.wait_ge(sem(f"P{c}"), n)
                            for j in range(4):
                                mm = pe.matmul(PS[:, 4 + c, j * P:(j + 1) * P], Pm[:, 4 * c + j, :], MT[:, 4 * c + j, :], start=True, stop=True)
                            mm.then_inc(sem(f"N2_done{c}"), 1)
                            if n < 6:
                                for j in range(4):
                                    mm = pe.matmul(PS[:, 6 + c, j * P:(j + 1) * P], MT[:, 4 * c + j, :], Pm[:, 4 * c + j, :], start=True, stop=True)
                                mm.then_inc(sem(f"N1_done{c}"), 1)

                @block.scalar
                def _(act):
                    act.wait_ge(sem("products"), 1)
                    act.activation(egB[:, :, :], PS[:, 1, :].rearrange("p (h i) -> p h i", h=HEADS), ACT.Exp).then_inc(sem("egB"), 1)
                    act.activation(ekd[:, 4:8], gcc[:, 4:8], ACT.Exp).then_inc(sem("egc"), 1)
                    act.wait_ge(sem("last_less"), 1)
                    act.activation(ekd[:, 0:4], ekd[:, 0:4], ACT.Exp).then_inc(sem("act"), 1)
                    act.wait_ge(sem("less"), C8)
                    act.activation(dec, dec, ACT.Exp).then_inc(sem("decays"), 1)
                    act.activation(proj[:, 48:64, :], proj[:, 48:64, :], ACT.Sigmoid).then_inc(sem("act"), 1)
                    act.activation(proj[:, 40:48, :], proj[:, 40:48, :], ACT.Silu).then_inc(sem("act"), 1)
                    for n in range(1, 7):
                        for c in range(2):
                            act.wait_ge(sem(f"P_done{c}"), n)
                            if n > 1:
                                act.wait_ge(sem(f"N2_done{c}"), n - 1)
                                act.wait_ge(sem(f"N1_done{c}"), n - 1)
                            act.copy(Pm[:, 4 * c:4 * c + 4, :], four(2 + c)).then_inc(sem(f"P{c}"), 1)

                @block.vector
                def _(dve):
                    link = Chain(dve, sem("dve"))
                    dve.wait_ge(sem("products"), 1)
                    for q in range(C8):
                        if q == 4:
                            dve.wait_ge(sem("egB"), 1)
                        dve.tensor_scalar(dec[:, q, :], PS[:, q // 4, (q % 4) * P:(q % 4 + 1) * P], gcc[:, q:q + 1], 0.0,
                                          ALU.subtract, ALU.min).then_inc(sem("less"), 1)
                    dve.tensor_tensor(ekd[:, 0:4], PS[:, 0, P - 1:512:P], gcc[:, 0:4], ALU.subtract).then_inc(sem("last_less"), 1)
                    dve.wait_ge(sem("egc"), 1)
                    dve.scalar_tensor_tensor(nbe[:, 4:8], ekd[:, 4:8], -1.0, beta[:, 4:8], ALU.mult, ALU.mult).then_inc(sem("nbe"), 1)
                    dve.wait_ge(sem("decays"), 1)
                    link(dve.tensor_tensor(dec, dec, rep(upto[:, 0, 0:P], C8), ALU.mult))
                    dve.tensor_tensor(QK, two(6), dec, ALU.mult).then_inc(sem("QK"), 1)
                    link(dve.tensor_tensor(LT, two(4), dec, ALU.mult))
                    link(dve.tensor_tensor(LT, LT, two(2), ALU.mult))
                    dve.wait_ge(sem("gcon"), 16)
                    link(dve.tensor_tensor(LT, LT, rep(strict, C8), ALU.mult))
                    link(dve.tensor_tensor(MT, LT, rep(levels[:, 0, :], C8), ALU.mult))
                    dve.scalar_tensor_tensor(MT, MT, -1.0, rep(ident, C8), ALU.mult, ALU.add).then_inc(sem("MT"), 1)
                    dve.wait_ge(sem("MT"), 1)
                    for c in range(2):
                        half = slice(4 * c, 4 * c + 4)
                        dve.tensor_tensor(Loff[:, half, :], LT[:, half, :], rep(levels[:, 1, :], 4), ALU.mult).then_inc(sem(f"Loff{c}"), 1)
                    dve.wait_ge(sem("M_turned"), 1)
                    for c in range(2):
                        dve.tensor_copy(M[:, 4 * c:4 * c + 4, :], four(c)).then_inc(sem(f"M{c}"), 1)
                    for n in range(1, 7):
                        for c in range(2):
                            half = slice(4 * c, 4 * c + 4)
                            if n < 6:
                                dve.wait_ge(sem(f"P_done{c}"), n)
                                dve.tensor_tensor(Loff[:, half, :], LT[:, half, :], rep(levels[:, n + 1, :], 4), ALU.mult
                                                  ).then_inc(sem(f"Loff{c}"), 1)
                        for c in range(2):
                            half = slice(4 * c, 4 * c + 4)
                            if n < 6:
                                dve.wait_ge(sem(f"N1_done{c}"), n)
                                dve.wait_ge(sem(f"M{c}"), n)
                                dve.tensor_tensor(M[:, half, :], M[:, half, :], four(6 + c), ALU.subtract).then_inc(sem(f"M{c}"), 1)
                            dve.wait_ge(sem(f"N2_done{c}"), n)
                            if n > 1:
                                dve.wait_ge(sem(f"MT{c}"), n - 1)
                            dve.tensor_tensor(MT[:, half, :], MT[:, half, :], four(4 + c), ALU.subtract).then_inc(sem(f"MT{c}"), 1)
            stages.end()

            sem = stages.begin()
            vn = Pm.rearrange("p a b -> p (a b)").rearrange("p (h v) -> p h v", h=HEADS)
            vs = dec.rearrange("p a b -> p (a b)").rearrange("p (h v) -> p h v", h=HEADS)
            state = M.rearrange("p a b -> p (a b)").rearrange("p (h v) -> p h v", h=HEADS)
            rhs = Loff.rearrange("p a b -> p (a b)").rearrange("p (h v) -> p h v", h=HEADS)
            qg = LT[:, 0:4, :]
            sq = cv[:, 8:16, :]
            r4 = proj[:, 24:28, :]
            y = cv[:, 0:8, :]
            heads2 = lambda b: PS[:, b:b + 2, :].rearrange("p a (c v) -> p (a c) v", c=2)
            o_of = lambda hd, b, c: PS[:, 4 + hd, b * T + c * P:b * T + (c + 1) * P]
            with nc.Block(no_gpsimd_drain=True) as block:
                @block.tensor
                def _(pe):
                    for hd in range(HEADS):
                        mm = pe.matmul(PS[:, hd // 2, (hd % 2) * 256:(hd % 2 + 1) * 256], MT[:, hd, :], vtok[:, hd, :], start=True, stop=True)
                    mm.then_inc(sem("u_done"), 1)
                    pe.wait_ge(sem("vs"), HEADS)
                    for hd in range(HEADS):
                        mm = pe.matmul(PS[:, 2 + hd // 2, (hd % 2) * 256:(hd % 2 + 1) * 256], ktok[:, hd, :], vs[:, hd, :], start=True, stop=True)
                    mm.then_inc(sem("state_done"), 1)
                    pe.wait_ge(sem("vn"), 1)
                    for hd in range(HEADS):
                        for b in range(2):
                            mm = pe.matmul(o_of(hd, b, 0), vn[:, hd, b * P:(b + 1) * P], QK[:, hd, :], start=True, stop=True)
                    mm.then_inc(sem("o0_done"), 1)
                    pe.wait_ge(sem("state"), 1)
                    for hd in range(HEADS):
                        mm = pe.matmul(PS[:, hd // 2, (hd % 2) * 256:(hd % 2 + 1) * 256], cv[:, 4 + hd, P:T], state[:, hd, :], start=True, stop=True)
                    mm.then_inc(sem("ks_done"), 1)
                    pe.wait_ge(sem("rhs"), HEADS)
                    for hd in range(HEADS):
                        mm = pe.matmul(PS[:, 2 + hd // 2, (hd % 2) * 256:(hd % 2 + 1) * 256], MT[:, 4 + hd, :], rhs[:, hd, :], start=True, stop=True)
                    mm.then_inc(sem("u1_done"), 1)
                    pe.wait_ge(sem("vn"), 2)
                    pe.wait_ge(sem("qg"), 1)
                    for hd in range(HEADS):
                        for b in range(2):
                            pe.matmul(o_of(hd, b, 1), vn[:, hd, b * P:(b + 1) * P], QK[:, 4 + hd, :], start=True, stop=False)
                            mm = pe.matmul(o_of(hd, b, 1), state[:, hd, b * P:(b + 1) * P], qg[:, hd, :], start=False, stop=True)
                        mm.then_inc(sem("o_done"), 1)
                    for hd in range(HEADS):
                        pe.wait_ge(sem("squares"), hd + 1)
                        for b in range(2):
                            mm = pe.matmul(PS[:, hd // 2, (hd % 2) * T:(hd % 2 + 1) * T], ones, sq[:, 2 * hd + b, :],
                                           start=(b == 0), stop=(b == 1))
                        mm.then_inc(sem("square_sums"), 1)

                @block.scalar
                def _(act):
                    act.wait_ge(sem("u_done"), 1)
                    act.copy(vn[:, :, :], heads2(0)).then_inc(sem("vn"), 1)
                    act.wait_ge(sem("state_done"), 1)
                    act.copy(state, heads2(2)).then_inc(sem("state"), 1)
                    for u in range(2):
                        high_a(act, A_AT["wout"][0] + u)
                    act.wait_ge(sem("u1_done"), 1)
                    act.wait_ge(sem("o0_done"), 1)
                    act.wait_ge(sem("vs"), HEADS)
                    act.copy(vn[:, :, :], heads2(2)).then_inc(sem("vn"), 1)
                    for hd in range(HEADS):
                        act.wait_ge(sem("o_done"), hd + 1)
                        act.activation(sq[:, 2 * hd:2 * hd + 2, :], PS[:, 4 + hd, :].rearrange("p (b t) -> p b t", b=2),
                                       ACT.Square).then_inc(sem("squares"), 1)
                    act.wait_ge(sem("square_sums"), HEADS)
                    act.activation(r4, PS[:, 0:2, :].rearrange("p a (b t) -> p (a b) t", b=2), ACT.Ln, bias=eps, scale=1.0 / 256
                                   ).then_inc(sem("ln"), 1)
                    act.wait_ge(sem("ln"), 1)
                    act.activation(r4, r4, ACT.Exp, scale=-0.5).then_inc(sem("root"), 1)

                @block.vector
                def _(dve):
                    link = Chain(dve, sem("dve"))
                    dve.tensor_tensor(qg, cv[:, 0:4, P:T], egB[:, :, :], ALU.mult).then_inc(sem("qg"), 1)
                    dve.wait_ge(sem("vn"), 1)
                    for hd in range(HEADS):
                        dve.tensor_scalar(vs[:, hd, :], vn[:, hd, :], ekd[:, hd:hd + 1], None, ALU.mult).then_inc(sem("vs"), 1)
                    dve.wait_ge(sem("ks_done"), 1)
                    for hd in range(HEADS):
                        dve.scalar_tensor_tensor(rhs[:, hd, :], PS[:, hd // 2, (hd % 2) * 256:(hd % 2 + 1) * 256],
                                                 nbe[:, 4 + hd:5 + hd], vtok[:, 4 + hd, :], ALU.mult, ALU.add).then_inc(sem("rhs"), 1)
                    for u in range(2):
                        low_a(dve, A_AT["wout"][0] + u)
                    dve.tensor_tensor(proj[:, 40:48, :], proj[:, 40:48, :], proj[:, 56:64, :], ALU.mult).then_inc(sem("gates"), 1)
                    dve.tensor_tensor(mix[:, :, :], mix[:, :, :], proj[:, 48:56, :], ALU.mult).then_inc(sem("gates"), 1)
                    dve.wait_ge(sem("gates"), 2)
                    dve.wait_ge(sem("root"), 1)
                    for hd in range(HEADS):
                        for b in range(2):
                            i = dve.scalar_tensor_tensor(y[:, 2 * hd + b, :], PS[:, 4 + hd, b * T:(b + 1) * T],
                                                         pr("gdn_w", b, b + 1), r4[:, hd, :], ALU.mult, ALU.mult)
                    link(i)
                    link(dve.tensor_tensor(y, y, proj[:, 40:48, :], ALU.mult))
                    dve.tensor_tensor(mix[:, :, :], mix[:, :, :], y, ALU.add).then_inc(sem("mix"), 1)
            stages.end()

    def down_pe(pe, high, low, used, hidden, first, last):
        for kf in range(2):
            for ob in range(KC):
                at = slice(ob * P, (ob + 1) * P)
                mm = mm3(pe, PS[:, 4 + ob // 2, (ob % 2) * T:(ob % 2 + 1) * T], high[:, kf, at], low[:, kf, at],
                         hidden[kf][0], hidden[kf][1], start=(first and kf == 0 and ob % 2 == 0), stop=last, skip_group_check=True)
        mm.then_inc(used, 1)

    def swiglu(name, steps, combB):
        sem = stages.begin()
        a0, b0 = A_AT[name][0], B_AT[name][0]
        modulate = name in C_UNITS
        with ExitStack() as st:
            silu = sb(f"silu{stages.k}", [P, 2, 512], st)
            hid_, hid_low = sb2(f"hid{stages.k}", [P, 2, 2, T], st)
            hid_high = st.enter_context(nc.sbuf_tensor(f"hid_high{stages.k}", [P, 2, 2, T], F32R))
            highB = st.enter_context(nc.sbuf_tensor(f"highB{stages.k}", [P, 2, 2, D], F32R))
            if modulate:
                bufC, acc = sb(f"bufC{stages.k}", [P, KC, 256], st), sb(f"acc{stages.k}", [P, 2, 256], st)
                sums = sb(f"sums{stages.k}", [P, 2 * C_UNITS[name][1]], st)
            turns = steps // 4

            with nc.Block(no_gpsimd_drain=True) as block:
                if modulate:
                    @block.gpsimd
                    def _(pool):
                        c_loads(pool, sem, bufC[:, :, :], name)

                @block.sync
                def _(sp):
                    refill_ab(sp, a0, b0, steps)

                def down(pe, s, i, first, last):
                    pe.wait_ge(b_low, plus(b0 + s + 1, i, 4))
                    pe.wait_ge(sem("hid_low"), plus(s + 1, i, 4))
                    down_pe(pe, highB[:, (b0 + s) % 2], lowB[:, (b0 + s) % NB], b_used, [(hid_high[:, s % 2, kf, :], hid_low[:, s % 2, kf, :]) for kf in range(2)], first, last)

                @block.tensor
                def _(pe):
                    def step(s, i=None):
                        if i is not None or s >= 2:
                            pe.wait_ge(sem("hidden"), plus(s - 1, i, 4))
                            if modulate and (i is not None or s >= 3):
                                pe.wait_ge(sem("c_out"), plus(s - 2, i, 4))
                        for j in range(2):
                            m = a0 + 2 * s + j
                            split_a_wait(pe, m, i)
                            for b in range(2):
                                at = slice(b * P, (b + 1) * P)
                                for k in range(KC):
                                    mm = mm3(pe, PS[:, 2 * (s % 2) + j, b * T:(b + 1) * T], highA[:, m % 2, k, at], lowA[:, m % NA, k, at],
                                             xh[:, k, :], xl[:, k, :], start=(k == 0), stop=(k == KC - 1))
                            mm.then_inc(a_used, 1)
                        if i is not None or s >= 1:
                            down(pe, s - 1, i, first=(i is None and s == 1), last=False)
                        if modulate and (i is not None or s >= 1):
                            pe.wait_ge(sem("silu"), plus(s + 1, i, 4))
                            c_sum(pe, sem, acc, 0, s - 1, i, 4, bank=2 * (s % 2), fixed=True)
                    for s in range(4):
                        step(s)
                    if turns > 1:
                        with pe.Fori(1, turns) as i:
                            for s in range(4):
                                step(s, i)
                    for s in range(4 * turns, steps):
                        step(s)
                    down(pe, steps - 1, None, False, True)
                    if modulate:
                        c_sum(pe, sem, acc, 0, steps - 1, bank=2 * (steps % 2))

                @block.scalar
                def _(act):
                    def step(s, i=None, ahead=True):
                        act.wait_ge(a_used, plus(a0 + 2 * s + 1, i, 8))
                        if i is not None or s >= 2:
                            act.wait_ge(sem("hidden"), plus(s - 1, i, 4))
                        act.activation(silu[:, s % 2, :], PS[:, 2 * (s % 2), :], ACT.Silu).then_inc(sem("silu"), 1)
                        if ahead:
                            high_a(act, a0 + 2 * s + 2, i)
                        act.wait_ge(sem("hidden"), plus(s + 1, i, 4))
                        if i is not None or s >= 2:
                            act.wait_ge(b_used, plus(b0 + s - 1, i, 4))
                        act.copy(hid_high[:, s % 2, :, :], hid_[:, s % 2, :, :]).then_inc(sem("hid_high"), 1)
                        if ahead:
                            high_a(act, a0 + 2 * s + 3, i)
                        high_b(act, highB, b0 + s, i)

                    for s in range(4):
                        step(s)
                    last = turns if steps % 4 else turns - 1
                    with act.Fori(1, last) as i:
                        for s in range(4):
                            step(s, i)
                    for s in range(4 * last, steps):
                        step(s, None, s + 1 < steps)

                @block.vector
                def _(dve):
                    def sums_out(m, i=None):
                        dve.wait_ge(sem("c_summed"), plus(m + 1, i, 4))
                        to = sums[:, 2 * m:2 * m + 2] if i is None else sums[:, bass.ds(i * 8 + 2 * m, 2)]
                        dve.tensor_copy(to, PS[:, 2 * ((m + 1) % 2), 0:2]).then_inc(sem("c_out"), 1)

                    def step(s, i=None, ahead=True):
                        hid = hid_[:, s % 2, :, :]
                        if ahead:
                            low_a(dve, a0 + 2 * s + 2, i)
                        dve.wait_ge(a_used, plus(a0 + 2 * s + 2, i, 8))
                        dve.wait_ge(sem("silu"), plus(s + 1, i, 4))
                        if i is not None or s >= 2:
                            dve.wait_ge(b_used, plus(b0 + s - 1, i, 4))
                        up = PS[:, 2 * (s % 2) + 1, :].rearrange("p (b t) -> p b t", b=2)
                        ins_ = dve.tensor_tensor(hid, silu[:, s % 2, :].rearrange("p (b t) -> p b t", b=2), up, ALU.mult)
                        if combB is not None:
                            ins_.then_inc(sem("unweighted"), 1)
                            dve.wait_ge(sem("unweighted"), plus(s + 1, i, 4))
                            comb = combB[:, s // 2, :] if i is None else combB[:, bass.ds(i * 2 + s // 2, 1), :].rearrange("p a t -> p (a t)")
                            ins_ = dve.tensor_tensor(hid, hid, rep(comb, 2), ALU.mult)
                        ins_.then_inc(sem("hidden"), 1)
                        dve.wait_ge(sem("hid_high"), plus(s + 1, i, 4))
                        dve.tensor_tensor(hid_low[:, s % 2, :, :], hid, hid_high[:, s % 2, :, :].bitcast(F32), ALU.subtract
                                          ).then_inc(sem("hid_low"), 1)
                        if modulate:
                            if i is not None or s >= 2:
                                sums_out(s - 2, i)
                            c_scale(dve, sem, bufC[:, :, :], acc, 1, C_UNITS[name][0], s, i, 4)
                        if ahead:
                            low_a(dve, a0 + 2 * s + 3, i)
                        low_b(dve, highB, b0 + s, i)

                    low_a(dve, a0 + 1)
                    for s in range(4):
                        step(s)
                    last = turns if steps % 4 else turns - 1
                    with dve.Fori(1, last) as i:
                        for s in range(4):
                            step(s, i)
                    for s in range(4 * last, steps):
                        step(s, None, s + 1 < steps)
                    if modulate:
                        sums_out(steps - 2)
                        sums_out(steps - 1)
                        mods_out(dve, sem, sem("c_out"), steps, sums[:, :], 48, 112,
                                 [(1, 0, pr("norm_mix2", 0, 8)), (1, 1, pr("norm_ffn2", 0, 8)), (2, 0, pr("norm_mix2", 8, 16))])
            stages.end()

    def moe():
        with ExitStack() as st:
            combB = sb("combB", [P, N_EXP, T], st)
            w = sb("route", [P, 2, 80], st)
            sem = stages.begin()
            lg = w[:, :, 0:20]
            eq, pre, oh = w[:, :, 20:24], w[:, :, 24:28], w[:, :, 28:32]
            el, pe_, oh1, oh2 = w[:, :, 32:36], w[:, :, 36:40], w[:, :, 40:44], w[:, :, 44:48]
            m1, m2, s1, gt = w[:, :, 48:49], w[:, :, 49:50], w[:, :, 50:51], w[:, :, 51:52]
            comb = sb("comb", [P, 2, N_EXP], st)
            prod = sb("prod", [P, 2, N_EXP], st)
            spread = lambda a, n: bass.AP(tensor=a.tensor, offset=a.offset, ap=[list(a.ap[0]), list(a.ap[1]), [0, n]])
            with nc.Block(no_gpsimd_drain=True) as block:
                @block.tensor
                def _(pe):
                    pe.wait_ge(sem("comb"), 1)
                    for e in range(N_EXP):
                        if e >= 8 and e % 2 == 0:
                            pe.wait_ge(sem("combB"), (e - 8) // 2 + 1)
                        for t in range(2):
                            mm = pe.matmul(PS[:, 4 + e // 2 % 4, (e % 2) * T + t * P:(e % 2) * T + (t + 1) * P],
                                           comb[:, t, e:e + 1].to_broadcast([P, P]), ident, start=True, stop=True)
                        if e % 2:
                            mm.then_inc(sem("combB_done"), 1)

                @block.scalar
                def _(act):
                    act.wait_ge(sem("less_max"), 1)
                    act.activation(pre, eq, ACT.Exp).then_inc(sem("group_exp"), 1)
                    act.wait_ge(sem("less_max2"), 1)
                    act.activation(pe_, el, ACT.Exp).then_inc(sem("expert_exp"), 1)
                    for n in range(N_EXP // 2):
                        act.wait_ge(sem("combB_done"), n + 1)
                        act.copy(combB[:, 2 * n:2 * n + 2, :], PS[:, 4 + n % 4, :].rearrange("p (e t) -> p e t", e=2)
                                 ).then_inc(sem("combB"), 1)

                @block.vector
                def _(dve):
                    link = Chain(dve, sem("dve"))

                    def first_of(dst, hit, at):
                        link(dve.tensor_copy(at, hit))
                        link(dve.tensor_tensor(at[:, :, 1:4], at[:, :, 1:4], hit[:, :, 0:3], ALU.add))
                        link(dve.tensor_tensor(at[:, :, 2:4], at[:, :, 2:4], hit[:, :, 0:2], ALU.add))
                        link(dve.tensor_tensor(at[:, :, 3:4], at[:, :, 3:4], hit[:, :, 0:1], ALU.add))
                        link(dve.tensor_scalar(at, at, 1.0, None, ALU.is_equal))
                        link(dve.tensor_tensor(dst, at, hit, ALU.mult))

                    link(dve.tensor_tensor(lg, PS[:, 4, 0:40].rearrange("p (t c) -> p t c", t=2), rep(pr("b_route"), 2), ALU.add))
                    link(dve.tensor_reduce(m1, lg[:, :, 0:4], AX_X, ALU.max))
                    dve.tensor_tensor(eq, lg[:, :, 0:4], spread(m1, 4), ALU.subtract).then_inc(sem("less_max"), 1)
                    dve.wait_ge(sem("group_exp"), 1)
                    link(dve.tensor_reduce(gt, pre, AX_X, ALU.add))
                    link(dve.reciprocal(gt, gt))
                    link(dve.tensor_tensor(pre, pre, spread(gt, 4), ALU.mult))
                    link(dve.tensor_reduce(gt, pre, AX_X, ALU.max))
                    link(dve.tensor_tensor(eq, pre, spread(gt, 4), ALU.is_equal))
                    first_of(oh, eq, pre)
                    for g in range(4):
                        link(dve.tensor_tensor(prod[:, :, 4 * g:4 * g + 4], lg[:, :, 4 + 4 * g:8 + 4 * g], spread(oh[:, :, g:g + 1], 4), ALU.mult))
                    link(dve.tensor_tensor(prod[:, :, 0:8], prod[:, :, 0:8], prod[:, :, 8:16], ALU.add))
                    link(dve.tensor_tensor(el, prod[:, :, 0:4], prod[:, :, 4:8], ALU.add))
                    link(dve.tensor_reduce(m1, el, AX_X, ALU.max))
                    dve.tensor_tensor(el, el, spread(m1, 4), ALU.subtract).then_inc(sem("less_max2"), 1)
                    dve.wait_ge(sem("expert_exp"), 1)
                    link(dve.tensor_reduce(s1, pe_, AX_X, ALU.add))
                    link(dve.reciprocal(s1, s1))
                    link(dve.tensor_tensor(pe_, pe_, spread(s1, 4), ALU.mult))
                    link(dve.tensor_reduce(m1, pe_, AX_X, ALU.max))
                    link(dve.tensor_tensor(eq, pe_, spread(m1, 4), ALU.is_equal))
                    first_of(oh1, eq, pre)
                    link(dve.scalar_tensor_tensor(pe_, oh1, -2.0, pe_, ALU.mult, ALU.add))
                    link(dve.tensor_reduce(m2, pe_, AX_X, ALU.max))
                    link(dve.tensor_tensor(eq, pe_, spread(m2, 4), ALU.is_equal))
                    first_of(oh2, eq, pre)
                    link(dve.tensor_tensor(s1, m1, m2, ALU.add))
                    link(dve.reciprocal(s1, s1))
                    link(dve.tensor_tensor(oh1, oh1, spread(m1, 4), ALU.mult))
                    link(dve.tensor_tensor(oh2, oh2, spread(m2, 4), ALU.mult))
                    link(dve.tensor_tensor(oh1, oh1, oh2, ALU.add))
                    link(dve.tensor_tensor(oh1, oh1, spread(s1, 4), ALU.mult))
                    link(dve.tensor_tensor(oh1, oh1, spread(gt, 4), ALU.mult))
                    for g in range(4):
                        i = dve.tensor_tensor(comb[:, :, 4 * g:4 * g + 4], oh1, spread(oh[:, :, g:g + 1], 4), ALU.mult)
                    i.then_inc(sem("comb"), 1)
            stages.end()
            swiglu("moe", 2 * N_EXP, combB)

    def mixer_two():
        with ExitStack() as st:
            yb, yb_low = sb2("yb", [P, 16, T], st)
            state_space(yb)
            att, att_low = sb2("att", [P, KC, T], st)
            attention(yb, att)
            sem = stages.begin()
            a0, n = A_AT["hyout"]
            high = st.enter_context(nc.sbuf_tensor("out_high", [P, 24, T], F32R))
            as_b = lambda w: w.rearrange("p k c -> p (k c)").rearrange("p (k c) -> p k c", k=2)
            pair = lambda u: yb[:, 2 * u:2 * u + 2, :] if u < 8 else att[:, 2 * u - 16:2 * u - 14, :]
            low_pair = lambda u: yb_low[:, 2 * u:2 * u + 2, :] if u < 8 else att_low[:, 2 * u - 16:2 * u - 14, :]
            with nc.Block(no_gpsimd_drain=True) as block:
                @block.sync
                def _(sp):
                    refill_a(sp, a0, n)

                @block.scalar
                def _(act):
                    for u in range(n):
                        act.copy(high[:, 2 * u:2 * u + 2, :], pair(u)).then_inc(sem("x_high"), 1)
                        high_a(act, a0 + u)

                @block.tensor
                def _(pe):
                    for u in range(n):
                        pe.wait_ge(sem("x_low"), u + 1)
                        split_a_wait(pe, a0 + u)
                        low = low_pair(u)
                        down_pe(pe, as_b(highA[:, (a0 + u) % 2]), as_b(lowA[:, (a0 + u) % NA]), a_used, [(high[:, 2 * u + kf, :], low[:, kf, :]) for kf in range(2)], u == 0, u == n - 1)

                @block.vector
                def _(dve):
                    for u in range(n):
                        dve.wait_ge(sem("x_high"), u + 1)
                        dve.tensor_tensor(low_pair(u), pair(u), high[:, 2 * u:2 * u + 2, :].bitcast(F32), ALU.subtract
                                          ).then_inc(sem("x_low"), 1)
                        low_a(dve, a0 + u)
            stages.end()

    def state_space(yb):
        with ExitStack() as st:
            zx = sb("zx", [P, 40, T], st)
            dts = sb("dts", [SSM_H, 7, T], st)
            sem = stages.begin()
            a0, n = A_AT["hyin"]
            cst = ExitStack()
            bufC, acc = sb("bufC2", [P, KC, 256], cst), sb("acc2", [P, 2, 256], cst)
            with nc.Block(no_gpsimd_drain=True) as block:
                @block.gpsimd
                def _(pool):
                    c_loads(pool, sem, bufC[:, :, :], "hyin")

                @block.sync
                def _(sp):
                    refill_a(sp, a0, n)

                @block.tensor
                def _(pe):
                    proj_pe(pe, sem, a0, n, c_units=C_UNITS["hyin"], acc=acc)

                @block.scalar
                def _(act):
                    proj_evac(act, 0, sem, a0, n, zx)

                @block.vector
                def _(dve):
                    dve.tensor_scalar(dts[:, 0, :], PS[0:SSM_H, 4, 0:T], pr("dt_bias2")[0:SSM_H, :], None, ALU.add).then_inc(sem("dt"), 1)
                    proj_evac(dve, 1, sem, a0, n, zx, (bufC[:, :, :], acc, "hyin", 1))
                    mods_out(dve, sem, sem("c_summed"), 8, PS[:, 5, 112:128], 112, 128, [])
            cst.close()
            stages.end()

            spare = spare_highA[:, :, :, :]
            bc = spare[:, 0, :, :]
            sem = stages.begin()
            xdt = zx[:, 16:32, :].rearrange("p a b -> p (a b)").rearrange("p (t c) -> p t c", t=2)
            tok = sb("tok", [P, 3, 2, SSM_H], st)
            cbm = sb("cbm", [P, 4, 384], st)
            na = sb("na", [SSM_H, 1], st)
            acsT = sb("acsT", [P, T], st)
            ON_PE = 10
            diag = spare[:, 1, 0:4, :].rearrange("p k t -> p (k t)").rearrange("p (a t i) -> p a t i", a=2, t=4)
            conv_to = lambda b: yb[:, b, :] if b < 16 else bc[:, b - 16, :]
            with nc.Block(no_gpsimd_drain=True) as block:
                @block.vector
                def _(dve):
                    link = Chain(dve, sem("dve"))
                    y, e, u, um, m0, dt, dA = [dts[:, i, :] for i in range(7)]
                    link(dve.tensor_scalar(e, y, -1.0, None, ALU.mult))
                    link(dve.tensor_tensor(e, y, e, ALU.min))
                    dve.tensor_scalar(m0, y, 0.0, None, ALU.max).then_inc(sem("minus_abs"), 1)
                    dve.wait_ge(sem("exp_minus_abs"), 1)
                    link(dve.tensor_scalar(u, e, 1.0, None, ALU.add))
                    link(dve.tensor_scalar(um, u, -1.0, None, ALU.add))
                    link(dve.tensor_scalar(y, um, 0.0, None, ALU.is_equal))
                    dve.tensor_tensor(um, um, y, ALU.add).then_inc(sem("u_minus_1"), 1)
                    dve.wait_ge(sem("ln_u"), 1)
                    link(dve.tensor_tensor(u, u, y, ALU.add))
                    link(dve.reciprocal(um, um))
                    link(dve.tensor_tensor(u, u, um, ALU.mult))
                    link(dve.tensor_tensor(u, u, e, ALU.mult))
                    link(dve.tensor_tensor(dt, u, m0, ALU.add))
                    link(dve.tensor_scalar(na[:, :], na[:, :], -1.0, None, ALU.mult))
                    dve.tensor_scalar(dA, dt, na[:, 0:1], None, ALU.mult).then_inc(sem("dA"), 1)
                    dve.wait_ge(sem("turned"), 1)
                    dve.tensor_copy(tok[:, 0:2, :, :], PS[:, 0, 0:128].rearrange("p (a t c) -> p a t c", a=2, t=2)).then_inc(sem("tok"), 1)
                    dve.wait_ge(sem("sums_done"), 1)
                    dve.tensor_copy(tok[:, 2, :, :], PS[:, 1, 0:64].rearrange("p (t c) -> p t c", t=2)).then_inc(sem("acs"), 1)
                    link(dve.memset(acsT[:, :], 0.0))
                    dve.tensor_copy(acsT[0:SSM_H, :], PS[0:SSM_H, 1, 128:384]).then_inc(sem("acs"), 1)
                    cw = pr("hconv").rearrange("p (b i) -> p b i", b=24)
                    for tap_ in range(4):
                        for b in range(ON_PE, 24):
                            x, o = zx[:, 16 + b, :], conv_to(b)
                            if tap_ == 0:
                                i = dve.tensor_scalar(o, x, cw[:, b, 3:4], pr("hconv_b", b, b + 1), ALU.mult, ALU.add)
                            else:
                                dve.wait_ge(sem("conv"), (24 - ON_PE) * (tap_ - 1) + b - ON_PE + 1)
                                i = dve.scalar_tensor_tensor(o[:, tap_:T], x[:, 0:T - tap_], cw[:, b, 3 - tap_:4 - tap_],
                                                             o[:, tap_:T], ALU.mult, ALU.add)
                            i.then_inc(sem("conv"), 1)
                    dve.wait_ge(sem("cb_done"), 1)
                    dve.tensor_tensor(cbm[:, :, 0:T], PS[:, 4:8, 0:T], rep(upto[:, 0, :], 4), ALU.mult).then_inc(sem("cbm"), 1)
                    dve.tensor_tensor(cbm[:, :, T:384], PS[:, 4:8, T:384], rep(upto[:, 0, 0:P], 4), ALU.mult).then_inc(sem("cbm"), 1)
                    for n8 in range(8):
                        t, c4 = n8 // 4, n8 % 4
                        dve.wait_ge(sem("x_turned"), n8 + 1)
                        dve.tensor_tensor(xdt[:, t, c4 * 512:(c4 + 1) * 512].rearrange("p (h d) -> p h d", h=8),
                                          PS[:, n8 % 4, :].rearrange("p (h d) -> p h d", h=8),
                                          wide(tok[:, 0, t, 8 * c4:8 * c4 + 8], 64), ALU.mult).then_inc(sem("xdt"), 1)

                @block.scalar
                def _(act):
                    act.activation(na[:, :], pr("a_log2")[0:SSM_H, :], ACT.Exp).then_inc(sem("act"), 1)
                    act.wait_ge(sem("minus_abs"), 1)
                    act.activation(dts[:, 1, :], dts[:, 1, :], ACT.Exp).then_inc(sem("exp_minus_abs"), 1)
                    act.wait_ge(sem("u_minus_1"), 1)
                    act.activation(dts[:, 2, :], dts[:, 2, :], ACT.Ln).then_inc(sem("ln_u"), 1)
                    cw = pr("hconv").rearrange("p (b i) -> p b i", b=24)
                    conv_act(act, sem, diag, lambda b, tp: cw[:, b, 3 - tp:4 - tp], ON_PE, 2, lambda b: yb[:, b, :],
                             lambda b: pr("hconv_b", b, b + 1))
                    act.wait_ge(sem("conv"), 4 * (24 - ON_PE))
                    act.activation(bc, bc, ACT.Silu).then_inc(sem("silu"), 1)
                    act.activation(yb[:, ON_PE:16, :], yb[:, ON_PE:16, :], ACT.Silu).then_inc(sem("silu"), 1)
                    act.activation(zx[:, 0:16, :], zx[:, 0:16, :], ACT.Silu).then_inc(sem("act"), 1)

                @block.tensor
                def _(pe):
                    pe.wait_ge(sem("dA"), 1)
                    for a in range(2):
                        for t in range(2):
                            mm = pe.transpose(PS[:, 0, (2 * a + t) * 32:(2 * a + t + 1) * 32], dts[:, 5 + a, t * P:(t + 1) * P], ident[0:SSM_H, 0:SSM_H])
                    mm.then_inc(sem("turned"), 1)
                    pe.wait_ge(sem("tok"), 1)
                    pe.matmul(PS[:, 1, 0:32], upto[:, 0, 0:P], tok[:, 1, 0, :], start=True, stop=True)
                    pe.matmul(PS[:, 1, 32:64], upto[:, 0, P:T], tok[:, 1, 0, :], start=True, stop=False)
                    pe.matmul(PS[:, 1, 32:64], upto[:, 1, P:T], tok[:, 1, 1, :], start=False, stop=True)
                    pe.matmul(PS[0:SSM_H, 1, 128:384], tok[:, 1, 0, :], upto[:, 0, :], start=True, stop=False)
                    pe.matmul(PS[0:SSM_H, 1, 128:384], tok[:, 1, 1, :], upto[:, 1, :], start=False, stop=True).then_inc(sem("sums_done"), 1)
                    conv_pe(pe, sem, diag, lambda b: zx[:, 16 + b, :], ON_PE, 2)
                    pe.wait_ge(sem("block_out"), ON_PE)
                    pe.wait_ge(sem("silu"), 1)
                    for g in range(4):
                        pe.matmul(PS[:, 4 + g, 0:T], bc[:, g, 0:P], bc[:, 4 + g, :], start=True, stop=True)
                        mm = pe.matmul(PS[:, 4 + g, T:384], bc[:, g, P:T], bc[:, 4 + g, P:T], start=True, stop=True)
                    mm.then_inc(sem("cb_done"), 1)
                    pe.wait_ge(sem("silu"), 2)
                    pe.wait_ge(sem("acs"), 2)
                    for n8 in range(8):
                        t, c4 = n8 // 4, n8 % 4
                        if n8 >= 4:
                            pe.wait_ge(sem("xdt"), n8 - 3)
                        for j in range(4):
                            mm = pe.transpose(PS[:, n8 % 4, j * P:(j + 1) * P], yb[:, 4 * c4 + j, t * P:(t + 1) * P], ident)
                        mm.then_inc(sem("x_turned"), 1)
            stages.end()

            sem = stages.begin()
            RB = 4
            dl = spare[:, 1, :, :].rearrange("p k c -> p (k c)")[:, 0:RB * 384].rearrange("p (b i) -> p b i", b=RB)
            mt = sb("mt", [P, RB, 384], st)
            acs = tok[:, 2, :, :]
            with nc.Block(no_gpsimd_drain=True) as block:
                @block.tensor
                def _(pe):
                    def spread_head(hd):
                        if hd >= RB:
                            pe.wait_ge(sem("less"), 2 * (hd - RB + 1))
                        pe.matmul(PS[:, hd % RB, 0:T], ident[:, hd:hd + 1].to_broadcast([P, P]), acsT[:, :],
                                  start=True, stop=True).then_inc(sem("spread"), 1)

                    for hd in range(RB - 1):
                        spread_head(hd)
                    for hd in range(SSM_H):
                        if hd + RB - 1 < SSM_H:
                            spread_head(hd + RB - 1)
                        pe.wait_ge(sem("mt"), hd + 1)
                        if hd >= 8:
                            pe.wait_ge(sem("y"), hd // 2 - 3)
                        at = (hd % 2) * 64
                        o = PS[at:at + 64, 4 + hd // 2 % 4, 0:T]
                        pe.matmul(o, xdt[:, 0, hd * 64:(hd + 1) * 64], mt[:, hd % RB, 0:T], start=True, stop=False, skip_group_check=True)
                        pe.matmul(o[:, P:T], xdt[:, 1, hd * 64:(hd + 1) * 64], mt[:, hd % RB, T:384], start=False, stop=True,
                                  skip_group_check=True).then_inc(sem("y_done"), 1)

                @block.scalar
                def _(act):
                    for hd in range(SSM_H):
                        act.wait_ge(sem("less"), 2 * hd + 2)
                        act.activation(dl[:, hd % RB, :], dl[:, hd % RB, :], ACT.Exp).then_inc(sem("decay"), 1)

                @block.vector
                def _(dve):
                    def out_pair(b):
                        dve.wait_ge(sem("y_done"), 2 * b + 2)
                        dve.scalar_tensor_tensor(yb[:, b, :], yb[:, b, :], pr("d_skip", b, b + 1), PS[:, 4 + b % 4, 0:T],
                                                 ALU.mult, ALU.add).then_inc(sem("y"), 1)

                    def less(hd):
                        dve.wait_ge(sem("spread"), hd + 1)
                        if hd >= RB:
                            dve.wait_ge(sem("mt"), hd - RB + 1)
                        dve.tensor_scalar(dl[:, hd % RB, 0:T], PS[:, hd % RB, 0:T], acs[:, 0, hd:hd + 1], 0.0, ALU.subtract, ALU.min
                                          ).then_inc(sem("less"), 1)
                        dve.tensor_scalar(dl[:, hd % RB, T:384], PS[:, hd % RB, P:T], acs[:, 1, hd:hd + 1], 0.0, ALU.subtract, ALU.min
                                          ).then_inc(sem("less"), 1)

                    less(0)
                    less(1)
                    for hd in range(SSM_H):
                        if hd + 2 < SSM_H:
                            less(hd + 2)
                        dve.wait_ge(sem("decay"), hd + 1)
                        if hd >= RB:
                            dve.wait_ge(sem("y_done"), hd - RB + 1)
                        dve.tensor_tensor(mt[:, hd % RB, :], dl[:, hd % RB, :], cbm[:, hd // 8, :], ALU.mult).then_inc(sem("mt"), 1)
                        if hd % 2 and hd > 1:
                            out_pair(hd // 2 - 1)
                    out_pair(SSM_H // 2 - 1)
            stages.end()

            sem = stages.begin()
            z = zx[:, 0:16, :]
            with nc.Block(no_gpsimd_drain=True) as block:
                @block.vector
                def _(dve):
                    link = Chain(dve, sem("dve"))
                    for q in range(4):
                        dve.tensor_tensor(yb[:, 4 * q:4 * q + 4, :], yb[:, 4 * q:4 * q + 4, :], z[:, 4 * q:4 * q + 4, :], ALU.mult
                                          ).then_inc(sem("gated"), 1)
                    for u in range(2):
                        low_a(dve, A_AT["hyqkv"][0] + u)

                @block.scalar
                def _(act):
                    for u in range(2):
                        high_a(act, A_AT["hyqkv"][0] + u)
                    for q in range(4):
                        act.wait_ge(sem("gated"), q + 1)
                        act.activation(z[:, 4 * q:4 * q + 4, :], yb[:, 4 * q:4 * q + 4, :], ACT.Square).then_inc(sem("squares"), 1)
                    act.wait_ge(sem("square_sums"), 1)
                    act.activation(rstd[:, :], PS[:, 0, 0:T], ACT.Sqrt, bias=eps, scale=1.0 / 2048).then_inc(sem("root"), 1)

                @block.tensor
                def _(pe):
                    for b in range(16):
                        pe.wait_ge(sem("squares"), b // 4 + 1)
                        mm = pe.matmul(PS[:, 0, 0:T], ones, z[:, b, :], start=(b == 0), stop=(b == 15))
                    mm.then_inc(sem("square_sums"), 1)
            stages.end()

    def attention(yb, att):
        with ExitStack() as st:
            qkv = sb("qkv", [P, 40, T], st)
            acon = sb("acon", [48, 2, TWIDE], st)
            sem = stages.begin()
            a0, n = A_AT["hyqkv"]
            at0 = CON["bucket"][0]
            cst = ExitStack()
            bufC, acc = sb("bufC3", [P, KC, 256], cst), sb("acc3", [P, 2, 256], cst)
            with nc.Block(no_gpsimd_drain=True) as block:
                @block.gpsimd
                def _(pool):
                    c_loads(pool, sem, bufC[:, :, :], "hyqkv")

                @block.sync
                def _(sp):
                    sp.dma_start(acon[:, :, :].rearrange("p a b -> p (a b)"), con_dram[0:48, at0:at0 + 2 * TWIDE]).then_inc(sem("acon"), 16)
                    refill_a(sp, a0, n)
                    sp.wait_ge(sem("rows"), 1)
                    sp.dma_start(bias_rows, acon[:, 0, :]).then_inc(sem("rows_out"), 16)
                    sp.wait_ge(sem("rows_out"), 16)

                @block.tensor
                def _(pe):
                    pe.wait_ge(sem("acon"), 16)
                    pe.matmul(PS[0:48, 4, 0:TWIDE], pr("rel")[0:32, :], acon[0:32, 0, :], start=True, stop=True).then_inc(sem("rows_done"), 1)
                    proj_pe(pe, sem, a0, n, dst_token=(16, 17, 18, 19), c_units=C_UNITS["hyqkv"], acc=acc)

                @block.scalar
                def _(act):
                    proj_evac(act, 0, sem, a0, n, qkv)

                @block.vector
                def _(dve):
                    dve.reciprocal(rstd[:, :], rstd[:, :]).then_inc(sem("rstd"), 1)
                    dve.wait_ge(sem("rstd"), 1)
                    for b in range(16):
                        dve.scalar_tensor_tensor(yb[:, b, :], yb[:, b, :], pr("ssm_g", b, b + 1), rstd[:, :], ALU.mult, ALU.mult
                                                 ).then_inc(sem("yb"), 1)
                    dve.wait_ge(sem("rows_done"), 1)
                    dve.tensor_tensor(acon[:, 0, :], PS[0:48, 4, 0:TWIDE], acon[:, 1, :], ALU.add).then_inc(sem("rows"), 1)
                    proj_evac(dve, 1, sem, a0, n, qkv, (bufC[:, :, :], acc, "hyqkv", 1), second=False)
                    mods_out(dve, sem, sem("c_summed"), 8, PS[:, 5, 128:144], 128, 144, [(2, 1, pr("norm_ffn2", 8, 16))])
            cst.close()
            stages.end()

            sem = stages.begin()
            NT = 4
            bias = spare_highA[:, :, :, :].rearrange("p a k c -> p (a k c)")[:, 0:NT * 3 * T].rearrange("p (n g c) -> p n g c", n=NT, g=3)
            s_ = spare_xh[:, :, :].rearrange("p k t -> p (k t)")[:, 0:6 * T].rearrange("p (a c) -> p a c", a=2)
            pt = xm[:, 0:2, :]
            pT = xm[:, 2:4, :]
            stat = sb("stat", [P, 2, 4], st)
            k_odd = sb("k_odd", [P, 8, T], st)
            k_of = lambda hd: (k_odd[:, hd // 2, :] if hd % 2 else qkv[:, 24 + hd // 2, :])
            steps = [(hd, it) for hd in range(ATT_H) for it in range(2)]
            with nc.Block(no_gpsimd_drain=True) as block:
                @block.sync
                def _(sp):
                    for hd in range(ATT_H):
                        if hd >= NT:
                            sp.wait_ge(sem("biased"), 2 * (hd - NT) + 2)
                        src = bass.AP(tensor=bias_rows.tensor, offset=hd * TWIDE,
                                      ap=[[1, P], [ATT_H * TWIDE, 3], [1, T]])
                        sp.dma_start(bias[:, hd % NT, :, :], src).then_inc(sem(f"bias{hd % NT}"), 16)

                @block.tensor
                def _(pe):
                    def scores(n):
                        hd, it = steps[n]
                        W = P * (it + 1)
                        if n >= 2:
                            pe.wait_ge(sem("biased"), n - 1)
                        for g in range(3):
                            mm = pe.matmul(PS[:, 2 * (n % 2) + g // 2, (g % 2) * T:(g % 2) * T + W],
                                           qkv[:, 8 * g + hd // 2, it * P:(it + 1) * P], k_of(hd)[:, 0:W], start=True, stop=True)
                        mm.then_inc(sem("scores"), 1)

                    def turn(n):
                        hd, it = steps[n]
                        pe.wait_ge(sem("normed"), n + 1)
                        if n >= 2:
                            pe.wait_ge(sem("pT"), n - 1)
                        for j in range(it + 1):
                            mm = pe.transpose(PS[:, 4 + n % 2, j * P:(j + 1) * P], pt[:, n % 2, j * P:(j + 1) * P], ident)
                        mm.then_inc(sem("turned"), 1)

                    def values(n):
                        hd, it = steps[n]
                        at = (hd % 2) * 64
                        pe.wait_ge(sem("pT"), n + 1)
                        if hd >= 4 and it == 0 and hd % 2 == 0:
                            pe.wait_ge(sem("att"), hd // 2 - 1)
                        for j in range(it + 1):
                            mm = pe.matmul(PS[at:at + 64, 6 + hd // 2 % 2, it * P:(it + 1) * P],
                                           qkv[:, 32 + 2 * (hd // 4) + j, (hd % 4) * 64:(hd % 4 + 1) * 64],
                                           pT[:, n % 2, j * P:(j + 1) * P], start=(j == 0), stop=(j == it))
                        mm.then_inc(sem("values"), 1)

                    pe.wait_ge(sem("k_zeros"), 2)
                    scores(0)
                    scores(1)
                    for n in range(len(steps)):
                        if n + 2 < len(steps):
                            scores(n + 2)
                        turn(n)
                        if n >= 1:
                            values(n - 1)
                    values(len(steps) - 1)

                @block.scalar
                def _(act):
                    def turn_out(n):
                        W = P * (steps[n][1] + 1)
                        act.wait_ge(sem("turned"), n + 1)
                        if n >= 2:
                            act.wait_ge(sem("values"), n - 1)
                        act.copy(pT[:, n % 2, 0:W], PS[:, 4 + n % 2, 0:W]).then_inc(sem("pT"), 1)

                    def pair_out(b):
                        act.wait_ge(sem("values"), 4 * b + 4)
                        act.copy(att[:, b, :], PS[:, 6 + b % 2, 0:T]).then_inc(sem("att"), 1)

                    act.copy(k_odd[64:P, :, :], qkv[64:P, 24:32, :]).then_inc(sem("k_odd"), 1)
                    for n, (hd, it) in enumerate(steps):
                        W3 = 3 * P * (it + 1)
                        act.wait_ge(sem("max"), n + 1)
                        act.activation(s_[:, n % 2, 0:W3], s_[:, n % 2, 0:W3], ACT.Exp, bias=stat[:, n % 2, 0:1],
                                       accum_out=stat[:, n % 2, 1:2]).then_inc(sem("exps"), 1)
                        if n >= 1:
                            turn_out(n - 1)
                        if n >= 6 and n % 4 == 2:
                            pair_out(n // 4 - 1)
                    turn_out(len(steps) - 1)
                    pair_out(ATT_H // 2 - 1)

                @block.vector
                def _(dve):
                    link = Chain(dve, sem("dve"))

                    def biased(n):
                        hd, it = steps[n]
                        W = P * (it + 1)
                        dve.wait_ge(sem("scores"), n + 1)
                        dve.wait_ge(sem(f"bias{hd % NT}"), 16 * (hd // NT + 1))
                        sc = s_[:, n % 2, 0:3 * W].rearrange("p (g c) -> p g c", g=3)
                        b_ = bias[:, hd % NT, :, W - 1:W]
                        keys_forward = bass.AP(tensor=b_.tensor, offset=b_.offset, ap=[list(b_.ap[0]), list(b_.ap[1]), [-1, W]])
                        psum = PS[:, 2 * (n % 2):2 * (n % 2) + 2, :].rearrange("p a (g c) -> p (a g) c", g=2)[:, 0:3, 0:W]
                        dve.scalar_tensor_tensor(sc, psum, 0.125, keys_forward, ALU.mult, ALU.add
                                                 ).then_inc(sem("biased"), 1)
                        dve.wait_ge(sem("biased"), n + 1)
                        dve.tensor_reduce(stat[:, n % 2, 0:1], s_[:, n % 2, 0:3 * W], AX_X, ALU.max, negate=True).then_inc(sem("max"), 1)

                    def normed(n):
                        hd, it = steps[n]
                        W = P * (it + 1)
                        p = s_[:, n % 2, :]
                        dve.wait_ge(sem("exps"), n + 1)
                        if n >= 2:
                            dve.wait_ge(sem("turned"), n - 1)
                        dve.reciprocal(stat[:, n % 2, 2:3], stat[:, n % 2, 1:2]).then_inc(sem("recip"), 1)
                        link(dve.tensor_tensor(pt[:, n % 2, 0:W], p[:, 0:W], p[:, W:2 * W], ALU.add))
                        dve.wait_ge(sem("recip"), n + 1)
                        link(dve.tensor_tensor(pt[:, n % 2, 0:W], pt[:, n % 2, 0:W], p[:, 2 * W:3 * W], ALU.add))
                        dve.tensor_scalar(pt[:, n % 2, 0:W], pt[:, n % 2, 0:W], stat[:, n % 2, 2:3], None, ALU.mult
                                          ).then_inc(sem("normed"), 1)

                    dve.memset(k_odd[0:64, :, :], 0.0).then_inc(sem("k_zeros"), 1)
                    dve.wait_ge(sem("k_odd"), 1)
                    dve.memset(qkv[64:P, 24:32, :], 0.0).then_inc(sem("k_zeros"), 1)
                    biased(0)
                    for n in range(len(steps)):
                        if n + 1 < len(steps):
                            biased(n + 1)
                        normed(n)
            stages.end()

    def conformer():
        with ExitStack() as st:
            ag = sb("ag", [P, 16, T], st)
            cvo, cvo_low = sb2("cvo", [P, KC, T], st)
            sem = stages.begin()
            a0, n = A_AT["cv1"]
            with nc.Block(no_gpsimd_drain=True) as block:
                @block.sync
                def _(sp):
                    refill_a(sp, a0, n)

                @block.tensor
                def _(pe):
                    proj_pe(pe, sem, a0, n)

                @block.scalar
                def _(act):
                    proj_evac(act, 0, sem, a0, n, ag)

                @block.vector
                def _(dve):
                    proj_evac(dve, 1, sem, a0, n, ag)
            stages.end()
            sem = stages.begin()
            u, sg = ag[:, 0:8, :], ag[:, 8:16, :]
            TAPS_N = 31
            PE_TAPS = 14
            diag = sb("diag", [P, 2, KC, P], st)
            with nc.Block(no_gpsimd_drain=True) as block:
                @block.vector
                def _(dve):
                    link = Chain(dve, sem("dve"))
                    dw = pr("dw").rearrange("p (b i) -> p b i", b=KC)
                    for b in range(KC):
                        dve.wait_ge(sem("gate"), b + 1)
                        i = dve.scalar_tensor_tensor(u[:, b, :], u[:, b, :], pr("b1", b, b + 1), sg[:, b, :], ALU.add, ALU.mult)
                        i.then_inc(sem("u"), 1)
                    for b in range(KC):
                        dve.memset(cvo[:, b, 0:PE_TAPS], 0.0).then_inc(sem("zeros"), 1)
                    dve.wait_ge(sem("zeros"), KC)
                    for n, tp in enumerate(range(PE_TAPS, TAPS_N)):
                        for b in range(KC):
                            x, o = u[:, b, :], cvo[:, b, :]
                            w = dw[:, b, TAPS_N - 1 - tp:TAPS_N - tp]
                            if n == 0:
                                dve.wait_ge(sem("u"), b + 1)
                                i = dve.tensor_scalar(o[:, tp:T], x[:, 0:T - tp], w, None, ALU.mult)
                            else:
                                dve.wait_ge(sem("conv"), KC * (n - 1) + b + 1)
                                i = dve.scalar_tensor_tensor(o[:, tp:T], x[:, 0:T - tp], w, o[:, tp:T], ALU.mult, ALU.add)
                            i.then_inc(sem("conv"), 1)
                    dve.wait_ge(sem("conv"), KC * (TAPS_N - PE_TAPS))
                    dve.wait_ge(sem("tap_done"), PE_TAPS)
                    for b in range(KC):
                        dve.scalar_tensor_tensor(cvo[:, b, :], PS[:, 4 + b // 2, (b % 2) * T:(b % 2 + 1) * T], pr("dw_b", b, b + 1),
                                                 cvo[:, b, :], ALU.add, ALU.add).then_inc(sem("conved"), 1)
                    for n in range(2):
                        low_a(dve, A_AT["cv2"][0] + n)
                    dve.wait_ge(sem("sums"), 1)
                    dve.scalar_tensor_tensor(cvo[:, :, :], rep(PS[:, 0, 0:T], KC), -1.0 / D, cvo[:, :, :], ALU.mult, ALU.add
                                             ).then_inc(sem("centred"), 1)
                    dve.wait_ge(sem("root"), 1)
                    link(dve.reciprocal(rstd[:, :], rstd[:, :]))
                    dve.tensor_tensor(cvo[:, :, :], cvo[:, :, :], rep(rstd[:, :], KC), ALU.mult).then_inc(sem("normed"), 1)

                @block.scalar
                def _(act):
                    for b in range(KC):
                        act.activation(sg[:, b, :], sg[:, b, :], ACT.Sigmoid, bias=pr("b1", 8 + b, 9 + b)).then_inc(sem("gate"), 1)
                    dw = pr("dw").rearrange("p (b i) -> p b i", b=KC)
                    for tp in range(PE_TAPS):
                        if tp >= 2:
                            act.wait_ge(sem("tap_done"), tp - 1)
                        for b in range(KC):
                            i = act.activation(diag[:, tp % 2, b, :], ident, ACT.Copy, scale=dw[:, b, TAPS_N - 1 - tp:TAPS_N - tp])
                        i.then_inc(sem("diag"), 1)
                    for n in range(2):
                        high_a(act, A_AT["cv2"][0] + n)
                    act.wait_ge(sem("centred"), 1)
                    for q in range(2):
                        act.activation(sg[:, 4 * q:4 * q + 4, :], cvo[:, 4 * q:4 * q + 4, :], ACT.Square).then_inc(sem("squares"), 1)
                    act.wait_ge(sem("square_sums"), 1)
                    act.activation(rstd[:, :], PS[:, 1, 0:T], ACT.Sqrt, bias=eps, scale=1.0 / D).then_inc(sem("root"), 1)
                    act.wait_ge(sem("normed"), 1)
                    for b in range(KC):
                        act.activation(cvo[:, b, :], cvo[:, b, :], ACT.Silu, bias=pr("ln_b", b, b + 1), scale=pr("ln_g", b, b + 1)
                                       ).then_inc(sem("out"), 1)

                @block.tensor
                def _(pe):
                    for tp in range(PE_TAPS):
                        pe.wait_ge(sem("diag"), tp + 1)
                        for b in range(KC):
                            if tp == 0:
                                pe.wait_ge(sem("u"), b + 1)
                            mm = pe.matmul(PS[:, 4 + b // 2, (b % 2) * T + tp:(b % 2 + 1) * T], diag[:, tp % 2, b, :], u[:, b, 0:T - tp],
                                           start=(tp == 0 and b % 2 == 0), stop=(tp == PE_TAPS - 1), skip_group_check=True)
                        mm.then_inc(sem("tap_done"), 1)
                    for b in range(KC):
                        pe.wait_ge(sem("conved"), b + 1)
                        mm = pe.matmul(PS[:, 0, 0:T], ones, cvo[:, b, :], start=(b == 0), stop=(b == KC - 1))
                    mm.then_inc(sem("sums"), 1)
                    for b in range(KC):
                        if b % 4 == 0:
                            pe.wait_ge(sem("squares"), b // 4 + 1)
                        mm = pe.matmul(PS[:, 1, 0:T], ones, sg[:, b, :], start=(b == 0), stop=(b == KC - 1))
                    mm.then_inc(sem("square_sums"), 1)
            stages.end()
            out_proj("cv2", cvo, cvo_low)

    first_stage()
    norm_stage(0, 0, "win", small_ab)
    mixer_one()
    norm_stage(1, 0, "moe", small_route, (0, 0, 16, None))
    moe()
    norm_h(pr("norm_out"), h, (4, 0, 40, None))
    norm_stage(0, 1, "hyin", small_dt)
    mixer_two()
    norm_stage(1, 1, "ffn0", None, (4, 1, 16, None))
    swiglu("ffn0", FF // 256, None)
    norm_stage(0, 2, "cv1", None, (4, 1, 40, None))
    conformer()
    norm_stage(1, 2, "ffn1", None, (0, 2, 16, pr("b2")))
    swiglu("ffn1", FF // 256, None)
    norm_h(pr("final"), xm, (4, 2, 40, None))
    ctx.close()


def put_a(dst, w):
    n = w.shape[1] // 256
    dst.reshape(n, P, KC, 256)[...] = w.reshape(KC, P, n, 256).transpose(2, 1, 0, 3)


def put_b(dst, w):
    n = w.shape[0] // 256
    dst.reshape(n, P, 2, D)[...] = w.reshape(n, 2, P, D).transpose(0, 2, 1, 3)


def put_paired(dst, a, b):
    for j, w in enumerate((a, b)):
        n = w.shape[1] // 256
        dst[j::2].reshape(n, P, KC, 256)[...] = w.reshape(KC, P, n, 256).transpose(2, 1, 0, 3)


def cols(v):
    return np.asarray(v).reshape(-1, P).T


def everywhere(v):
    return np.broadcast_to(np.asarray(v).reshape(1, -1), (P, np.asarray(v).size))


def layout(i):
    i = {k: np.asarray(v) for k, v in i.items()}
    w_in = i["w_in"][0]
    hy = i["hy_w_in_2"][0]
    eg = i["w_gate"][0].reshape(N_EXP, D, FF_EXP)
    eu = i["w_up"][0].reshape(N_EXP, D, FF_EXP)
    ed = i["w_down"][0].reshape(N_EXP, FF_EXP, D)
    wa = np.empty((A_ALL, P, UNIT), w_in.dtype)
    wb = np.empty((B_ALL, P, UNIT), w_in.dtype)
    in_a = lambda name, a=0, b=None: wa[A_AT[name][0] + a:A_AT[name][0] + (A_AT[name][1] if b is None else b)]
    in_b = lambda name, a=0, b=None: wb[B_AT[name][0] + a:B_AT[name][0] + (B_AT[name][1] if b is None else b)]
    put_a(in_a("mod"), i["mod_w"][0][:, :2048])
    wc = np.empty((C_ALL, P, UNIT), w_in.dtype)
    put_a(wc[0:16], i["mod_w"][0][:, 2048:])
    put_a(wc[16:40], i["ada_w_2"][0])
    put_a(wc[40:64], i["ada_w_2"][1])
    put_a(in_a("win", 0, 24), w_in[:, :6144])
    put_a(in_a("win", 24), w_in[:, 6152:])
    put_a(in_a("wout"), i["w_out"][0])
    for e in range(N_EXP):
        put_paired(in_a("moe", 4 * e, 4 * e + 4), eg[e], eu[e])
        put_b(in_b("moe", 2 * e, 2 * e + 2), ed[e])
    put_a(in_a("hyin"), hy[:, :5120])
    put_a(in_a("hyqkv"), hy[:, 5152:])
    put_b(in_a("hyout"), i["hy_w_out_2"][0])
    put_a(in_a("cv1"), i["cv_w_pw1_2"][0])
    put_a(in_a("cv2"), i["cv_w_pw2_2"][0])
    for l in range(2):
        put_paired(in_a(f"ffn{l}"), i["ffn_w_gate_2"][l], i["ffn_w_up_2"][l])
        put_b(in_b(f"ffn{l}"), i["ffn_w_down_2"][l])
    f = wa.dtype
    par = np.zeros((P, N_PAR), f)

    def put(name, v):
        at, w = PAR[name]
        v = np.asarray(v)
        par[:v.shape[0], at:at + w] = v.reshape(v.shape[0], w)

    put("c", cols(i["c"][0]))
    put("c2", cols(i["c_2"][0]))
    put("mod_b", cols(i["mod_b"][0]))
    put("ada_b", cols(i["ada_b_2"]))
    put("norm_mix", cols(i["norm_mix_w"][0]))
    put("norm_ffn", cols(i["norm_ffn_w"][0]))
    put("norm_out", cols(i["norm_out_w"]))
    put("norm_mix2", cols(i["norm_mix_g_2"]))
    put("norm_ffn2", cols(i["norm_ffn_g_2"]))
    put("final", cols(i["final_norm_g_2"]))
    put("gconv", i["gdn_conv_w"][0].reshape(4, 16, P).transpose(2, 1, 0))
    put("a_log", everywhere(i["gdn_a_log"][0]))
    put("dt_bias", everywhere(i["gdn_dt_bias"][0]))
    put("gdn_w", cols(i["gdn_norm_w"][0]))
    put("b_route", everywhere(np.concatenate([i["b_group"][0], i["b_router"][0].reshape(-1)])))
    put("w_route", np.concatenate([i["w_group"][0], i["w_router"][0]], 1).reshape(KC, P, 20).transpose(1, 0, 2))
    put("w_ab", w_in[:, 6144:6152].reshape(KC, P, 8).transpose(1, 0, 2))
    put("hconv", i["hy_conv_w_2"][0].reshape(4, 24, P).transpose(2, 1, 0))
    put("hconv_b", cols(i["hy_conv_b_2"][0]))
    put("w_dt", hy[:, 5120:5152].reshape(KC, P, SSM_H).transpose(1, 0, 2))
    put("dt_bias2", i["hy_dt_bias_2"][0][:, None])
    put("a_log2", i["hy_a_log_2"][0][:, None])
    put("d_skip", cols(np.repeat(i["hy_d_skip_2"][0], 64)))
    put("ssm_g", cols(i["hy_ssm_norm_g_2"][0]))
    put("rel", i["rel_table_2"])
    put("b1", cols(i["cv_b_pw1_2"][0]))
    put("dw", i["cv_w_dw_2"][0].reshape(31, 8, P).transpose(2, 1, 0))
    put("dw_b", cols(i["cv_b_dw_2"][0]))
    put("ln_g", cols(i["cv_ln_g_2"][0]))
    put("ln_b", cols(i["cv_ln_b_2"][0]))
    put("b2", cols(i["cv_b_pw2_2"][0]))
    x = np.ascontiguousarray(i["x"][0].T.reshape(KC, P, T).transpose(1, 0, 2))
    return {"wa": wa, "wb": wb, "wc": wc, "par": par, "con": constants(), "xT": x}


def kernel(**inputs):
    import concourse.bacc as _bacc
    from concourse.bass_utils import run_bass_kernel_spmd as _run

    nc = _bacc.Bacc("TRN2", target_bir_lowering=False, num_devices=1)
    arrays = layout(inputs)
    ins = [nc.dram_tensor(n, a.shape, mybir.dt.from_np(a.dtype), kind="ExternalInput").ap() for n, a in arrays.items()]
    out = nc.dram_tensor("out", (P, KC, T), F32, kind="ExternalOutput").ap()
    program(nc, ins, out)
    r = _run(nc, [arrays], core_ids=[0])
    y = r.results[0]["out"]
    return y.transpose(1, 0, 2).reshape(D, T).T.reshape(1, T, D)
```
